# Optimizing a Trainium2 kernel written in Bass

```python
import jax, jax.numpy as jnp
from jax import lax
import numpy as np
import jax
import jax.numpy as jnp

D_MODEL = 1024
BATCH = 1
SEQ = 512
DEPTH = 2

HEAD_DIM = 64
N_Q_HEADS = 8
N_KV_HEADS = 2
GQA_GROUP = N_Q_HEADS // N_KV_HEADS
WINDOW = 128
ROPE_THETA = 10000.0
RET_HEADS = 4
RET_QK_DIM = 128
RET_V_DIM = 2 * RET_QK_DIM
RET_CHUNK = 128
RET_THETA = 10000.0
D_FF = 4 * D_MODEL
EPS = 1e-6

ATT_Q = N_Q_HEADS * HEAD_DIM
ATT_KV = N_KV_HEADS * HEAD_DIM
RET_QK = RET_HEADS * RET_QK_DIM
RET_V = RET_HEADS * RET_V_DIM
SPLIT_SIZES = (ATT_Q, ATT_KV, ATT_KV, RET_QK, RET_QK, RET_V, RET_V, D_MODEL, D_MODEL)
W_IN = sum(SPLIT_SIZES)
SPLIT_POINTS = tuple(int(v) for v in np.cumsum(SPLIT_SIZES)[:-1])


def rmsnorm(x, g):
    xf = x.astype(jnp.float32)
    y = xf * lax.rsqrt(jnp.mean(xf * xf, axis=-1, keepdims=True) + EPS)
    return (y * g.astype(jnp.float32)).astype(x.dtype)

def rope_half(x, pos):
    half = x.shape[-1] // 2
    inv = ROPE_THETA ** (-jnp.arange(half, dtype=jnp.float32) / half)
    ang = pos.astype(jnp.float32)[:, None] * inv[None, :]
    cos = jnp.cos(ang)[None, :, None, :]
    sin = jnp.sin(ang)[None, :, None, :]
    xf = x.astype(jnp.float32)
    x1, x2 = xf[..., :half], xf[..., half:]
    return jnp.concatenate([x1 * cos - x2 * sin, x2 * cos + x1 * sin], axis=-1).astype(x.dtype)

def rotate_every_two(x):
    x1, x2 = x[..., ::2], x[..., 1::2]
    return jnp.stack([-x2, x1], axis=-1).reshape(x.shape)

def retention_rotation(x, pos):
    dk = x.shape[-1]
    theta = 1.0 / (RET_THETA ** jnp.linspace(0.0, 1.0, dk // 2, dtype=jnp.float32))
    theta = jnp.repeat(theta, 2)
    ang = pos.astype(jnp.float32)[:, None] * theta[None, :]
    cos = jnp.cos(ang)[None, :, None, :]
    sin = jnp.sin(ang)[None, :, None, :]
    xf = x.astype(jnp.float32)
    return (xf * cos + rotate_every_two(xf) * sin).astype(x.dtype)

def sliding_window_sink_attention(q, k, v, sinks):
    B, S = q.shape[0], q.shape[1]
    C = WINDOW
    nb = S // C
    qb = q.reshape(B, nb, C, N_KV_HEADS, GQA_GROUP, HEAD_DIM)
    kb = k.reshape(B, nb, C, N_KV_HEADS, HEAD_DIM)
    vb = v.reshape(B, nb, C, N_KV_HEADS, HEAD_DIM)

    def band(t):
        prev = jnp.pad(t, ((0, 0), (1, 0), (0, 0), (0, 0), (0, 0)))[:, :-1]
        return jnp.concatenate([prev, t], axis=2)

    kk, vv = band(kb), band(vb)
    s = jnp.einsum('bnqhgd,bnkhd->bnhgqk', qb, kk).astype(jnp.float32) * (HEAD_DIM ** -0.5)
    qi = jnp.arange(C)[:, None] + C
    kj = jnp.arange(2 * C)[None, :]
    rel = qi - kj
    valid = (rel >= 0) & (rel < WINDOW)
    first = (jnp.arange(nb) > 0)[:, None, None] | (kj >= C)[None]
    mask = valid[None] & first
    s = jnp.where(mask[None, :, None, None], s, -jnp.inf)
    sink = jnp.broadcast_to(
        sinks.astype(jnp.float32).reshape(1, 1, N_KV_HEADS, GQA_GROUP, 1, 1),
        s.shape[:-1] + (1,))
    p = jax.nn.softmax(jnp.concatenate([s, sink], axis=-1), axis=-1)[..., :-1]
    o = jnp.einsum('bnhgqk,bnkhd->bnqhgd', p.astype(v.dtype), vv)
    return o.reshape(B, S, ATT_Q)

def chunkwise_retention(q, k, v):
    B, S = q.shape[0], q.shape[1]
    C = RET_CHUNK
    nc = S // C
    log_g = jnp.log(1.0 - 2.0 ** (-5.0 - jnp.arange(RET_HEADS, dtype=jnp.float32)))
    idx = jnp.arange(C, dtype=jnp.float32)
    rel = idx[:, None] - idx[None, :]
    dmask = jnp.where(rel[None] >= 0, jnp.exp(log_g[:, None, None] * jnp.maximum(rel, 0.0)[None]), 0.0)

    qc = q.astype(jnp.float32).reshape(B, nc, C, RET_HEADS, RET_QK_DIM)
    kc = k.astype(jnp.float32).reshape(B, nc, C, RET_HEADS, RET_QK_DIM)
    vc = v.astype(jnp.float32).reshape(B, nc, C, RET_HEADS, RET_V_DIM)

    s = jnp.einsum('bnihd,bnjhd->bnhij', qc, kc) * dmask[None, None]
    inner = jnp.einsum('bnhij,bnjhe->bnihe', s, vc)

    zeta = jnp.exp(log_g[None, :] * (C - 1.0 - idx)[:, None])
    kv = jnp.einsum('bnjhd,bnjhe->nbhde', kc, vc * zeta[None, None, :, :, None])
    g_chunk = jnp.exp(log_g * C)[None, :, None, None]

    def step(R, kv_n):
        return R * g_chunk + kv_n, R

    R0 = jnp.zeros((B, RET_HEADS, RET_QK_DIM, RET_V_DIM), jnp.float32)
    _, R_prev = lax.scan(step, R0, kv)
    xi = jnp.exp(log_g[None, :] * (idx + 1.0)[:, None])
    cross = jnp.einsum('bnihd,nbhde->bnihe', qc, R_prev) * xi[None, None, :, :, None]
    return (inner + cross).reshape(B, S, RET_HEADS, RET_V_DIM)

def hybrid_layer(x, g_mix, w_in, sinks, w_a, w_b, w_out, g_mlp, w_up, w_down):
    B, S, _ = x.shape
    pos = jnp.arange(S)
    h = rmsnorm(x, g_mix)
    z = h @ w_in
    aq, ak, av, rq, rk, rv, rg, ga, gb = jnp.split(z, SPLIT_POINTS, axis=-1)

    aq = rope_half(aq.reshape(B, S, N_Q_HEADS, HEAD_DIM), pos)
    ak = rope_half(ak.reshape(B, S, N_KV_HEADS, HEAD_DIM), pos)
    av = av.reshape(B, S, N_KV_HEADS, HEAD_DIM)
    ya = sliding_window_sink_attention(aq, ak, av, sinks) @ w_a

    rq = retention_rotation(rq.reshape(B, S, RET_HEADS, RET_QK_DIM), pos)
    rk = retention_rotation(rk.reshape(B, S, RET_HEADS, RET_QK_DIM), pos) * (RET_QK_DIM ** -0.5)
    rv = rv.reshape(B, S, RET_HEADS, RET_V_DIM)
    r = chunkwise_retention(rq, rk, rv)
    r = r * lax.rsqrt(jnp.mean(r * r, axis=-1, keepdims=True) + EPS)
    r = r.reshape(B, S, RET_V) * jax.nn.silu(rg.astype(jnp.float32))
    yb = r.astype(x.dtype) @ w_b

    mixed = jax.nn.sigmoid(ga) * ya + jax.nn.sigmoid(gb) * yb
    x = x + mixed @ w_out

    h2 = rmsnorm(x, g_mlp)
    x = x + jnp.square(jax.nn.relu(h2 @ w_up)) @ w_down
    return x

def first_inputs(seed: int = 0) -> dict:
    key = jax.random.key(seed)
    ks = jax.random.split(key, 12)
    f32 = jnp.float32

    def nrm(k, shape, fan_in):
        return jax.random.normal(k, shape, f32) * (fan_in ** -0.5)

    return {
        "x": jax.random.normal(ks[0], (BATCH, SEQ, D_MODEL), f32),
        "g_mix": 1.0 + 0.05 * jax.random.normal(ks[1], (DEPTH, D_MODEL), f32),
        "w_in": nrm(ks[2], (DEPTH, D_MODEL, W_IN), D_MODEL),
        "sinks": 0.5 * jax.random.normal(ks[3], (DEPTH, N_Q_HEADS), f32),
        "w_a": nrm(ks[4], (DEPTH, ATT_Q, D_MODEL), ATT_Q),
        "w_b": nrm(ks[5], (DEPTH, RET_V, D_MODEL), RET_V),
        "w_out": nrm(ks[6], (DEPTH, D_MODEL, D_MODEL), D_MODEL),
        "g_mlp": 1.0 + 0.05 * jax.random.normal(ks[7], (DEPTH, D_MODEL), f32),
        "w_up": nrm(ks[8], (DEPTH, D_MODEL, D_FF), D_MODEL),
        "w_down": nrm(ks[9], (DEPTH, D_FF, D_MODEL), D_FF),
        "g_final": 1.0 + 0.05 * jax.random.normal(ks[10], (D_MODEL,), f32),
    }

def first_block(x, g_mix, w_in, sinks, w_a, w_b, w_out, g_mlp, w_up, w_down, g_final):
    for l in range(DEPTH):
        x = hybrid_layer(x, g_mix[l], w_in[l], sinks[l], w_a[l], w_b[l], w_out[l],
                         g_mlp[l], w_up[l], w_down[l])
    return rmsnorm(x, g_final)


GRID_W = 64
CTX_LEN = 256
D_MIX = D_MODEL
D_MLSTM = D_MIX // 2
D_NA = D_MIX - D_MLSTM
H_MLSTM = D_MLSTM // HEAD_DIM
H_NA = D_NA // HEAD_DIM
N_GATE = 4 * H_MLSTM
D_IN = 4 * D_MLSTM + 3 * D_NA + N_GATE
MLSTM_CHUNK = 64
NA_ROWS_MAX = 8
NA_COLS = 16
D_FF_2 = 4 * D_MODEL
N_MOD = 6
ROPE_BASE = 10000.0
F_BIAS_LO = 3.0
F_BIAS_HI = 6.0


def rmsnorm_2(x, g):
    x32 = x.astype(jnp.float32)
    y = x32 * lax.rsqrt(jnp.mean(x32 * x32, axis=-1, keepdims=True) + EPS)
    return (y * g.astype(jnp.float32)).astype(x.dtype)

def sq_relu_mlp(h, w1, w2):
    return jnp.square(jax.nn.relu(h @ w1)) @ w2

def split_heads(a, n_heads):
    b, t, _ = a.shape
    return a.reshape(b, t, n_heads, HEAD_DIM).transpose(0, 2, 1, 3)

def merge_heads(a):
    b, h, t, d = a.shape
    return a.transpose(0, 2, 1, 3).reshape(b, t, h * d)

def head_layernorm(h, g):
    mu = jnp.mean(h, axis=-1, keepdims=True)
    var = jnp.mean(jnp.square(h - mu), axis=-1, keepdims=True)
    return merge_heads((h - mu) * lax.rsqrt(var + EPS)) * g.astype(jnp.float32)

def axial_rope_tables(n_tokens):
    t = jnp.arange(n_tokens)
    row = (t // GRID_W).astype(jnp.float32)
    col = (t % GRID_W).astype(jnp.float32)
    n_freq = HEAD_DIM // 4
    inv_freq = ROPE_BASE ** (-jnp.arange(n_freq, dtype=jnp.float32) / n_freq)
    ang = jnp.concatenate([row[:, None] * inv_freq, col[:, None] * inv_freq], axis=-1)
    return jnp.cos(ang), jnp.sin(ang)

def apply_rope(x, cos, sin):
    x1, x2 = jnp.split(x, 2, axis=-1)
    return jnp.concatenate([x1 * cos - x2 * sin, x1 * sin + x2 * cos], axis=-1)

def mlstm_scan(q, k, v, log_i, log_f, state):
    B, H, T, d = q.shape
    L = MLSTM_CHUNK
    nc = T // L

    def chunks(a):
        return jnp.moveaxis(a.reshape(a.shape[:2] + (nc, L) + a.shape[3:]), 2, 0)

    causal = jnp.tril(jnp.ones((L, L), dtype=bool))

    def step(carry, xs):
        C, n, m = carry
        qc, kc, vc, ic, fc = xs
        b = jnp.cumsum(fc, axis=-1)
        d_intra = jnp.where(causal, b[..., :, None] - b[..., None, :] + ic[..., None, :], -jnp.inf)
        d_prev = b + m[..., None]
        m_t = jnp.maximum(d_prev, jnp.max(d_intra, axis=-1))
        w_intra = jnp.exp(d_intra - m_t[..., None])
        w_prev = jnp.exp(d_prev - m_t)
        s = jnp.einsum('bhtd,bhsd->bhts', qc, kc) * w_intra
        num = w_prev[..., None] * jnp.einsum('bhtd,bhde->bhte', qc, C) + jnp.einsum('bhts,bhse->bhte', s, vc)
        qn = w_prev * jnp.einsum('bhtd,bhd->bht', qc, n) + jnp.sum(s, axis=-1)
        h = num / jnp.maximum(jnp.abs(qn), jnp.exp(-m_t))[..., None]
        b_end = b[..., -1]
        d_end = b_end[..., None] - b + ic
        m_new = jnp.maximum(b_end + m, jnp.max(d_end, axis=-1))
        w_c = jnp.exp(b_end + m - m_new)
        w_s = jnp.exp(d_end - m_new[..., None])
        C = w_c[..., None, None] * C + jnp.einsum('bhs,bhsd,bhse->bhde', w_s, kc, vc)
        n = w_c[..., None] * n + jnp.einsum('bhs,bhsd->bhd', w_s, kc)
        return (C, n, m_new), h

    state, h = lax.scan(step, state, (chunks(q), chunks(k), chunks(v), chunks(log_i), chunks(log_f)))
    return jnp.moveaxis(h, 0, 2).reshape(B, H, T, d), state

def mlstm_group(q, k, v, o, gates, qc, kc, vc, oc, gates_c, b_gate, norm_g, cos, sin, need_ctx):
    f32 = jnp.float32
    scale = HEAD_DIM ** -0.5

    def prep(a):
        return split_heads(a, H_MLSTM).astype(f32)

    qx = apply_rope(prep(q), cos, sin) * scale
    kx = apply_rope(prep(k), cos, sin)
    vx = prep(v)
    qcx = prep(qc) * scale
    kcx = prep(kc)
    vcx = prep(vc)

    def gate_split(g):
        return jnp.split((g.astype(f32) + b_gate.astype(f32)).transpose(0, 2, 1), 4, axis=1)

    i_fw, i_bw, f_fw, f_bw = gate_split(gates)
    ic_fw, ic_bw, fc_fw, fc_bw = gate_split(gates_c)
    B, H, _, d = qx.shape
    state0 = (jnp.zeros((B, H, d, d), f32), jnp.zeros((B, H, d), f32), jnp.zeros((B, H), f32))

    def direction(rev, ig, fg, igc, fgc):
        flip = (lambda a: jnp.flip(a, axis=2)) if rev else (lambda a: a)
        hc, st = mlstm_scan(flip(qcx), flip(kcx), flip(vcx), flip(igc), jax.nn.log_sigmoid(flip(fgc)), state0)
        hx, _ = mlstm_scan(flip(qx), flip(kx), flip(vx), flip(ig), jax.nn.log_sigmoid(flip(fg)), st)
        return flip(hx), flip(hc)

    hx_f, hc_f = direction(False, i_fw, f_fw, ic_fw, fc_fw)
    hx_b, hc_b = direction(True, i_bw, f_bw, ic_bw, fc_bw)
    y = (head_layernorm(hx_f + hx_b, norm_g) * jax.nn.sigmoid(o.astype(f32))).astype(q.dtype)
    yc = None
    if need_ctx:
        yc = (head_layernorm(hc_f + hc_b, norm_g) * jax.nn.sigmoid(oc.astype(f32))).astype(q.dtype)
    return y, yc

def neighborhood_attention(q, k, v, qc, kc, vc, rpb, rows, need_ctx):
    B, S, _ = q.shape
    scale = HEAD_DIM ** -0.5
    kr_n = min(NA_ROWS_MAX, rows)

    def grid(a):
        return split_heads(a, H_NA).reshape(B, H_NA, rows, GRID_W, HEAD_DIM)

    qg = grid(q * scale)
    kg = grid(k)
    vg = grid(v)
    kch = split_heads(kc, H_NA)
    vch = split_heads(vc, H_NA)
    cols = jnp.arange(GRID_W)
    col_start = jnp.clip(cols - NA_COLS // 2, 0, GRID_W - NA_COLS)
    col_mask = (cols[None, :] >= col_start[:, None]) & (cols[None, :] < col_start[:, None] + NA_COLS)
    dc_idx = jnp.clip(cols[None, :] - cols[:, None] + NA_COLS - 1, 0, 2 * NA_COLS - 2)
    rpb_cols = rpb.astype(jnp.float32)[:, :, dc_idx]

    def row_block(r):
        rs = jnp.clip(r - kr_n // 2, 0, rows - kr_n)
        q_r = lax.dynamic_index_in_dim(qg, r, axis=2, keepdims=False)
        k_r = lax.dynamic_slice_in_dim(kg, rs, kr_n, axis=2)
        v_r = lax.dynamic_slice_in_dim(vg, rs, kr_n, axis=2)
        bias = jnp.take(rpb_cols, rs + jnp.arange(kr_n) - r + NA_ROWS_MAX - 1, axis=1)
        s_loc = jnp.einsum('bhqd,bhrkd->bhqrk', q_r, k_r).astype(jnp.float32) + bias.transpose(0, 2, 1, 3)
        s_loc = jnp.where(col_mask[:, None, :], s_loc, -jnp.inf)
        s_ctx = jnp.einsum('bhqd,bhcd->bhqc', q_r, kch).astype(jnp.float32)
        s = jnp.concatenate([s_loc.reshape(B, H_NA, GRID_W, kr_n * GRID_W), s_ctx], axis=-1)
        p = jax.nn.softmax(s, axis=-1).astype(v.dtype)
        p_loc = p[..., :kr_n * GRID_W].reshape(B, H_NA, GRID_W, kr_n, GRID_W)
        p_ctx = p[..., kr_n * GRID_W:]
        return jnp.einsum('bhqrk,bhrkd->bhqd', p_loc, v_r) + jnp.einsum('bhqc,bhcd->bhqd', p_ctx, vch)

    out = lax.map(row_block, jnp.arange(rows))
    y = out.transpose(1, 0, 3, 2, 4).reshape(B, S, H_NA * HEAD_DIM)
    yc = None
    if need_ctx:
        qch = split_heads(qc * scale, H_NA)
        sc = jnp.einsum('bhqd,bhkd->bhqk', qch, kch).astype(jnp.float32)
        pc = jax.nn.softmax(sc, axis=-1).astype(vc.dtype)
        yc = merge_heads(jnp.einsum('bhqk,bhkd->bhqd', pc, vch))
    return y, yc

def token_mixers(p, pc, b_gate, norm_g, rpb, cos, sin, rows, need_ctx):
    cuts = [int(i) for i in np.cumsum([D_MLSTM] * 4 + [D_NA] * 3)]
    qm, km, vm, om, qn, kn, vn, gm = jnp.split(p, cuts, axis=-1)
    qmc, kmc, vmc, omc, qnc, knc, vnc, gmc = jnp.split(pc, cuts, axis=-1)
    y_m, yc_m = mlstm_group(qm, km, vm, om, gm, qmc, kmc, vmc, omc, gmc, b_gate, norm_g, cos, sin, need_ctx)
    y_n, yc_n = neighborhood_attention(qn, kn, vn, qnc, knc, vnc, rpb, rows, need_ctx)
    y = jnp.concatenate([y_m, y_n], axis=-1)
    yc = jnp.concatenate([yc_m, yc_n], axis=-1) if need_ctx else None
    return y, yc

def second_inputs(seed: int = 0) -> dict:
    key = jax.random.key(seed)
    ks = jax.random.split(key, 16)
    nrm = jax.random.normal
    f32 = jnp.float32
    x = nrm(ks[0], (BATCH, SEQ, D_MODEL), f32)
    c = nrm(ks[1], (BATCH, D_MODEL), f32)
    ctx = nrm(ks[2], (BATCH, CTX_LEN, D_MODEL), f32)
    c_ctx = nrm(ks[3], (D_MODEL,), f32)
    w_ada = nrm(ks[4], (DEPTH, D_MODEL, N_MOD * D_MODEL), f32) * (0.5 * D_MODEL ** -0.5)
    b_ada = 0.02 * nrm(ks[5], (DEPTH, N_MOD * D_MODEL), f32)
    norm1_g = 1.0 + 0.02 * nrm(ks[6], (DEPTH, D_MODEL), f32)
    w_in = nrm(ks[7], (DEPTH, D_MODEL, D_IN), f32) * D_MODEL ** -0.5
    i_bias = 0.1 * nrm(ks[8], (DEPTH, 2 * H_MLSTM), f32)
    f_base = jnp.tile(jnp.linspace(F_BIAS_LO, F_BIAS_HI, H_MLSTM, dtype=f32), 2)
    f_bias = f_base[None, :] + 0.1 * nrm(ks[9], (DEPTH, 2 * H_MLSTM), f32)
    b_gate = jnp.concatenate([i_bias, f_bias], axis=-1)
    mlstm_norm_g = 1.0 + 0.02 * nrm(ks[10], (DEPTH, D_MLSTM), f32)
    rpb = 0.1 * nrm(ks[11], (DEPTH, H_NA, 2 * NA_ROWS_MAX - 1, 2 * NA_COLS - 1), f32)
    w_out = nrm(ks[12], (DEPTH, D_MIX, D_MODEL), f32) * D_MIX ** -0.5
    norm2_g = 1.0 + 0.02 * nrm(ks[13], (DEPTH, D_MODEL), f32)
    km1, km2 = jax.random.split(ks[14])
    w_mlp1 = nrm(km1, (DEPTH, D_MODEL, D_FF_2), f32) * D_MODEL ** -0.5
    w_mlp2 = nrm(km2, (DEPTH, D_FF_2, D_MODEL), f32) * D_FF_2 ** -0.5
    final_g = 1.0 + 0.02 * nrm(ks[15], (D_MODEL,), f32)
    return {"x": x, "c": c, "ctx": ctx, "c_ctx": c_ctx, "w_ada": w_ada, "b_ada": b_ada,
            "norm1_g": norm1_g, "w_in": w_in, "b_gate": b_gate, "mlstm_norm_g": mlstm_norm_g,
            "rpb": rpb, "w_out": w_out, "norm2_g": norm2_g, "w_mlp1": w_mlp1, "w_mlp2": w_mlp2,
            "final_g": final_g}

def second_block(x, c, ctx, c_ctx, w_ada, b_ada, norm1_g, w_in, b_gate, mlstm_norm_g, rpb, w_out,
              norm2_g, w_mlp1, w_mlp2, final_g):
    B, S, D = x.shape
    rows = S // GRID_W
    cos, sin = axial_rope_tables(S)
    silu_c = jax.nn.silu(c)
    silu_cc = jax.nn.silu(c_ctx)
    xc = ctx
    for l in range(DEPTH):
        need_ctx = l < DEPTH - 1
        mod = silu_c @ w_ada[l] + b_ada[l]
        mod_c = silu_cc @ w_ada[l] + b_ada[l]
        sh1, sc1, g1, sh2, sc2, g2 = jnp.split(mod[:, None, :], N_MOD, axis=-1)
        sh1c, sc1c, g1c, sh2c, sc2c, g2c = jnp.split(mod_c, N_MOD, axis=-1)
        h = rmsnorm_2(x, norm1_g[l]) * (1.0 + sc1) + sh1
        hc = rmsnorm_2(xc, norm1_g[l]) * (1.0 + sc1c) + sh1c
        y, yc = token_mixers(h @ w_in[l], hc @ w_in[l], b_gate[l], mlstm_norm_g[l], rpb[l],
                             cos, sin, rows, need_ctx)
        x = x + g1 * (y @ w_out[l])
        h = rmsnorm_2(x, norm2_g[l]) * (1.0 + sc2) + sh2
        x = x + g2 * sq_relu_mlp(h, w_mlp1[l], w_mlp2[l])
        if need_ctx:
            xc = xc + g1c * (yc @ w_out[l])
            hc = rmsnorm_2(xc, norm2_g[l]) * (1.0 + sc2c) + sh2c
            xc = xc + g2c * sq_relu_mlp(hc, w_mlp1[l], w_mlp2[l])
    return rmsnorm_2(x, final_g)


def setup_inputs(seed=0):
    out = dict(first_inputs(seed))
    for name, value in second_inputs(seed + 1).items():
        if name != "x":
            out[name + "_2"] = value
    return out


def reference(
    x, g_mix, w_in, sinks, w_a, w_b, w_out, g_mlp, w_up, w_down, g_final, c_2, ctx_2, c_ctx_2,
    w_ada_2, b_ada_2, norm1_g_2, w_in_2, b_gate_2, mlstm_norm_g_2, rpb_2, w_out_2, norm2_g_2,
    w_mlp1_2, w_mlp2_2, final_g_2,
):
    x = first_block(
        x, g_mix, w_in, sinks, w_a, w_b, w_out, g_mlp, w_up, w_down, g_final,
    )
    return second_block(
        x, c_2, ctx_2, c_ctx_2, w_ada_2, b_ada_2, norm1_g_2, w_in_2, b_gate_2, mlstm_norm_g_2,
        rpb_2, w_out_2, norm2_g_2, w_mlp1_2, w_mlp2_2, final_g_2,
    )


_drawn_inputs = setup_inputs


def setup_inputs(seed=0):
    import zlib

    import numpy as np

    out = dict(_drawn_inputs(seed))
    spreads = {}
    factors = {'sinks': 6.938,
     'norm1_g_2': 5.777,
     'mlstm_norm_g_2': 8.0,
     'rpb_2': 8.0,
     'norm2_g_2': 4.381,
     'final_g_2': 2.844}
    for name, (base, spread) in spreads.items():
        noise = np.random.default_rng([zlib.crc32(name.encode()), seed]).standard_normal(out[name].shape)
        drawn = base * np.exp(spread * noise) if base else spread * noise
        out[name] = jnp.asarray(drawn.astype(out[name].dtype))
    for name, factor in factors.items():
        out[name] = (out[name] * factor).astype(out[name].dtype)
    return out
```

```python
P = 128
D_MODEL, SEQ, DEPTH = 1024, 512, 2
KT = D_MODEL // P
TT = SEQ // P
D_FF = 4 * D_MODEL
QUARTERS = D_FF // D_MODEL
EPS = 1e-6
HEAD = 64
WINDOW = 128
ATT_HEADS, ATT_GROUPS = 8, 2
ATT_Q, ATT_KV = 512, 128
RET_HEADS, RET_QK, RET_V = 4, 128, 256
CTX = 256
ALL = CTX + SEQ
ST = ALL // P
CT = CTX // P
GRID_W, GRID_ROWS, NA_COLS, NA_ROWS = 64, 8, 16, 8
H2 = 8
NMOD = 6
RING, RAW = 4, 2
MASKED = -1e30

IN_1 = 48
WA_1 = 4
LAYER_1 = IN_1 + WA_1 + 2 * KT + QUARTERS * 2 * KT
LAYER_2 = 32 + KT + QUARTERS * 2 * KT
CHUNKS = DEPTH * (LAYER_1 + LAYER_2) + RING
ADA = NMOD * KT
V_GMIX, V_GMLP, V_N1, V_N2, V_GF, V_FIN, V_BADA, V_MN, V_BG, V_SINK, N_VEC = \
    0, 16, 32, 48, 64, 72, 80, 176, 184, 186, 202


def weight_stream(inp):
    import numpy as np

    def block(w, rows, cols):
        return w[np.asarray(rows)][:, np.asarray(cols)].reshape(-1, P, len(cols)).transpose(1, 0, 2)

    chunks = []
    every = np.arange(D_MODEL)

    def put(*blocks):
        chunks.append(np.concatenate([b.reshape(P, -1) for b in blocks], axis=1))

    def pad(n=1):
        for _ in range(n):
            chunks.append(np.zeros((P, KT * P), np.float32))

    def tile(w, start, width=P):
        put(block(w, every, np.arange(start, start + width)))

    def mlp(up, down):
        for q in range(QUARTERS):
            for m in range(KT):
                tile(up, q * D_MODEL + m * P)
            for m in range(KT):
                put(block(down, q * D_MODEL + every, np.arange(m * P, (m + 1) * P)))

    pair = [np.concatenate([np.arange(h * HEAD, (h + 1) * HEAD) for h in (t, t + 4)]) for t in range(4)]
    at = np.cumsum([0, ATT_Q, ATT_KV, ATT_KV, RET_HEADS * RET_QK, RET_HEADS * RET_QK,
                    RET_HEADS * RET_V, RET_HEADS * RET_V, D_MODEL])
    for l in range(DEPTH):
        w = inp["w_in"][l]
        for t in range(4):
            put(block(w, every, pair[t]))
        for t in range(8):
            tile(w, at[3] + t * P)
        tile(w, at[1])
        tile(w, at[2])
        pad(2)
        for t in range(8):
            tile(w, at[5] + t * P)
        for t in range(8):
            tile(w, at[6] + t * P)
        rows = np.concatenate(pair)
        for t in range(0, 8, 2):
            put(*[block(inp["w_a"][l], rows, np.arange(m * P, (m + 1) * P)) for m in (t, t + 1)])
        for m in range(8):
            tile(w, at[7] + m * P)
            tile(w, at[8] + m * P)
            tile(inp["w_b"][l], m * P)
        for m in range(8):
            tile(inp["w_out"][l], m * P)
        mlp(inp["w_up"][l], inp["w_down"][l])
    for l in range(DEPTH):
        w = inp["w_in_2"][l]
        for t in range(12):
            tile(w, 2048 + t * P)
        gates = np.zeros((D_MODEL, P), np.float32)
        for g, start in enumerate((0, 32, 64, 96)):
            gates[:, start:start + H2] = w[:, 3584 + g * H2:3584 + (g + 1) * H2]
        tile(gates, 0)
        pad(3)
        for t in range(16):
            tile(w, t * P)
        for m in range(8):
            tile(inp["w_out_2"][l], m * P)
        mlp(inp["w_mlp1_2"][l], inp["w_mlp2_2"][l])
    pad(RING)
    out = np.stack(chunks)
    assert out.shape[0] == CHUNKS
    return out


def columns(v):
    import numpy as np
    return np.ascontiguousarray(np.asarray(v).reshape(-1, P).T)


def constants_1():
    import numpy as np
    f = np.float32
    p = np.arange(P)
    pos = np.arange(SEQ, dtype=f)
    d = p % HEAD
    inv = f(10000.0) ** (-np.arange(32, dtype=f) / f(32))
    ang = pos[None, :] * inv[d % 32][:, None]
    att_cos, att_sin = np.cos(ang), np.sin(ang) * np.where(d < 32, -1, 1)[:, None]
    theta = f(1.0) / (f(10000.0) ** np.linspace(0.0, 1.0, 64, dtype=f))
    ang = pos[None, :] * theta[p // 2][:, None]
    ret_cos, ret_sin = np.cos(ang), np.sin(ang) * np.where(p % 2 == 0, -1, 1)[:, None]
    rel = p[:, None] + WINDOW - np.arange(2 * WINDOW)[None, :]
    mask = np.where((rel >= 0) & (rel < WINDOW), 0.0, MASKED)
    decay = []
    for h in range(RET_HEADS):
        log_g = np.log(f(1.0) - f(2.0) ** f(-5.0 - h))
        r = (np.arange(SEQ)[None, :] - p[:, None]).astype(f)
        decay.append(np.where(r >= 0, np.exp(log_g * np.maximum(r, 0)), 0) * f(RET_QK ** -0.5))
    swap_ret = np.eye(P)[p ^ 1]
    return np.concatenate([mask, mask, att_cos, att_sin, ret_cos, ret_sin, swap_ret, *decay], axis=1).astype(f)


def constants_0():
    import numpy as np
    p = np.arange(P)
    return np.concatenate([np.eye(P), np.ones((P, P)), np.eye(P)[p ^ 32]], axis=1).astype(np.float32)


def hybrid_then_dit(nc, dram, out):
    import concourse.bass as bass
    from concourse import mybir
    from contextlib import ExitStack

    F, R = mybir.dt.float32, mybir.dt.float32r
    ALU, ACT, AX = mybir.AluOpType, mybir.ActivationFunctionType, mybir.AxisListType
    ds = bass.ds

    KB = 1024
    BASE = 16512

    def sb(name, at, shape, dt=F):
        return nc.alloc_sbuf_tensor_at(name, [P, *shape], dt, offset=BASE + int(at))

    x = sb("x", 0, [KT, SEQ])
    w_raw = sb("w_raw", 24 * KB, [RAW, KT * P])
    w_hi = sb("w_hi", 32 * KB, [RING, KT * P], R)
    w_lo = sb("w_lo", 48 * KB, [RING, KT * P], R)
    h_hi = sb("h_hi", 64 * KB, [KT, SEQ], R)
    h_lo = sb("h_lo", 88 * KB, [KT, SEQ], R)
    CONST = 112 * KB
    c0 = sb("c0", CONST, [3 * P])
    ident, ones, swap_half = c0[:, 0:P], c0[:, P:2 * P], c0[:, 2 * P:3 * P]
    C1 = 4 * WINDOW + 4 * SEQ + P + RET_HEADS * SEQ
    c1 = sb("c1", CONST + 1536, [C1])
    att_mask = c1[:, 0:512].rearrange("p (h k) -> p h k", h=2)
    att_cos, att_sin = c1[:, 512:1024], c1[:, 1024:1536]
    ret_cos, ret_sin = c1[:, 1536:2048], c1[:, 2048:2560]
    swap_pair = c1[:, 2560:2688]
    decay = c1[:, 2688:C1].rearrange("p (h i) -> p h i", h=RET_HEADS)
    VECS = 132 * KB
    assert CONST + 1536 + 4 * C1 <= VECS
    vec = sb("vec", VECS, [N_VEC])
    SMALL = VECS + 4 * N_VEC + 24
    gain_now = sb("gain_now", SMALL, [KT])
    sink_now = sb("sink_now", SMALL + 32, [2, ATT_HEADS])
    eps = sb("eps", SMALL + 96, [1])
    rms = sb("rms", SMALL + 128, [2, 16])
    mod = sb("mod", SMALL + 256, [2, DEPTH * ADA])
    mod_3 = sb("mod_3", SMALL + 1056, [2, 3])
    tiny = sb("tiny", SMALL + 1088, [2, 16])
    DYN = 135 * KB
    assert SMALL + 1088 + 128 <= DYN
    stage = sb("stage", 80 * KB, [2, SEQ])
    stage_2 = sb("stage_2", 84 * KB, [2, SEQ])
    tmp = sb("tmp", 104 * KB, [2, SEQ])
    tmp_2 = sb("tmp_2", 108 * KB, [2, SEQ])
    tmp_3 = sb("tmp_3", 16 * KB, [2, SEQ])
    diag = sb("diag", 22 * KB, [TT, P])
    rqk = sb("rqk", DYN, [2 * RET_HEADS, SEQ])
    rv = sb("rv", DYN + 16 * KB, [TT, RET_HEADS * RET_V])
    r_hi = sb("r_hi", DYN, [KT, SEQ], R)
    r_lo = sb("r_lo", DYN + 16 * KB, [KT, SEQ], R)
    U = DYN + 32 * KB
    aq = sb("aq", U, [4, SEQ])
    ak = sb("ak", U + 8 * KB, [SEQ])
    av = sb("av", U + 10 * KB, [TT, ATT_KV])
    pt_sb = sb("pt_sb", U + 12 * KB, [2, 2, 2, P])
    s_sb = sb("s_sb", 16 * KB, [2, 2, 2 * WINDOW])
    p_sb = sb("p_sb", U + 32 * KB, [2, 2, 2 * WINDOW])
    o_hi = sb("o_hi", U + 16 * KB, [4, SEQ], R)
    o_lo = sb("o_lo", U + 24 * KB, [4, SEQ], R)
    r_raw = sb("r_raw", U, [KT, SEQ])
    a_sb = [sb("a_sb0", U + 32 * KB, [1280]), sb("a_sb1", 16 * KB, [1280])]
    y_a = sb("y_a", U, [KT, SEQ])
    mix_hi = sb("mix_hi", U + 16 * KB, [KT, SEQ], R)
    mix_lo = sb("mix_lo", U, [KT, SEQ], R)
    u_hi = sb("u_hi", DYN, [KT, SEQ], R)
    u_lo = sb("u_lo", DYN + 16 * KB, [KT, SEQ], R)
    ada_w = sb("ada_w", U, [3, D_MODEL])
    ada_junk = sb("ada_junk", U + 12 * KB, [D_MODEL])
    c_silu = sb("c_silu", U + 16 * KB, [2, D_MODEL])
    c_raw = sb("c_raw", U + 24 * KB, [2, D_MODEL])

    cx = sb("cx", 16 * KB, [KT, CTX])
    c_hi = sb("c_hi", 64 * KB, [KT, ALL], R)
    c_lo = sb("c_lo", 88 * KB, [KT, ALL], R)
    C2 = 2 * SEQ + 2 * P + GRID_W
    c2 = sb("c2", CONST + 1536, [C2])
    rope_cos, rope_sin = c2[:, 0:SEQ], c2[:, SEQ:2 * SEQ]
    causal = [c2[:, 2 * SEQ:2 * SEQ + P], c2[:, 2 * SEQ + P:2 * SEQ + 2 * P]]
    col_mask = c2[:, 2 * SEQ + 2 * P:C2]
    GATE = CONST + 1536 + 4 * C2
    gates = sb("gates", GATE, [ALL])
    cum_f = sb("cum_f", GATE + 3 * KB, [ALL])
    run_m = sb("run_m", GATE + 6 * KB, [ALL])
    key_w = sb("key_w", GATE + 9 * KB, [ALL])
    key_t = sb("key_t", GATE, [ST, P])
    cols = sb("cols", GATE + 12 * KB, [4, ST * H2])
    assert GATE + 12 * KB + 16 * ST * H2 <= VECS
    gain_2 = sb("gain_2", SMALL + 1088 + 128, [2, KT])
    assert SMALL + 1088 + 128 + 64 <= DYN
    sq_2 = sb("sq_2", DYN + 48 * KB, [2, ALL])
    hf_2 = sb("hf_2", DYN + 54 * KB, [2, ALL])
    diag_2 = sb("diag_2", DYN + 60 * KB, [ST, P])
    qn = sb("qn", DYN, [4, ALL])
    kn = sb("kn", DYN + 12 * KB, [4, ALL])
    yn_hi = sb("yn_hi", DYN, [4, ALL], R)
    yn_lo = sb("yn_lo", DYN + 12 * KB, [4, ALL], R)
    vn = sb("vn", DYN + 24 * KB, [ST, H2 * HEAD])
    bias = sb("bias", DYN + 36 * KB, [2, (2 * NA_ROWS - 2) * GRID_W])
    sn = sb("sn", DYN + 43 * KB, [2, ALL])
    pn = sb("pn", DYN + 49 * KB, [2, ALL])
    zn = sb("zn", DYN + 55 * KB, [2, ALL])
    qm = sb("qm", DYN + 24 * KB, [4, ALL])
    km = sb("km", DYN + 36 * KB, [4, ALL])
    ym_hi = sb("ym_hi", DYN + 24 * KB, [4, ALL], R)
    ym_lo = sb("ym_lo", DYN + 36 * KB, [4, ALL], R)
    vm = sb("vm", DYN + 48 * KB, [ST, H2, HEAD + 1])
    OM = DYN + 48 * KB + 4 * ST * H2 * (HEAD + 1)
    om = sb("om", OM, [4, ALL])
    assert OM + 12 * KB <= 207 * KB + 512
    zm = sb("zm", OM, [2, ALL])
    rope_a = sb("rope_a", OM + 6 * KB, [SEQ])
    rope_b = sb("rope_b", OM + 8 * KB, [SEQ])
    PAIRS = 42
    gw = sb("gw", 64 * KB, [2, PAIRS * P])
    m_row = sb("m_row", 12 * KB, [2, 2, ALL])
    hs = sb("hs", 0, [ST, H2, HEAD])
    hb = sb("hb", 106 * KB, [ST, HEAD])
    hq = sb("hq", 12 * KB, [ST, H2, HEAD])
    yu = sb("yu", 64 * KB, [4, ALL])
    u2_hi = sb("u2_hi", DYN, [KT, ALL], R)
    u2_lo = sb("u2_lo", DYN + 24 * KB, [KT, ALL], R)
    x_spill = nc.dram_tensor("x_spill", [P, KT, SEQ], F, kind="Internal").ap()
    cx_spill = nc.dram_tensor("cx_spill", [P, KT, CTX], F, kind="Internal").ap()
    m_spill = nc.dram_tensor("m_spill", [2, H2, ALL], F, kind="Internal").ap()

    RET_COL = [0, 512, 896, 1152, 1280]

    ctx = ExitStack()
    with ctx:
        ps = ctx.enter_context(nc.psum_tensor("ps", [P, 8, SEQ], F))

        def sem(name):
            return ctx.enter_context(nc.semaphore(name))

        x_loaded, vec_loaded, c0_loaded, c1_loaded = sem("x_loaded"), sem("vec_loaded"), sem("c0_loaded"), sem("c1_loaded")
        raw_ready = [sem(f"raw_ready{j}") for j in range(RAW)]
        c_loaded = sem("c_loaded")
        ada_ready = [sem(f"ada_ready{j}") for j in range(3)]
        stored = sem("stored")
        hi_ready, lo_ready, chunk_used = sem("hi_ready"), sem("lo_ready"), sem("chunk_used")
        bank_read = [sem(f"bank_read{j}") for j in range(RING)]
        sq_ready, sq_used, std_ready = sem("sq_ready"), sem("sq_used"), sem("std_ready")
        rinv_ready, diag_ready, rb_ready = sem("rinv_ready"), sem("diag_ready"), sem("rb_ready")
        hf_ready, hhi_ready, hlo_ready = sem("hf_ready"), sem("hhi_ready"), sem("hlo_ready")
        eps_set = sem("eps_set")
        rot_ready, rope_half_done, rope_done = sem("rot_ready"), sem("rope_half_done"), sem("rope_done")
        vt_ready, v_done = sem("vt_ready"), sem("v_done")
        layer_vec = sem("layer_vec")
        sc_ready, s_done, mx_done, nm_ready = sem("sc_ready"), sem("s_done"), sem("mx_done"), sem("nm_ready")
        exp_done, den_done, p_ready, pt_ready = sem("exp_done"), sem("den_done"), sem("p_ready"), sem("pt_ready")
        pt_copied, pv_ready, ohi_ready, olo_ready = sem("pt_copied"), sem("pv_ready"), sem("ohi_ready"), sem("olo_ready")
        rs_ready, a_ready, inner_ready, rcopy_done = sem("rs_ready"), sem("a_ready"), sem("inner_ready"), sem("rcopy_done")
        rsq_used, rstd_ready, rrinv_ready = sem("rsq_used"), sem("rstd_ready"), sem("rrinv_ready")
        rdiag_ready, rrb_ready = sem("rdiag_ready"), sem("rrb_ready")
        tanh_ready, sl_ready, rr_ready, rhi_ready, rlo_ready = sem("tanh_ready"), sem("sl_ready"), sem("rr_ready"), sem("rhi_ready"), sem("rlo_ready")
        ya_ready, ta_ready, t12_ready, mx_ready, mhi_ready, mlo_ready = \
            sem("ya_ready"), sem("ta_ready"), sem("t12_ready"), sem("mx_ready"), sem("mhi_ready"), sem("mlo_ready")
        relu_ready, v2_ready, uhi_ready, ulo_ready = sem("relu_ready"), sem("v2_ready"), sem("uhi_ready"), sem("ulo_ready")
        ct_ready, cs_ready, ada_sum, ada_used = sem("ct_ready"), sem("cs_ready"), sem("ada_sum"), sem("ada_used")

        N_ROPE, N_VT, N_ATT, N_MLP = 4 + 8 + 1, 1 + 8, 16, QUARTERS * KT
        G1 = LAYER_1 // RING
        G_RET, G_KV, G_RV, G_RG, G_WA, G_MIX, G_OUT, G_MLP = 1, 3, 4, 6, 8, 9, 15, 17
        units = [(n, g, i) for n in range(TT) for g in range(ATT_GROUPS) for i in range(2)]

        cx_loaded, c2_loaded, xf_done, spilled, reloaded = sem("cx_loaded"), sem("c2_loaded"), sem("xf_done"), sem("spilled"), sem("reloaded")
        mod_ready, gain_ready = sem("mod_ready"), sem("gain_ready")
        z_ready, zrot_ready, ztok_ready, rope_part, rope_2 = sem("z_ready"), sem("zrot_ready"), sem("ztok_ready"), sem("rope_part"), sem("rope_2")
        om_half = sem("om_half")
        bias_loaded = [sem(f"bias_loaded{j}") for j in range(2)]
        bias_ready = sem("bias_ready")
        ns_ready, nsx_done, nsc_done, nmx_done, nneg_ready = sem("ns_ready"), sem("nsx_done"), sem("nsc_done"), sem("nmx_done"), sem("nneg_ready")
        nexp_done, nrec_done, np_ready, npt_ready = sem("nexp_done"), sem("nrec_done"), sem("np_ready"), sem("npt_ready")
        npt_copied, npv_ready, nhi_ready, nlo_ready = sem("npt_copied"), sem("npv_ready"), sem("nhi_ready"), sem("nlo_ready")
        gate_v, gate_a, m_stored, key_ready, key_copied = sem("gate_v"), sem("gate_a"), sem("m_stored"), sem("key_ready"), sem("key_copied")
        m_loaded = [sem(f"m_loaded{j}") for j in range(2)]
        ms_ready, mw_ready, mdiag_ready, mg_ready, mpv_ready = sem("ms_ready"), sem("mw_ready"), sem("mdiag_ready"), sem("mg_ready"), sem("mpv_ready")
        post_v, head_done, ln_v, ln_a, yt_ready, yu_ready = sem("post_v"), sem("head_done"), sem("ln_v"), sem("ln_a"), sem("yt_ready"), sem("yu_ready")
        yhi_ready, ylo_ready = sem("yhi_ready"), sem("ylo_ready")

        G2 = LAYER_2 // RING
        G_VN, G_GATE, G_QM, G_VM, G_OM, G_OUT2, G_UP = 2, 3, 4, 6, 7, 8, 10
        START_2 = DEPTH * G1
        X, C = slice(CTX, ALL), slice(0, CTX)
        FIRST_MOD = 2 * DEPTH
        N_UNITS = H2 * ST

        def natt_units(need_ctx):
            return [(h, c, t) for h in range(H2) for c, n in ((0, TT), (1, CT if need_ctx else 0)) for t in range(n)]

        def key_tiles(d, t):
            if d == 0:
                return list(range(t + 1))
            return list(range(t, CT)) if t < CT else list(range(CT)) + list(range(t, ST))

        def gw_layout(first):
            at, runs, where = 0, [[] for _ in range(ST)], {}
            for s in range(ST):
                for d in range(2):
                    seen = [t for t in range(first, ST) if s in key_tiles(d, t)]
                    while seen:
                        n = 1
                        while n < len(seen) and seen[n] == seen[0] + n:
                            n += 1
                        runs[s].append((d, seen[0], seen[0] + n, at))
                        for t in seen[:n]:
                            where[d, s, t] = at + (t - seen[0]) * P
                        at, seen = at + n * P, seen[n:]
            assert at <= PAIRS * P
            return runs, where

        block = ctx.enter_context(nc.Block())

        @block.sync
        def _(sp):
            sp.dma_start(x[:, :, :], dram["x"]).then_inc(x_loaded, 16)
            sp.dma_start(c0[:, :], dram["c0"]).then_inc(c0_loaded, 16)
            sp.dma_start(vec[:, :], dram["vec"]).then_inc(vec_loaded, 16)
            for j in range(RAW):
                sp.dma_start(w_raw[:, j, :], dram["w"][j, :, :]).then_inc(raw_ready[j], 16)
            sp.dma_start(c1[:, :], dram["c1"]).then_inc(c1_loaded, 16)
            with sp.Fori(1, CHUNKS // RAW) as g:
                for j in range(RAW):
                    sp.wait_ge(lo_ready, g * RAW + (j + 1 - RAW))
                    sp.dma_start(w_raw[:, j, :], dram["w"][g * RAW + j, :, :]).then_inc(raw_ready[j], 16)
            for k in range(KT):
                sp.wait_ge(xf_done, KT + (k + 1))
                sp.dma_start(out[:, k, :], x[:, k, :]).then_inc(stored, 16)
            sp.wait_ge(stored, KT * 16)

        @block.gpsimd
        def _(pool):
            with pool.Fori(0, CHUNKS // RING) as g:
                for j in range(RING):
                    pool.wait_ge(hi_ready, g * RING + (j + 1))
                    nc.gpsimd.tensor_tensor(w_lo[:, j, :], w_raw[:, j % RAW, :], w_hi[:, j, :].bitcast(F),
                                            ALU.subtract).then_inc(lo_ready, 1)

        @block.tensor
        def _(pe):
            def product(g, j, bank, rhs_hi, rhs_lo, blocks=range(KT)):
                n = len(blocks)
                for k, b in enumerate(blocks):
                    w = slice(b * P, (b + 1) * P)
                    nc.tensor.matmul(bank, w_hi[:, j, w], rhs_hi[:, k, :], start=(k == 0), stop=False)
                    nc.tensor.matmul(bank, w_hi[:, j, w], rhs_lo[:, k, :], start=False, stop=False)
                    last = nc.tensor.matmul(bank, w_lo[:, j, w], rhs_hi[:, k, :], start=False, stop=(k == n - 1))
                return last

            def arrive(g, j, more=0):
                pe.wait_ge(lo_ready, g * RING + (j + 1 + more))
                pe.wait_ge(bank_read[j], g + 2)

            def chunk(g, j, rhs_hi, rhs_lo, pads=0):
                arrive(g, j, pads)
                product(g, j, ps[:, j, :], rhs_hi, rhs_lo).then_inc(chunk_used, 1 + pads)

            def norm(n):
                for k in range(KT):
                    pe.wait_ge(sq_ready, n * KT + (k + 1))
                    for t in range(TT):
                        last = nc.tensor.matmul(ps[:, 4, t:t + 1], stage[:, k % 2, t * P:(t + 1) * P], ones[:, 0:1],
                                                start=(k == 0 and t == 0), stop=(k == KT - 1), skip_group_check=True)
                    last.then_inc(sq_used, 1)
                pe.wait_ge(diag_ready, n + 1)
                nc.tensor.matmul(ps[:, 5, :], ones, diag[:, :, :].rearrange("p t q -> p (t q)"),
                                 start=True, stop=True).then_inc(rb_ready, 1)

            def rotate(l, n, g, j, swap):
                pe.wait_ge(bank_read[j], g + 3)
                if not isinstance(n, int) or n >= 2:
                    pe.wait_ge(rope_half_done, l * (2 * N_ROPE) + n * 2 - 2)
                nc.tensor.matmul(ps[:, 4 + j % 2, :], swap, stage[:, j % 2, :], start=True, stop=True).then_inc(rot_ready, 1)

            def transposed(v, g, j, first=False):
                pe.wait_ge(bank_read[j], g + 3)
                if not first:
                    pe.wait_ge(v_done, v)
                for t in range(TT):
                    last = nc.tensor.transpose(ps[:, 6, t * P:(t + 1) * P], stage[:, j % 2, t * P:(t + 1) * P], ident)
                last.then_inc(vt_ready, 1)

            pe.wait_ge(c0_loaded, 16)
            with pe.Fori(0, DEPTH) as l:
                g0 = l * G1
                norm(2 * l)

                pe.wait_ge(hlo_ready, 2 * l * KT + KT)
                pe.wait_ge(c1_loaded, 16)
                for j in range(RING):
                    chunk(g0, j, h_hi, h_lo)
                    if j > 0:
                        rotate(l, j - 1, g0, j - 1, swap_half)
                rotate(l, 3, g0, 3, swap_half)
                with pe.Fori(0, 2) as i:
                    g = g0 + i + G_RET
                    for j in range(RING):
                        chunk(g, j, h_hi, h_lo)
                        if j > 0:
                            rotate(l, i * 4 + (3 + j), g, j - 1, swap_pair)
                    rotate(l, i * 4 + 7, g, 3, swap_pair)
                chunk(g0 + G_KV, 0, h_hi, h_lo)
                chunk(g0 + G_KV, 1, h_hi, h_lo, pads=2)
                rotate(l, 12, g0 + G_KV, 0, swap_half)
                transposed(None, g0 + G_KV, 1, first=True)

                pe.wait_ge(rope_done, l * N_ROPE + N_ROPE)
                pe.wait_ge(v_done, l * N_VT + 1)

                def scores(u):
                    n, g, i = units[u]
                    rows = slice(g * HEAD, (g + 1) * HEAD)
                    keys = slice(max(n - 1, 0) * P, (n + 1) * P)
                    wide = keys.stop - keys.start
                    for e in range(2):
                        last = nc.tensor.matmul(ps[:, u % 2, e * 2 * P:e * 2 * P + wide], aq[rows, 2 * i + e, n * P:(n + 1) * P],
                                                ak[rows, keys], start=True, stop=True)
                    last.then_inc(sc_ready, 1)

                def weighted(u):
                    n, g, i = units[u]
                    pe.wait_ge(pt_copied, l * N_ATT + (u + 1))
                    if u >= 2:
                        pe.wait_ge(olo_ready, l * N_ATT + (u - 1))
                    first = 0 if n else 1
                    for b in range(first, 2):
                        last = nc.tensor.matmul(ps[g * HEAD:(g + 1) * HEAD, 4 + u % 2, 0:2 * P],
                                                av[:, n - 1 + b, g * HEAD:(g + 1) * HEAD], pt_sb[:, u % 2, b, :, :],
                                                start=(b == first), stop=(b == 1))
                    last.then_inc(pv_ready, 1)

                scores(0)
                scores(1)
                for u in range(N_ATT):
                    n, g, i = units[u]
                    pe.wait_ge(p_ready, l * N_ATT + (u + 1))
                    if u >= 2:
                        pe.wait_ge(pt_copied, l * N_ATT + (u - 1))
                    for b in range(0 if n else 1, 2):
                        for e in range(2):
                            at = (b if n else 0) * P
                            last = nc.tensor.transpose(ps[:, 2 + u % 2, (b * 2 + e) * P:(b * 2 + e + 1) * P],
                                                       p_sb[:, u % 2, e, at:at + P], ident)
                    last.then_inc(pt_ready, 1)
                    if u + 2 < N_ATT:
                        scores(u + 2)
                    if u >= 1:
                        weighted(u - 1)
                weighted(N_ATT - 1)

                with pe.Fori(0, 2) as i:
                    g = g0 + i + G_RV
                    for j in range(RING):
                        chunk(g, j, h_hi, h_lo)
                        if j > 0:
                            transposed(l * N_VT + i * 4 + j, g, j - 1)
                    transposed(l * N_VT + i * 4 + 4, g, 3)

                pe.wait_ge(v_done, l * N_VT + N_VT)
                pe.wait_ge(olo_ready, l * N_ATT + N_ATT)

                def ret_scores(h):
                    for t in range(TT):
                        if h >= 1:
                            pe.wait_ge(a_ready, l * 16 + (4 * (h - 1) + (t + 1 if t < 2 else 4)))
                        bank = ps[:, t, 0:SEQ - t * P] if t < 3 else ps[:, 2, 256:384]
                        nc.tensor.matmul(bank, rqk[:, RET_HEADS + h, t * P:(t + 1) * P], rqk[:, h, t * P:SEQ],
                                         start=True, stop=True).then_inc(rs_ready, 1)

                def ret_inner(h):
                    b = 4 + 2 * (h % 2)
                    if h >= 2:
                        pe.wait_ge(rcopy_done, l * 16 + 4 * (h - 1))
                    for t in range(TT):
                        pe.wait_ge(a_ready, l * 16 + (4 * h + t + 1))
                        for e in range(2):
                            last = nc.tensor.matmul(ps[:, b + e, t * P:SEQ], rv[:, t, h * RET_V + e * P:h * RET_V + (e + 1) * P],
                                                    a_sb[h % 2][:, RET_COL[t]:RET_COL[t + 1]], start=(t == 0), stop=(t == TT - 1))
                    last.then_inc(inner_ready, 1)

                def ret_squares(h):
                    pe.wait_ge(rcopy_done, l * 16 + 4 * (h + 1))
                    for t in range(TT):
                        for e in range(2):
                            last = nc.tensor.matmul(ps[:, 3, 4 * h + t:4 * h + t + 1], stage_2[:, e, t * P:(t + 1) * P], ones[:, 0:1],
                                                    start=(h == 0 and t == 0 and e == 0), stop=(e == 1), skip_group_check=True)
                    last.then_inc(rsq_used, 1)

                ret_scores(0)
                for h in range(RET_HEADS):
                    if h + 1 < RET_HEADS:
                        ret_scores(h + 1)
                    ret_inner(h)
                    if h >= 1:
                        ret_squares(h - 1)
                ret_squares(RET_HEADS - 1)
                for h in range(RET_HEADS):
                    pe.wait_ge(rdiag_ready, l * 4 + (h + 1))
                    nc.tensor.matmul(ps[:, 4 + h, :], ones, diag[:, :, :].rearrange("p t q -> p (t q)"),
                                     start=True, stop=True).then_inc(rrb_ready, 1)

                with pe.Fori(0, 2) as i:
                    for j in range(RING):
                        chunk(g0 + i + G_RG, j, h_hi, h_lo)
                pe.wait_ge(rr_ready, l * 8 + 8)
                for j in range(RING):
                    arrive(g0 + G_WA, j)
                    product(g0 + G_WA, j, ps[:, j, :], o_hi, o_lo, range(0, 4))
                    product(g0 + G_WA, j, ps[:, 4 + j, :], o_hi, o_lo, range(4, 8)).then_inc(chunk_used, 1)
                with pe.Fori(0, 2) as i:
                    pe.wait_ge(rlo_ready, l * 8 + 8)
                    for c in range(12):
                        src = (r_hi, r_lo) if c % 3 == 2 else (h_hi, h_lo)
                        chunk(g0 + i * 3 + (G_MIX + c // RING), c % RING, *src)
                with pe.Fori(0, 2) as i:
                    pe.wait_ge(mlo_ready, l * 8 + 8)
                    for j in range(RING):
                        chunk(g0 + i + G_OUT, j, mix_hi, mix_lo)
                norm(2 * l + 1)
                with pe.Fori(0, QUARTERS) as q:
                    with pe.Fori(0, 2) as i:
                        pe.wait_ge(hlo_ready, 2 * l * KT + 2 * KT)
                        for j in range(RING):
                            chunk(g0 + q * 4 + i + G_MLP, j, h_hi, h_lo)
                    with pe.Fori(0, 2) as i:
                        for j in range(RING):
                            arrive(g0 + q * 4 + i + (G_MLP + 2), j)
                            for k in range(KT):
                                pe.wait_ge(ulo_ready, l * N_MLP + q * KT + (k + 1))
                                w = slice(k * P, (k + 1) * P)
                                nc.tensor.matmul(ps[:, j, :], w_hi[:, j, w], u_hi[:, k, :], start=(k == 0), stop=False)
                                nc.tensor.matmul(ps[:, j, :], w_hi[:, j, w], u_lo[:, k, :], start=False, stop=False)
                                last = nc.tensor.matmul(ps[:, j, :], w_lo[:, j, w], u_hi[:, k, :], start=False, stop=(k == KT - 1))
                            last.then_inc(chunk_used, 1)

            def norm_2(n, first, read=None):
                if read is not None:
                    pe.wait_ge(bank_read[0], read + 3)
                for k in range(KT):
                    pe.wait_ge(sq_ready, n * KT + (k + 1))
                    for t in range(first, ST):
                        last = nc.tensor.matmul(ps[:, 4, t:t + 1], sq_2[:, k % 2, t * P:(t + 1) * P], ones[:, 0:1],
                                                start=(k == 0 and t == first), stop=(k == KT - 1), skip_group_check=True)
                    last.then_inc(sq_used, 1)
                pe.wait_ge(diag_ready, n + 1)
                if first == 0:
                    nc.tensor.matmul(ps[:, 6, 0:CTX], ones, diag_2[:, 0:CT, :].rearrange("p t q -> p (t q)"), start=True, stop=True)
                nc.tensor.matmul(ps[:, 5, :], ones, diag_2[:, CT:ST, :].rearrange("p t q -> p (t q)"),
                                 start=True, stop=True).then_inc(rb_ready, 1)

            def blocks_2(j, k, hi, lo, need_ctx):
                w = slice(k * P, (k + 1) * P)
                for part, bank in ((X, ps[:, j, :]), (C, ps[:, 4 + j, 0:CTX]))[:2 if need_ctx else 1]:
                    nc.tensor.matmul(bank, w_hi[:, j, w], hi[:, part], start=(k == 0), stop=False)
                    nc.tensor.matmul(bank, w_hi[:, j, w], lo[:, part], start=False, stop=False)
                    last = nc.tensor.matmul(bank, w_lo[:, j, w], hi[:, part], start=False, stop=(k == KT - 1))
                return last

            def chunk_2(g, j, hi, lo, need_ctx=True, pads=0):
                arrive(g, j, pads)
                for k in range(KT):
                    last = blocks_2(j, k, hi(k), lo(k), need_ctx)
                last.then_inc(chunk_used, 1 + pads)

            def normed(g, j, need_ctx=True, pads=0):
                chunk_2(g, j, lambda k: c_hi[:, k, :], lambda k: c_lo[:, k, :], need_ctx, pads)

            def to_tokens(j, z, n):
                pe.wait_ge(z_ready, n + 1)
                for t in range(ST):
                    bank = ps[:, 4 + j, t * P:(t + 1) * P] if t < CT else ps[:, j, (t - CT) * P:(t - CT + 1) * P]
                    last = nc.tensor.transpose(bank, z[:, j % 2, t * P:(t + 1) * P], ident)
                last.then_inc(ztok_ready, 1)

            def turn(j, n):
                pe.wait_ge(z_ready, n + 1)
                nc.tensor.matmul(ps[:, j, :], swap_half, zm[:, j % 2, X], start=True, stop=True).then_inc(zrot_ready, 1)

            def neighborhood(L, need_ctx):
                units, base = natt_units(need_ctx), L * N_UNITS

                def scores(u):
                    h, c, t = units[u]
                    rows, s = slice(h % 2 * HEAD, h % 2 * HEAD + HEAD), 2 * (u % 2)
                    if u >= 2:
                        pe.wait_ge(nneg_ready, base + (u - 1))
                    at = (0 if c else CTX) + t * P
                    query = qn[rows, h // 2, at:at + P]
                    if not c:
                        nc.tensor.matmul(ps[:, s, :], query, kn[rows, h // 2, X], start=True, stop=True)
                    nc.tensor.matmul(ps[:, s + 1, 0:CTX], query, kn[rows, h // 2, C], start=True, stop=True).then_inc(ns_ready, 1)

                def by_key(u):
                    h, c, t = units[u]
                    pe.wait_ge(np_ready, base + (u + 1))
                    if u >= 1:
                        pe.wait_ge(npt_copied, base + u)
                    if not c:
                        for s in range(TT):
                            nc.tensor.transpose(ps[:, 4, s * P:(s + 1) * P], sn[:, u % 2, CTX + s * P:CTX + (s + 1) * P], ident)
                    for s in range(CT):
                        last = nc.tensor.transpose(ps[:, 5, s * P:(s + 1) * P], sn[:, u % 2, s * P:(s + 1) * P], ident)
                    last.then_inc(npt_ready, 1)

                def weighted(u):
                    h, c, t = units[u]
                    rows = slice(h % 2 * HEAD, h % 2 * HEAD + HEAD)
                    pe.wait_ge(npt_copied, base + (u + 1))
                    if h >= 1 and (c, t) == (0, 0):
                        pe.wait_ge(nlo_ready, L * H2 + h)
                    keys = CT if c else ST
                    for s in range(keys):
                        last = nc.tensor.matmul(ps[rows, 6 + c, t * P:(t + 1) * P], vn[:, s, h * HEAD:(h + 1) * HEAD],
                                                pn[:, u % 2, s * P:(s + 1) * P], start=(s == 0), stop=(s == keys - 1))
                    last.then_inc(npv_ready, 1)

                scores(0)
                scores(1)
                for u in range(len(units)):
                    by_key(u)
                    if u + 2 < len(units):
                        scores(u + 2)
                    if u >= 1:
                        weighted(u - 1)
                weighted(len(units) - 1)
                pe.wait_ge(nlo_ready, L * H2 + H2)

            def mlstm(L, first):
                runs, where = gw_layout(first)
                pe.wait_ge(gate_a, L * 3 + 3)
                for t in range(ST):
                    bank = ps[:, 0, t * P:(t + 1) * P] if t < TT else ps[:, 1, (t - TT) * P:(t - TT + 1) * P]
                    last = nc.tensor.transpose(bank, key_w[:, t * P:(t + 1) * P], ident)
                last.then_inc(key_ready, 1)
                pe.wait_ge(key_copied, L + 1)

                def scores(h):
                    rows = slice(h % 2 * HEAD, h % 2 * HEAD + HEAD)
                    for s in range(ST):
                        n = h * ST + s
                        b = 2 * (n % 2)
                        if n >= 2:
                            pe.wait_ge(mg_ready, L * N_UNITS + (n - 1))
                        key = km[rows, h // 2, s * P:(s + 1) * P]
                        nc.tensor.matmul(ps[:, b, first * P:SEQ], key, qm[rows, h // 2, first * P:SEQ], start=True, stop=True)
                        nc.tensor.matmul(ps[:, b + 1, 0:ALL - SEQ], key, qm[rows, h // 2, SEQ:ALL],
                                         start=True, stop=True).then_inc(ms_ready, 1)

                def results(h):
                    b = 4 + 2 * (h % 2)
                    pe.wait_ge(mg_ready, L * N_UNITS + (h + 1) * ST)
                    if h >= 2:
                        pe.wait_ge(head_done, L * H2 + (h - 1))
                    for d in range(2):
                        for t in range(first, ST):
                            seen = key_tiles(d, t)
                            for s in seen:
                                at = where[d, s, t]
                                last = nc.tensor.matmul(ps[:, b + d, t * (HEAD + 1):(t + 1) * (HEAD + 1)], gw[:, h % 2, at:at + P],
                                                        vm[:, s, h, :], start=(s == seen[0]), stop=(s == seen[-1]))
                    last.then_inc(mpv_ready, 1)

                scores(0)
                for h in range(H2):
                    if h + 1 < H2:
                        scores(h + 1)
                    results(h)
                pe.wait_ge(ln_v, L * 6 + 6)
                for f in range(4):
                    for t in range(first, ST):
                        bank = ps[:, 2 * f + 1, t * P:(t + 1) * P] if t < CT else ps[:, 2 * f, (t - CT) * P:(t - CT + 1) * P]
                        last = nc.tensor.transpose(bank, hs[:, t, 2 * f:2 * f + 2, :].rearrange("p h d -> p (h d)"), ident)
                    last.then_inc(yt_ready, 1)

            norm_2(FIRST_MOD, CT)
            for L in range(DEPTH):
                need_ctx = L + 1 < DEPTH
                first = 0 if need_ctx else CT
                g0 = START_2 + L * G2
                nz = L * 16
                norm_2(FIRST_MOD + 1 + 2 * L, 0, g0 - 1 if L else None)
                pe.wait_ge(hlo_ready, (FIRST_MOD + 2 * L + 1) * KT)
                pe.wait_ge(c2_loaded, 16)
                with pe.Fori(0, G_VN) as i:
                    for j in range(RING):
                        normed(g0 + i, j)
                for j in range(RING):
                    normed(g0 + G_VN, j)
                    if j > 0:
                        to_tokens(j - 1, zn, nz + j - 1)
                to_tokens(3, zn, nz + 3)
                normed(g0 + G_GATE, 0, pads=3)
                for j in range(RING):
                    pe.wait_ge(bank_read[j], g0 + G_GATE + 3)
                neighborhood(L, need_ctx)
                with pe.Fori(0, 2) as i:
                    for j in range(RING):
                        normed(g0 + i + G_QM, j)
                        if j > 0:
                            turn(j - 1, i * 4 + (nz + 4 + j - 1))
                    turn(3, i * 4 + (nz + 7))
                for j in range(RING):
                    normed(g0 + G_VM, j)
                    if j > 0:
                        to_tokens(j - 1, zm, nz + 12 + j - 1)
                to_tokens(3, zm, nz + 15)
                for j in range(RING):
                    normed(g0 + G_OM, j)
                for j in range(RING):
                    pe.wait_ge(bank_read[j], g0 + G_OM + 3)
                mlstm(L, first)
                pe.wait_ge(ylo_ready, L * 4 + 4)
                y_hi = lambda k: ym_hi[:, k, :] if k < 4 else yn_hi[:, k - 4, :]
                y_lo = lambda k: ym_lo[:, k, :] if k < 4 else yn_lo[:, k - 4, :]
                with pe.Fori(0, 2) as i:
                    for j in range(RING):
                        chunk_2(g0 + i + G_OUT2, j, y_hi, y_lo, need_ctx)
                norm_2(FIRST_MOD + 2 + 2 * L, first, g0 + G_OUT2 + 1)
                pe.wait_ge(hlo_ready, (FIRST_MOD + 2 * L + 2) * KT)
                with pe.Fori(0, QUARTERS) as q:
                    with pe.Fori(0, 2) as i:
                        for j in range(RING):
                            normed(g0 + q * 4 + i + G_UP, j, need_ctx)
                    with pe.Fori(0, 2) as i:
                        for j in range(RING):
                            arrive(g0 + q * 4 + i + (G_UP + 2), j)
                            for k in range(KT):
                                pe.wait_ge(ulo_ready, q * KT + ((DEPTH + L) * N_MLP + k + 1))
                                last = blocks_2(j, k, u2_hi[:, k, :], u2_lo[:, k, :], need_ctx)
                            last.then_inc(chunk_used, 1)
            norm_2(FIRST_MOD + 1 + 2 * DEPTH, CT)

        @block.scalar
        def _(act):
            def split(g, j):
                act.wait_ge(chunk_used, g * RING + (j + 1))
                act.wait_ge(raw_ready[j % RAW], g * 32 + 16 * (RING // RAW + 1 + j // RAW))
                nc.scalar.activation(w_hi[:, j, :], w_raw[:, j % RAW, :], ACT.Copy).then_inc(hi_ready, 1)

            def norm(n, g, gain_shift=None):
                for k in range(KT):
                    act.wait_ge(bank_read[k % RING], g + (k // RING + 3))
                    if k >= 2:
                        act.wait_ge(sq_used, n * KT + (k - 1))
                    nc.scalar.activation(stage[:, k % 2, :], x[:, k, :], ACT.Square).then_inc(sq_ready, 1)
                act.wait_ge(sq_used, n * KT + KT)
                nc.scalar.activation(rms[:, 0, 0:TT], ps[:, 4, 0:TT], ACT.Sqrt, bias=eps[:, 0:1], scale=1.0 / D_MODEL).then_inc(std_ready, 1)
                for k in range(KT):
                    act.wait_ge(hf_ready, n * KT + (k + 1))
                    nc.scalar.activation(h_hi[:, k, :], tmp[:, k % 2, :], ACT.Copy).then_inc(hhi_ready, 1)

            for j in range(RING):
                act.wait_ge(raw_ready[j % RAW], 16 * (1 + j // RAW))
                nc.scalar.activation(w_hi[:, j, :], w_raw[:, j % RAW, :], ACT.Copy).then_inc(hi_ready, 1)

            with act.Fori(0, DEPTH) as l:
                g0 = l * G1

                def to_stage(g, j):
                    act.wait_ge(chunk_used, g * RING + (j + 1))
                    nc.scalar.activation(stage[:, j % 2, :], ps[:, j, :], ACT.Copy).then_inc(bank_read[j], 1)

                norm(2 * l, g0 - 2)
                for j in range(RING):
                    if j >= 2:
                        act.wait_ge(rope_half_done, l * (2 * N_ROPE) + 2 * (j - 1))
                    to_stage(g0, j)
                    split(g0, j)
                with act.Fori(0, 2) as i:
                    for j in range(RING):
                        act.wait_ge(rope_half_done, l * (2 * N_ROPE) + i * 8 + 2 * (3 + j))
                        to_stage(g0 + i + G_RET, j)
                        split(g0 + i + G_RET, j)
                for j in range(2):
                    act.wait_ge(rope_half_done, l * (2 * N_ROPE) + 2 * (11 + j))
                    to_stage(g0 + G_KV, j)
                    split(g0 + G_KV, j)
                for j in range(2, RING):
                    act.sem_inc(bank_read[j], 1)
                    split(g0 + G_KV, j)

                def probabilities_by_key(u):
                    n = units[u][0]
                    act.wait_ge(pt_ready, l * N_ATT + (u + 1))
                    if u >= 2:
                        act.wait_ge(pv_ready, l * N_ATT + (u - 1))
                    b = slice(0 if n else 1, 2)
                    nc.scalar.activation(pt_sb[:, u % 2, b, :, :],
                                         ps[:, 2 + u % 2, :].rearrange("p (b e q) -> p b e q", b=2, e=2)[:, b, :, :],
                                         ACT.Copy).then_inc(pt_copied, 1)

                def output_upper(u):
                    n, g, i = units[u]
                    rows = slice(g * HEAD, (g + 1) * HEAD)
                    act.wait_ge(pv_ready, l * N_ATT + (u + 1))
                    nc.scalar.activation(o_hi[rows, 2 * i:2 * i + 2, n * P:(n + 1) * P],
                                         ps[rows, 4 + u % 2, 0:2 * P].rearrange("p (e q) -> p e q", e=2), ACT.Copy).then_inc(ohi_ready, 1)

                for u in range(N_ATT):
                    wide = 2 * P if units[u][0] else P
                    act.wait_ge(nm_ready, l * N_ATT + (u + 1))
                    for e in range(2):
                        nc.scalar.activation(p_sb[:, u % 2, e, 0:wide], s_sb[:, u % 2, e, 0:wide], ACT.Exp,
                                             bias=tiny[:, u % 2, e:e + 1], accum_out=tiny[:, u % 2, 4 + e:5 + e])
                    nc.scalar.activation(tiny[:, u % 2, 6:8], tiny[:, u % 2, 2:4], ACT.Exp).then_inc(exp_done, 1)
                    if u >= 1:
                        probabilities_by_key(u - 1)
                    if u >= 2:
                        output_upper(u - 2)
                probabilities_by_key(N_ATT - 1)
                output_upper(N_ATT - 2)
                output_upper(N_ATT - 1)

                with act.Fori(0, 2) as i:
                    for j in range(RING):
                        act.wait_ge(v_done, l * N_VT + i * 4 + (j + 1) if j < 1 else l * N_VT + i * 4 + j)
                        to_stage(g0 + i + G_RV, j)
                        split(g0 + i + G_RV, j)
                for h in range(RET_HEADS):
                    act.wait_ge(inner_ready, l * RET_HEADS + (h + 1))
                    b = 4 + 2 * (h % 2)
                    for e in range(2):
                        nc.scalar.activation(r_raw[:, 2 * h + e, :], ps[:, b + e, :], ACT.Copy).then_inc(rcopy_done, 1)
                    if h >= 1:
                        act.wait_ge(rsq_used, l * RET_HEADS + h)
                    for e in range(2):
                        nc.scalar.activation(stage_2[:, e, :], ps[:, b + e, :], ACT.Square).then_inc(rcopy_done, 1)
                act.wait_ge(rsq_used, l * RET_HEADS + RET_HEADS)
                nc.scalar.activation(rms[:, 0, 0:16], ps[:, 3, 0:16], ACT.Sqrt, bias=eps[:, 0:1], scale=1.0 / RET_V).then_inc(rstd_ready, 1)
                with act.Fori(0, 2) as i:
                    g = g0 + i + G_RG
                    for j in range(RING):
                        act.wait_ge(chunk_used, g * RING + (j + 1))
                        act.wait_ge(bank_read[(j + 2) % RING], g + (3 if j >= 2 else 2))
                        nc.scalar.activation(stage[:, j % 2, :], ps[:, j, :], ACT.Tanh, scale=0.5).then_inc(tanh_ready, 1)
                        split(g, j)
                        act.wait_ge(rr_ready, l * KT + i * 4 + (j + 1))
                        nc.scalar.activation(r_hi[:, ds(i * 4 + j, 1), :].rearrange("p o t -> p (o t)"), tmp_2[:, j % 2, :], ACT.Copy).then_inc(rhi_ready, 1)
                for j in range(RING):
                    act.wait_ge(chunk_used, (g0 + G_WA) * RING + (j + 1))
                    nc.scalar.activation(y_a[:, 2 * j, :], ps[:, j, :], ACT.Copy)
                    nc.scalar.activation(y_a[:, 2 * j + 1, :], ps[:, 4 + j, :], ACT.Copy).then_inc(bank_read[j], 1)
                    split(g0 + G_WA, j)
                with act.Fori(0, 2) as i:
                    for m in range(RING):
                        for c in range(3 * m, 3 * m + 3):
                            g, j = g0 + i * 3 + (G_MIX + c // RING), c % RING
                            if c % 3 < 2:
                                act.wait_ge(chunk_used, g * RING + (j + 1))
                                nc.scalar.activation((stage, stage_2)[c % 3][:, m % 2, :], ps[:, j, :], ACT.Tanh, scale=0.5).then_inc(bank_read[j], 1)
                            split(g, j)
                        act.wait_ge(mx_ready, l * KT + i * 4 + (m + 1))
                        nc.scalar.activation(mix_hi[:, ds(i * 4 + m, 1), :].rearrange("p o t -> p (o t)"), tmp_2[:, m % 2, :], ACT.Copy).then_inc(mhi_ready, 1)
                with act.Fori(0, 2) as i:
                    for j in range(RING):
                        split(g0 + i + G_OUT, j)
                norm(2 * l + 1, g0 + G_OUT)
                act.dma_start(c_raw[:, :, :], dram["c"].broadcast_to([P, 2, D_MODEL])).then_inc(c_loaded, 16)
                act.wait_ge(c_loaded, l * 16 + 16)
                nc.scalar.activation(c_silu[:, :, :], c_raw[:, :, :], ACT.Tanh, scale=0.5).then_inc(ct_ready, 1)

                def ada_load(n):
                    act.wait_ge(ada_used, n + 1)
                    for s in range(3):
                        act.dma_start(ada_w[:, s, :], dram["ada"][ds(n * 3 + s, 1), :, :].rearrange("o p k -> p (o k)")).then_inc(ada_ready[s], 16)

                with act.Fori(0, QUARTERS) as q:
                    with act.Fori(0, 2) as i:
                        g = g0 + q * 4 + i + G_MLP
                        ada_load(l * 16 + q * 4 + i)
                        for j in range(RING):
                            act.wait_ge(chunk_used, g * RING + (j + 1))
                            nc.scalar.activation(stage[:, j % 2, :], ps[:, j, :], ACT.Relu).then_inc(bank_read[j], 1)
                            split(g, j)
                            act.wait_ge(v2_ready, l * N_MLP + q * KT + i * 4 + (j + 1))
                            nc.scalar.activation(u_hi[:, ds(i * 4 + j, 1), :].rearrange("p o t -> p (o t)"), tmp[:, j % 2, :], ACT.Copy).then_inc(uhi_ready, 1)
                    with act.Fori(0, 2) as i:
                        ada_load(l * 16 + q * 4 + i + 2)
                        for j in range(RING):
                            split(g0 + q * 4 + i + (G_MLP + 2), j)

            def norm_2(n, first, m, L, col, read=None):
                for k in range(KT):
                    if read is not None:
                        act.wait_ge(bank_read[k % RING], read + (k // RING + 3))
                    else:
                        act.wait_ge(xf_done, k + 1)
                    if k >= 2:
                        act.wait_ge(sq_used, n * KT + (k - 1))
                    if first == 0:
                        nc.scalar.activation(sq_2[:, k % 2, C], cx[:, k, :], ACT.Square)
                    nc.scalar.activation(sq_2[:, k % 2, X], x[:, k, :], ACT.Square).then_inc(sq_ready, 1)
                act.wait_ge(sq_used, n * KT + KT)
                nc.scalar.activation(rms[:, 0, first:ST], ps[:, 4, first:ST], ACT.Sqrt, bias=eps[:, 0:1], scale=1.0 / D_MODEL).then_inc(std_ready, 1)
                if m is None:
                    return
                for k in range(KT):
                    act.wait_ge(hf_ready, m * KT + (k + 1))
                    at = L * ADA + col + k
                    if first == 0:
                        nc.scalar.activation(c_hi[:, k, C], hf_2[:, k % 2, C], ACT.Identity, bias=mod[:, 1, at:at + 1])
                    nc.scalar.activation(c_hi[:, k, X], hf_2[:, k % 2, X], ACT.Identity, bias=mod[:, 0, at:at + 1]).then_inc(hhi_ready, 1)

            def z_slot(g, j):
                act.wait_ge(chunk_used, g * RING + (j + 1))
                act.wait_ge(bank_read[(j + 2) % RING], g + (3 if j >= 2 else 2))

            def copy_out(g, j, z):
                z_slot(g, j)
                nc.scalar.activation(z[:, j % 2, C], ps[:, 4 + j, 0:CTX], ACT.Copy)
                nc.scalar.activation(z[:, j % 2, X], ps[:, j, :], ACT.Copy).then_inc(z_ready, 1)
                split(g, j)

            def load_bias(L, h):
                act.dma_start(bias[:, h % 2, :], dram["rpb"][L, h, :, :]).then_inc(bias_loaded[h % 2], 16)

            def neighborhood(L, need_ctx):
                units, base = natt_units(need_ctx), L * N_UNITS
                per = len(units) // H2

                def context_scores(u):
                    act.wait_ge(ns_ready, base + (u + 1))
                    if u >= 2:
                        act.wait_ge(npt_ready, base + (u - 1))
                    nc.scalar.activation(sn[:, u % 2, C], ps[:, 2 * (u % 2) + 1, 0:CTX], ACT.Copy, scale=HEAD ** -0.5).then_inc(nsc_done, 1)

                def by_key(u):
                    act.wait_ge(npt_ready, base + (u + 1))
                    if u >= 2:
                        act.wait_ge(npv_ready, base + (u - 1))
                    if not units[u][1]:
                        nc.scalar.activation(pn[:, u % 2, X], ps[:, 4, :], ACT.Copy)
                        nc.scalar.activation(pn[:, u % 2, C], ps[:, 5, 0:CTX], ACT.Copy).then_inc(npt_copied, 1)
                    else:
                        nc.scalar.activation(pn[:, u % 2, C], ps[:, 5, 0:CTX], ACT.Copy).then_inc(npt_copied, 1)

                def upper(h):
                    rows = slice(h % 2 * HEAD, h % 2 * HEAD + HEAD)
                    act.wait_ge(npv_ready, base + (h + 1) * per)
                    if need_ctx:
                        nc.scalar.activation(yn_hi[rows, h // 2, C], ps[rows, 7, 0:CTX], ACT.Copy)
                    nc.scalar.activation(yn_hi[rows, h // 2, X], ps[rows, 6, :], ACT.Copy).then_inc(nhi_ready, 1)
                    if h + 2 < H2:
                        load_bias(L, h + 2)

                context_scores(0)
                for u in range(len(units)):
                    wide = CTX if units[u][1] else ALL
                    if u + 1 < len(units):
                        context_scores(u + 1)
                    act.wait_ge(nneg_ready, base + (u + 1))
                    nc.scalar.activation(sn[:, u % 2, 0:wide], sn[:, u % 2, 0:wide], ACT.Exp, bias=tiny[:, u % 2, 0:1],
                                         accum_out=tiny[:, u % 2, 1:2]).then_inc(nexp_done, 1)
                    if u >= 1:
                        by_key(u - 1)
                    if u >= 2 and (u - 1) % per == 0:
                        upper((u - 2) // per)
                by_key(len(units) - 1)
                upper(H2 - 1)

            def gate_rows(L):
                f = slice(64, P)
                act.wait_ge(gate_v, L * 9 + 2)
                nc.scalar.activation(cum_f[f, :], cum_f[f, :], ACT.Exp).then_inc(gate_a, 1)
                act.wait_ge(gate_a, L * 3 + 1)
                nc.scalar.activation(cum_f[f, :], cum_f[f, :], ACT.Ln, bias=ones[f, 0:1]).then_inc(gate_a, 1)

            def gate_rows_end(L):
                act.wait_ge(gate_v, L * 9 + 9)
                for d in range(2):
                    act.dma_start(m_spill[d, :, :], run_m[32 * d:32 * d + H2, :]).then_inc(m_stored, 16)
                nc.scalar.activation(key_w[64:P, :], key_w[64:P, :], ACT.Exp, scale=-1.0).then_inc(gate_a, 1)

            def mlstm(L, first):
                runs, where = gw_layout(first)
                last_row = first * P

                def load_maxima(h):
                    act.dma_start(m_row[:, h % 2, :, :], m_spill[:, h, :].rearrange("d (o t) -> o d t", o=1).broadcast_to([P, 2, ALL])).then_inc(m_loaded[h % 2], 16)

                act.wait_ge(m_stored, (L + 1) * 32)
                act.wait_ge(spilled, (L + 1) * 32)
                load_maxima(0)
                load_maxima(1)
                act.wait_ge(key_ready, L + 1)
                nc.scalar.activation(key_t[:, 0:TT, :], ps[:, 0, :].rearrange("p (t c) -> p t c", t=TT), ACT.Copy)
                nc.scalar.activation(key_t[:, TT:ST, :], ps[:, 1, 0:CTX].rearrange("p (t c) -> p t c", t=CT), ACT.Copy).then_inc(key_copied, 1)
                act.wait_ge(key_copied, L + 1)
                for h in range(H2):
                    act.wait_ge(m_loaded[h % 2], (L * 4 + h // 2 + 1) * 16)
                    act.wait_ge(mdiag_ready, L * H2 + h + 1)
                    for s in range(ST):
                        for d, t0, t1, at in runs[s]:
                            for a, b in ((t0, s), (s + 1, t1)) if t0 <= s < t1 else ((t0, t1),):
                                if a < b:
                                    last = nc.scalar.activation(gw[:, h % 2, at + (a - t0) * P:at + (b - t0) * P], m_row[:, h % 2, d, a * P:b * P], ACT.Exp,
                                                                bias=key_t[:, s, 32 * d + h:32 * d + h + 1], scale=-1.0)
                            if t0 <= s < t1:
                                one = gw[:, h % 2, at + (s - t0) * P:at + (s - t0 + 1) * P]
                                last = nc.scalar.activation(one, one, ACT.Exp, scale=-1.0)
                        last.then_inc(mw_ready, 1)
                    if h + 2 < H2:
                        act.wait_ge(mw_ready, L * N_UNITS + (h + 1) * ST)
                        load_maxima(h + 2)
                act.wait_ge(ln_v, L * 6 + 3)
                nc.scalar.activation(hq[:, first:ST, :, :], hs[:, first:ST, :, :], ACT.Square).then_inc(ln_a, 1)
                act.wait_ge(ln_v, L * 6 + 4)
                nc.scalar.activation(cols[:, 2, first * H2:ST * H2], cols[:, 1, first * H2:ST * H2], ACT.Sqrt, bias=eps[:, 0:1], scale=1.0 / HEAD).then_inc(ln_a, 1)
                act.wait_ge(yt_ready, L * 4 + 4)
                act.dma_start(x[:, :, :], x_spill).then_inc(reloaded, 16)
                act.dma_start(cx[:, :, :], cx_spill).then_inc(reloaded, 16)
                for f in range(4):
                    act.wait_ge(yu_ready, L * 4 + (f + 1))
                    nc.scalar.activation(ym_hi[:, f, last_row:ALL], yu[:, f, last_row:ALL], ACT.Copy).then_inc(yhi_ready, 1)

            act.wait_ge(hlo_ready, FIRST_MOD * KT)
            act.dma_start(c2[:, :], dram["c2"]).then_inc(c2_loaded, 16)
            act.dma_start(cx[:, :, :], dram["ctx"]).then_inc(cx_loaded, 16)
            act.wait_ge(ada_used, DEPTH * (ADA // 3) + 1)
            norm_2(FIRST_MOD, CT, None, None, None, START_2 - 2)
            act.wait_ge(cx_loaded, 16)
            for L in range(DEPTH):
                need_ctx = L + 1 < DEPTH
                first = 0 if need_ctx else CT
                g0 = START_2 + L * G2
                norm_2(FIRST_MOD + 1 + 2 * L, 0, FIRST_MOD + 2 * L, L, 0, g0 - 2 if L else None)
                act.wait_ge(hlo_ready, (FIRST_MOD + 2 * L + 1) * KT)
                act.dma_start(x_spill, x[:, :, :]).then_inc(spilled, 16)
                act.dma_start(cx_spill, cx[:, :, :]).then_inc(spilled, 16)
                for t, dst in enumerate((qn, kn)):
                    for j in range(RING):
                        act.wait_ge(chunk_used, (g0 + t) * RING + (j + 1))
                        nc.scalar.activation(dst[:, j, C], ps[:, 4 + j, 0:CTX], ACT.Copy)
                        nc.scalar.activation(dst[:, j, X], ps[:, j, :], ACT.Copy).then_inc(bank_read[j], 1)
                        split(g0 + t, j)
                load_bias(L, 0)
                load_bias(L, 1)
                for j in range(RING):
                    copy_out(g0 + G_VN, j, zn)
                split(g0 + G_GATE, 0)
                for j in range(1, RING):
                    act.sem_inc(bank_read[j], 1)
                    split(g0 + G_GATE, j)
                neighborhood(L, need_ctx)
                gate_rows(L)
                for t, dst in enumerate((qm, km)):
                    for j in range(RING):
                        z_slot(g0 + t + G_QM, j)
                        nc.scalar.activation(dst[:, j, C], ps[:, 4 + j, 0:CTX], ACT.Copy)
                        nc.scalar.activation(zm[:, j % 2, X], ps[:, j, :], ACT.Copy).then_inc(z_ready, 1)
                        split(g0 + t + G_QM, j)
                    if t == 0:
                        gate_rows_end(L)
                for j in range(RING):
                    copy_out(g0 + G_VM, j, zm)
                act.wait_ge(bank_read[3], g0 + G_VM + 3)
                for j in range(RING):
                    act.wait_ge(chunk_used, (g0 + G_OM) * RING + (j + 1))
                    nc.scalar.activation(om[:, j, C], ps[:, 4 + j, 0:CTX], ACT.Tanh, scale=0.5)
                    nc.scalar.activation(om[:, j, X], ps[:, j, :], ACT.Tanh, scale=0.5).then_inc(bank_read[j], 1)
                    split(g0 + G_OM, j)
                mlstm(L, first)
                with act.Fori(0, 2) as i:
                    for j in range(RING):
                        split(g0 + i + G_OUT2, j)
                norm_2(FIRST_MOD + 2 + 2 * L, first, FIRST_MOD + 2 * L + 1, L, 3 * KT, g0 + G_OUT2)
                lo = first * P
                with act.Fori(0, QUARTERS) as q:
                    with act.Fori(0, 2) as i:
                        g = g0 + q * 4 + i + G_UP
                        for j in range(RING):
                            act.wait_ge(chunk_used, g * RING + (j + 1))
                            if need_ctx:
                                nc.scalar.activation(sq_2[:, j % 2, C], ps[:, 4 + j, 0:CTX], ACT.Relu)
                            nc.scalar.activation(sq_2[:, j % 2, X], ps[:, j, :], ACT.Relu).then_inc(bank_read[j], 1)
                            split(g, j)
                            act.wait_ge(v2_ready, q * KT + i * 4 + ((DEPTH + L) * N_MLP + j + 1))
                            nc.scalar.activation(u2_hi[:, ds(i * 4 + j, 1), lo:ALL].rearrange("p o t -> p (o t)"), hf_2[:, j % 2, lo:ALL], ACT.Copy).then_inc(uhi_ready, 1)
                    with act.Fori(0, 2) as i:
                        for j in range(RING):
                            split(g0 + q * 4 + i + (G_UP + 2), j)
            norm_2(FIRST_MOD + 1 + 2 * DEPTH, CT, None, None, None, START_2 + DEPTH * G2 - 2)

        @block.vector
        def _(dve):
            def spread(col):
                return (diag[:, :, :], ident.rearrange("p (o q) -> p o q", o=1).broadcast_to([P, TT, P]),
                        rms[:, 1, col:col + TT].rearrange("p (t o) -> p t o", o=1).broadcast_to([P, TT, P]), ALU.mult)

            def norm(n):
                dve.wait_ge(std_ready, n + 1)
                nc.vector.reciprocal(rms[:, 1, 0:TT], rms[:, 0, 0:TT]).then_inc(rinv_ready, 1)
                dve.wait_ge(rinv_ready, n + 1)
                nc.vector.tensor_tensor(*spread(0)).then_inc(diag_ready, 1)
                dve.wait_ge(rb_ready, n + 1)

                def lower(k):
                    dve.wait_ge(hhi_ready, n * KT + (k + 1))
                    nc.vector.tensor_tensor(h_lo[:, k, :], tmp[:, k % 2, :], h_hi[:, k, :].bitcast(F), ALU.subtract).then_inc(hlo_ready, 1)

                for k in range(KT):
                    if k >= 2:
                        dve.wait_ge(hlo_ready, n * KT + (k - 1))
                    nc.vector.scalar_tensor_tensor(tmp[:, k % 2, :], x[:, k, :], gain_now[:, k:k + 1], ps[:, 5, :],
                                                   ALU.mult, ALU.mult).then_inc(hf_ready, 1)
                    if k >= 1:
                        lower(k - 1)
                lower(KT - 1)

            nc.vector.memset(eps[:, :], EPS).then_inc(eps_set, 1)
            dve.wait_ge(eps_set, 1)
            dve.wait_ge(x_loaded, 16)
            dve.wait_ge(vec_loaded, 16)
            for j in range(RING):
                dve.sem_inc(bank_read[j], 2)
            dve.sem_inc(ada_used, 1)
            dve.wait_ge(c0_loaded, 16)
            dve.wait_ge(c1_loaded, 16)

            with dve.Fori(0, DEPTH) as l:
                g0 = l * G1
                nc.vector.tensor_copy(gain_now[:, :], vec[:, ds(l * KT + V_GMIX, KT)]).then_inc(layer_vec, 1)
                nc.vector.tensor_copy(sink_now[:, 0, :], vec[:, ds(l * ATT_HEADS + V_SINK, ATT_HEADS)]).then_inc(layer_vec, 1)
                dve.wait_ge(layer_vec, l * 4 + 2)
                nc.vector.tensor_scalar(sink_now[:, 1, :], sink_now[:, 0, :], -1.0, None, ALU.mult).then_inc(layer_vec, 1)
                norm(2 * l)

                def rope(n, g, j, cos, sin, dst):
                    dve.wait_ge(bank_read[j], g + 3)
                    if not isinstance(n, int) or n:
                        dve.wait_ge(rope_done, l * N_ROPE + n)
                    nc.vector.tensor_tensor(tmp[:, j % 2, :], stage[:, j % 2, :], cos, ALU.mult).then_inc(rope_half_done, 1)
                    dve.wait_ge(rot_ready, l * N_ROPE + n + 1)
                    nc.vector.tensor_tensor(tmp_2[:, j % 2, :], ps[:, 4 + j % 2, :], sin, ALU.mult).then_inc(rope_half_done, 1)
                    dve.wait_ge(rope_half_done, l * (2 * N_ROPE) + n * 2 + 2)
                    nc.vector.tensor_tensor(dst, tmp[:, j % 2, :], tmp_2[:, j % 2, :], ALU.add).then_inc(rope_done, 1)

                for j in range(RING):
                    rope(j, g0, j, att_cos, att_sin, aq[:, j, :])
                with dve.Fori(0, 2) as i:
                    for j in range(RING):
                        rope(i * 4 + (4 + j), g0 + i + G_RET, j, ret_cos, ret_sin,
                             rqk[:, ds(i * 4 + j, 1), :].rearrange("p o t -> p (o t)"))
                rope(12, g0 + G_KV, 0, att_cos, att_sin, ak[:, :])
                dve.wait_ge(vt_ready, l * N_VT + 1)
                nc.vector.tensor_copy(av[:, :, :], ps[:, 6, :].rearrange("p (t d) -> p t d", t=TT)).then_inc(v_done, 1)

                def normalised(u):
                    wide = 2 * P if units[u][0] else P
                    c = tiny[:, u % 2, :]
                    dve.wait_ge(exp_done, l * N_ATT + (u + 1))
                    nc.vector.tensor_tensor(c[:, 8:10], c[:, 4:6], c[:, 6:8], ALU.add).then_inc(den_done, 1)
                    dve.wait_ge(den_done, l * (2 * N_ATT) + (2 * u + 1))
                    nc.vector.reciprocal(c[:, 10:12], c[:, 8:10]).then_inc(den_done, 1)
                    dve.wait_ge(den_done, l * (2 * N_ATT) + (2 * u + 2))
                    for e in range(2):
                        last = nc.vector.tensor_scalar(p_sb[:, u % 2, e, 0:wide], p_sb[:, u % 2, e, 0:wide], c[:, 10 + e:11 + e], None, ALU.mult)
                    last.then_inc(p_ready, 1)

                def output_lower(u):
                    n, g, i = units[u]
                    rows = slice(g * HEAD, (g + 1) * HEAD)
                    at = (rows, slice(2 * i, 2 * i + 2), slice(n * P, (n + 1) * P))
                    dve.wait_ge(ohi_ready, l * N_ATT + (u + 1))
                    nc.vector.tensor_tensor(o_lo[at], ps[rows, 4 + u % 2, 0:2 * P].rearrange("p (e q) -> p e q", e=2),
                                            o_hi[at].bitcast(F), ALU.subtract).then_inc(olo_ready, 1)

                for u in range(N_ATT):
                    n, g, i = units[u]
                    wide = 2 * P if n else P
                    c, h = tiny[:, u % 2, :], 4 * g + 2 * i
                    dve.wait_ge(sc_ready, l * N_ATT + (u + 1))
                    if u >= 2:
                        dve.wait_ge(exp_done, l * N_ATT + (u - 1))
                    nc.vector.scalar_tensor_tensor(s_sb[:, u % 2, :, 0:wide], ps[:, u % 2, :].rearrange("p (e k) -> p e k", e=2)[:, :, 0:wide],
                                                   HEAD ** -0.5, att_mask[:, :, 2 * P - wide:2 * P], ALU.mult, ALU.add).then_inc(s_done, 1)
                    dve.wait_ge(s_done, l * N_ATT + (u + 1))
                    nc.vector.tensor_reduce(c[:, 12:14], s_sb[:, u % 2, :, 0:wide], AX.X, ALU.max).then_inc(mx_done, 1)
                    dve.wait_ge(mx_done, l * (2 * N_ATT) + (2 * u + 1))
                    nc.vector.scalar_tensor_tensor(c[:, 0:2], c[:, 12:14], -1.0, sink_now[:, 1, h:h + 2], ALU.mult, ALU.min).then_inc(mx_done, 1)
                    dve.wait_ge(mx_done, l * (2 * N_ATT) + (2 * u + 2))
                    nc.vector.tensor_tensor(c[:, 2:4], c[:, 0:2], sink_now[:, 0, h:h + 2], ALU.add).then_inc(nm_ready, 1)
                    if u >= 1:
                        normalised(u - 1)
                    if u >= 2:
                        output_lower(u - 2)
                normalised(N_ATT - 1)
                output_lower(N_ATT - 2)
                output_lower(N_ATT - 1)

                with dve.Fori(0, 2) as i:
                    for j in range(RING):
                        dve.wait_ge(vt_ready, l * N_VT + i * 4 + (2 + j))
                        nc.vector.tensor_copy(rv[:, :, ds(i * 4 * P + j * P, P)], ps[:, 6, :].rearrange("p (t d) -> p t d", t=TT)).then_inc(v_done, 1)
                for h in range(RET_HEADS):
                    if h >= 2:
                        dve.wait_ge(inner_ready, l * RET_HEADS + (h - 1))
                    for t in range(TT):
                        dve.wait_ge(rs_ready, l * 16 + (4 * h + (t + 1 if t < 2 else 4)))
                        c = slice(RET_COL[t], RET_COL[t + 1])
                        wide = SEQ - t * P
                        src = ps[:, t, 0:wide] if t < 3 else ps[:, 2, 256:384]
                        nc.vector.tensor_tensor(a_sb[h % 2][:, c], src, decay[:, h, 0:wide], ALU.mult).then_inc(a_ready, 1)
                dve.wait_ge(rstd_ready, l + 1)
                nc.vector.reciprocal(rms[:, 1, 0:16], rms[:, 0, 0:16]).then_inc(rrinv_ready, 1)
                dve.wait_ge(rrinv_ready, l + 1)
                for h in range(RET_HEADS):
                    if h >= 1:
                        dve.wait_ge(rrb_ready, l * RET_HEADS + h)
                    nc.vector.tensor_tensor(*spread(4 * h)).then_inc(rdiag_ready, 1)
                with dve.Fori(0, 2) as i:
                    dve.wait_ge(rrb_ready, l * RET_HEADS + RET_HEADS)
                    g = g0 + i + G_RG

                    def ret_lower(j):
                        dve.wait_ge(rhi_ready, l * KT + i * 4 + (j + 1))
                        one = (slice(None), ds(i * 4 + j, 1), slice(None))
                        nc.vector.tensor_tensor(r_lo[one].rearrange("p o t -> p (o t)"), tmp_2[:, j % 2, :],
                                                r_hi[one].rearrange("p o t -> p (o t)").bitcast(F), ALU.subtract).then_inc(rlo_ready, 1)

                    for j in range(RING):
                        dve.wait_ge(tanh_ready, l * KT + i * 4 + (j + 1))
                        nc.vector.scalar_tensor_tensor(stage_2[:, j % 2, :], stage[:, j % 2, :], 1.0, ps[:, j, :], ALU.add, ALU.mult).then_inc(bank_read[j], 1)
                        nc.vector.tensor_tensor(tmp[:, j % 2, :], r_raw[:, ds(i * 4 + j, 1), :].rearrange("p o t -> p (o t)"),
                                                ps[:, ds(i * 2 + (4 + j // 2), 1), :].rearrange("p o t -> p (o t)"), ALU.mult).then_inc(sl_ready, 1)
                        dve.wait_ge(sl_ready, l * KT + i * 4 + (j + 1))
                        dve.wait_ge(bank_read[j], g + 3)
                        if j >= 2:
                            dve.wait_ge(rlo_ready, l * KT + i * 4 + (j - 1))
                        nc.vector.tensor_tensor(tmp_2[:, j % 2, :], stage_2[:, j % 2, :], tmp[:, j % 2, :], ALU.mult).then_inc(rr_ready, 1)
                        if j >= 1:
                            ret_lower(j - 1)
                    ret_lower(RING - 1)
                    dve.wait_ge(rlo_ready, l * KT + i * 4 + RING)
                with dve.Fori(0, 2) as i:
                    for m in range(RING):
                        (ga, ja), (gb, jb), (gy, jy) = [(g0 + i * 3 + (G_MIX + c // RING), c % RING) for c in range(3 * m, 3 * m + 3)]
                        one = (slice(None), ds(i * 4 + m, 1), slice(None))
                        dve.wait_ge(bank_read[ja], ga + 3)
                        nc.vector.scalar_tensor_tensor(tmp[:, m % 2, :], stage[:, m % 2, :], 1.0, y_a[one].rearrange("p o t -> p (o t)"),
                                                       ALU.add, ALU.mult).then_inc(t12_ready, 1)
                        dve.wait_ge(bank_read[jb], gb + 3)
                        dve.wait_ge(chunk_used, gy * RING + (jy + 1))
                        nc.vector.scalar_tensor_tensor(tmp_3[:, m % 2, :], stage_2[:, m % 2, :], 1.0, ps[:, jy, :],
                                                       ALU.add, ALU.mult).then_inc(bank_read[jy], 1)
                        dve.wait_ge(t12_ready, l * KT + i * 4 + (m + 1))
                        dve.wait_ge(bank_read[jy], gy + 3)
                        if m >= 2:
                            dve.wait_ge(mlo_ready, l * KT + i * 4 + (m - 1))
                        nc.vector.scalar_tensor_tensor(tmp_2[:, m % 2, :], tmp_3[:, m % 2, :], 0.5, tmp[:, m % 2, :],
                                                       ALU.mult, ALU.add).then_inc(mx_ready, 1)
                        dve.wait_ge(mhi_ready, l * KT + i * 4 + (m + 1))
                        nc.vector.tensor_tensor(mix_lo[one].rearrange("p o t -> p (o t)"), tmp_2[:, m % 2, :],
                                                mix_hi[one].rearrange("p o t -> p (o t)").bitcast(F), ALU.subtract).then_inc(mlo_ready, 1)
                    dve.wait_ge(mlo_ready, l * KT + i * 4 + RING)
                with dve.Fori(0, 2) as i:
                    for j in range(RING):
                        dve.wait_ge(chunk_used, (g0 + i + G_OUT) * RING + (j + 1))
                        one = x[:, ds(i * 4 + j, 1), :].rearrange("p o t -> p (o t)")
                        nc.vector.scalar_tensor_tensor(one, ps[:, j, :], 0.5, one, ALU.mult, ALU.add).then_inc(bank_read[j], 1)
                nc.vector.tensor_copy(gain_now[:, :], vec[:, ds(l * KT + V_GMLP, KT)]).then_inc(layer_vec, 1)
                dve.wait_ge(layer_vec, l * 4 + 4)
                norm(2 * l + 1)
                dve.wait_ge(ct_ready, l + 1)
                nc.vector.scalar_tensor_tensor(c_silu[:, :, :], c_silu[:, :, :], 1.0, c_raw[:, :, :], ALU.add, ALU.mult).then_inc(cs_ready, 1)
                def ada_products(n):
                    for s in range(3):
                        dve.wait_ge(ada_ready[s], n * 16 + 16)
                        for v in range(2):
                            if s or v:
                                dve.wait_ge(ada_sum, n * 6 + (2 * s + v))
                            nc.vector.scalar_tensor_tensor(ada_junk[:, :], ada_w[:, s, :], 0.5, c_silu[:, v, :], ALU.mult, ALU.mult,
                                                           accum_out=mod_3[:, v, s:s + 1]).then_inc(ada_sum, 1)
                    dve.wait_ge(ada_sum, n * 6 + 6)
                    nc.vector.tensor_copy(mod[:, :, ds(n * 3, 3)], mod_3[:, :, :]).then_inc(ada_used, 1)

                with dve.Fori(0, QUARTERS) as q:
                    with dve.Fori(0, 2) as i:
                        dve.wait_ge(cs_ready, l + 1)
                        g = g0 + q * 4 + i + G_MLP

                        def hidden_lower(j):
                            dve.wait_ge(uhi_ready, l * N_MLP + q * KT + i * 4 + (j + 1))
                            one = (slice(None), ds(i * 4 + j, 1), slice(None))
                            nc.vector.tensor_tensor(u_lo[one].rearrange("p o t -> p (o t)"), tmp[:, j % 2, :],
                                                    u_hi[one].rearrange("p o t -> p (o t)").bitcast(F), ALU.subtract).then_inc(ulo_ready, 1)

                        for j in range(RING):
                            dve.wait_ge(bank_read[j], g + 3)
                            if j >= 2:
                                dve.wait_ge(ulo_ready, l * N_MLP + q * KT + i * 4 + (j - 1))
                            nc.vector.tensor_tensor(tmp[:, j % 2, :], stage[:, j % 2, :], stage[:, j % 2, :], ALU.mult).then_inc(v2_ready, 1)
                            if j >= 1:
                                hidden_lower(j - 1)
                        hidden_lower(RING - 1)
                        dve.wait_ge(ulo_ready, l * N_MLP + q * KT + i * 4 + RING)
                        ada_products(l * 16 + q * 4 + i)
                    with dve.Fori(0, 2) as i:
                        g = g0 + q * 4 + i + (G_MLP + 2)
                        for j in range(RING):
                            dve.wait_ge(chunk_used, g * RING + (j + 1))
                            one = x[:, ds(i * 4 + j, 1), :].rearrange("p o t -> p (o t)")
                            nc.vector.tensor_tensor(one, ps[:, j, :], one, ALU.add).then_inc(bank_read[j], 1)
                        ada_products(l * 16 + q * 4 + i + 2)

            def norm_2(n, first):
                dve.wait_ge(std_ready, n + 1)
                nc.vector.reciprocal(rms[:, 1, first:ST], rms[:, 0, first:ST]).then_inc(rinv_ready, 1)
                dve.wait_ge(rinv_ready, n + 1)
                wide = [P, ST - first, P]
                nc.vector.tensor_tensor(diag_2[:, first:ST, :], ident.rearrange("p (o q) -> p o q", o=1).broadcast_to(wide),
                                        rms[:, 1, first:ST].rearrange("p (t o) -> p t o", o=1).broadcast_to(wide), ALU.mult).then_inc(diag_ready, 1)
                dve.wait_ge(rb_ready, n + 1)

            def plain(n, gain):
                norm_2(n, CT)
                for k in range(KT):
                    nc.vector.scalar_tensor_tensor(x[:, k, :], x[:, k, :], vec[:, gain + k:gain + k + 1], ps[:, 5, :],
                                                   ALU.mult, ALU.mult).then_inc(xf_done, 1)

            def modulated(n, first, m, L, gain, col):
                for v in range(2):
                    at = L * ADA + col + KT
                    nc.vector.scalar_tensor_tensor(gain_2[:, v, :], mod[:, v, at:at + KT], 1.0, vec[:, gain + L * KT:gain + (L + 1) * KT],
                                                   ALU.add, ALU.mult).then_inc(gain_ready, 1)
                dve.wait_ge(gain_ready, 2 * (m - FIRST_MOD) + 2)
                norm_2(n, first)
                parts = ((C, cx, 1, ps[:, 6, 0:CTX]), (X, x, 0, ps[:, 5, :]))[1 if first else 0:]

                def lower(k):
                    dve.wait_ge(hhi_ready, m * KT + (k + 1))
                    at = L * ADA + col + k
                    for part, stream, v, bank in parts:
                        last = nc.vector.scalar_tensor_tensor(c_lo[:, k, part], hf_2[:, k % 2, part], mod[:, v, at:at + 1],
                                                              c_hi[:, k, part].bitcast(F), ALU.add, ALU.subtract)
                    last.then_inc(hlo_ready, 1)

                for k in range(KT):
                    if k >= 2:
                        dve.wait_ge(hlo_ready, m * KT + (k - 1))
                    for part, stream, v, bank in parts:
                        last = nc.vector.scalar_tensor_tensor(hf_2[:, k % 2, part], stream[:, k, :], gain_2[:, v, k:k + 1], bank, ALU.mult, ALU.mult)
                    last.then_inc(hf_ready, 1)
                    if k >= 1:
                        lower(k - 1)
                lower(KT - 1)

            def tokens(g, j, n, dst):
                dve.wait_ge(ztok_ready, n + 1)
                nc.vector.tensor_copy(dst[0], ps[:, 4 + j, 0:CTX].rearrange("p (t d) -> p t d", t=CT))
                nc.vector.tensor_copy(dst[1], ps[:, j, :].rearrange("p (t d) -> p t d", t=TT)).then_inc(bank_read[j], 1)

            def gate_rows(L):
                f = slice(64, P)
                nc.vector.tensor_scalar(cum_f[f, :], gates[f, :], -1.0, None, ALU.mult).then_inc(gate_v, 1)
                dve.wait_ge(gate_v, L * 9 + 1)
                nc.vector.tensor_tensor(cum_f[f, :], cum_f[f, :], gates[f, :], ALU.min).then_inc(gate_v, 1)

            def gate_sums(L):
                fw, bw, both, f = slice(0, 32), slice(32, 64), slice(0, 64), slice(64, P)
                back_c = (bw, slice(CTX - 1, None, -1))

                def scans(dst, first_op, second_op, one, src, step):
                    n = CTX
                    nc.vector.tensor_tensor_scan(dst[fw, :], one(fw, ALL), src[fw, :], 0.0, first_op, second_op)
                    nc.vector.tensor_tensor_scan(dst[bw, C][:, ::-1], one(bw, n), src[bw, C][:, ::-1], 0.0, first_op, second_op).then_inc(gate_v, 1)
                    dve.wait_ge(gate_v, L * 9 + step)
                    nc.vector.tensor_tensor_scan(dst[bw, X][:, ::-1], one(bw, SEQ), src[bw, X][:, ::-1], dst[bw, 0:1], first_op, second_op).then_inc(gate_v, 1)
                    dve.wait_ge(gate_v, L * 9 + step + 1)

                dve.wait_ge(gate_a, L * 3 + 2)
                nc.vector.scalar_tensor_tensor(run_m[both, :], gates[f, :], 0.0, cum_f[f, :], ALU.min, ALU.subtract).then_inc(gate_v, 1)
                dve.wait_ge(gate_v, L * 9 + 3)
                scans(cum_f, ALU.mult, ALU.add, lambda rows, n: ones[rows, 0:1].broadcast_to([32, n]), run_m, 4)
                nc.vector.tensor_tensor(key_w[both, :], gates[both, :], cum_f[both, :], ALU.subtract).then_inc(gate_v, 1)
                dve.wait_ge(gate_v, L * 9 + 6)
                same = {ALL: lambda r: key_w[r, :], CTX: lambda r: key_w[r, C][:, ::-1], SEQ: lambda r: key_w[r, X][:, ::-1]}
                scans(run_m, ALU.max, ALU.max, lambda rows, n: same[n](rows), key_w, 7)
                nc.vector.tensor_tensor(key_w[f, :], cum_f[both, :], run_m[both, :], ALU.add).then_inc(gate_v, 1)

            def neighborhood(L, need_ctx):
                units, base = natt_units(need_ctx), L * N_UNITS
                per = len(units) // H2

                def normalised(u):
                    wide = CTX if units[u][1] else ALL
                    dve.wait_ge(nexp_done, base + (u + 1))
                    nc.vector.reciprocal(tiny[:, u % 2, 2:3], tiny[:, u % 2, 1:2]).then_inc(nrec_done, 1)
                    dve.wait_ge(nrec_done, base + (u + 1))
                    nc.vector.tensor_scalar(sn[:, u % 2, 0:wide], sn[:, u % 2, 0:wide], tiny[:, u % 2, 2:3], None, ALU.mult).then_inc(np_ready, 1)

                def lower(h):
                    rows = slice(h % 2 * HEAD, h % 2 * HEAD + HEAD)
                    dve.wait_ge(nhi_ready, L * H2 + (h + 1))
                    if need_ctx:
                        nc.vector.tensor_tensor(yn_lo[rows, h // 2, C], ps[rows, 7, 0:CTX], yn_hi[rows, h // 2, C].bitcast(F), ALU.subtract)
                    nc.vector.tensor_tensor(yn_lo[rows, h // 2, X], ps[rows, 6, :], yn_hi[rows, h // 2, X].bitcast(F), ALU.subtract).then_inc(nlo_ready, 1)

                for u, (h, c, t) in enumerate(units):
                    wide = CTX if c else ALL
                    if (c, t) == (0, 0):
                        table = bias[:, h % 2, :].rearrange("p (e k) -> p e k", k=GRID_W)
                        dve.wait_ge(bias_loaded[h % 2], (L * 4 + h // 2 + 1) * 16)
                        nc.vector.tensor_tensor(table, table, col_mask.rearrange("p (o k) -> p o k", o=1).broadcast_to([P, 2 * NA_ROWS - 2, GRID_W]),
                                                ALU.add).then_inc(bias_ready, 1)
                        dve.wait_ge(bias_ready, L * H2 + h + 1)
                    dve.wait_ge(ns_ready, base + (u + 1))
                    if u >= 2:
                        dve.wait_ge(npt_ready, base + (u - 1))
                    if not c:
                        at = (NA_ROWS - 2 - 2 * t) * GRID_W
                        nc.vector.scalar_tensor_tensor(sn[:, u % 2, X], ps[:, 2 * (u % 2), :], HEAD ** -0.5, bias[:, h % 2, at:at + SEQ],
                                                       ALU.mult, ALU.add).then_inc(nsx_done, 1)
                        dve.wait_ge(nsx_done, L * (H2 * TT) + h * TT + t + 1)
                    dve.wait_ge(nsc_done, base + (u + 1))
                    nc.vector.tensor_reduce(tiny[:, u % 2, 3:4], sn[:, u % 2, 0:wide], AX.X, ALU.max).then_inc(nmx_done, 1)
                    dve.wait_ge(nmx_done, base + (u + 1))
                    nc.vector.tensor_scalar(tiny[:, u % 2, 0:1], tiny[:, u % 2, 3:4], -1.0, None, ALU.mult).then_inc(nneg_ready, 1)
                    if u >= 1:
                        normalised(u - 1)
                    if u >= 2 and (u - 1) % per == 0:
                        lower((u - 2) // per)
                normalised(len(units) - 1)
                lower(H2 - 1)

            def mlstm(L, first):
                runs, where = gw_layout(first)
                dve.wait_ge(spilled, (L + 1) * 32)

                def diagonals(h):
                    dve.wait_ge(m_loaded[h % 2], (L * 4 + h // 2 + 1) * 16)
                    if h >= 2:
                        dve.wait_ge(mpv_ready, L * H2 + (h - 1))
                    for s in range(first, ST):
                        for d in range(2):
                            at = where[d, s, s]
                            last = nc.vector.scalar_tensor_tensor(gw[:, h % 2, at:at + P], m_row[:, h % 2, d, s * P:(s + 1) * P],
                                                                  key_t[:, s, 32 * d + h:32 * d + h + 1], causal[d], ALU.subtract, ALU.max)
                    last.then_inc(mdiag_ready, 1)

                def scored(h):
                    for s in range(ST):
                        n = h * ST + s
                        dve.wait_ge(mw_ready, L * N_UNITS + (n + 1))
                        dve.wait_ge(ms_ready, L * N_UNITS + (n + 1))
                        b = 2 * (n % 2)
                        score = ps[:, b:b + 2, :].rearrange("p b t -> p (b t)")
                        for d, t0, t1, at in runs[s]:
                            w = gw[:, h % 2, at:at + (t1 - t0) * P]
                            last = nc.vector.scalar_tensor_tensor(w, score[:, t0 * P:t1 * P], HEAD ** -0.5, w, ALU.mult, ALU.mult)
                        last.then_inc(mg_ready, 1)

                def result(h):
                    b, n = 4 + 2 * (h % 2), (L * H2 + h) * 6
                    both = ps[:, b:b + 2, 0:ST * (HEAD + 1)].rearrange("p d (t c) -> p d t c", c=HEAD + 1)[:, :, first:ST, :]
                    total = both[:, :, :, HEAD]
                    least = key_t[:, first:ST, 64:P].rearrange("p t (d c) -> p d t c", c=32)[:, :, :, h]
                    den, inv = [cols[:, i, 0:2 * ST].rearrange("p (d t) -> p d t", d=2)[:, :, first:ST] for i in range(2)]

                    def over(d):
                        return inv[:, d, :].rearrange("p (t o) -> p t o", o=1).broadcast_to([P, ST - first, HEAD])

                    dve.wait_ge(mpv_ready, L * H2 + (h + 1))
                    nc.vector.tensor_scalar(den, total, -1.0, None, ALU.mult).then_inc(post_v, 1)
                    dve.wait_ge(post_v, n + 1)
                    nc.vector.tensor_tensor(den, den, total, ALU.max).then_inc(post_v, 1)
                    dve.wait_ge(post_v, n + 2)
                    nc.vector.tensor_tensor(den, den, least, ALU.max).then_inc(post_v, 1)
                    dve.wait_ge(post_v, n + 3)
                    nc.vector.reciprocal(inv, den).then_inc(post_v, 1)
                    dve.wait_ge(post_v, n + 4)
                    nc.vector.tensor_tensor(hs[:, first:ST, h, :], both[:, 0, :, 0:HEAD], over(0), ALU.mult).then_inc(post_v, 1)
                    nc.vector.tensor_tensor(hb[:, first:ST, :], both[:, 1, :, 0:HEAD], over(1), ALU.mult).then_inc(head_done, 1)
                    dve.wait_ge(post_v, n + 5)
                    dve.wait_ge(head_done, L * H2 + (h + 1))
                    nc.vector.tensor_tensor(hs[:, first:ST, h, :], hs[:, first:ST, h, :], hb[:, first:ST, :], ALU.add).then_inc(post_v, 1)

                dve.wait_ge(key_copied, L + 1)
                diagonals(0)
                diagonals(1)
                scored(0)
                for h in range(H2):
                    if h + 1 < H2:
                        scored(h + 1)
                    result(h)
                    if h + 2 < H2:
                        diagonals(h + 2)
                dve.wait_ge(post_v, (L + 1) * H2 * 6)
                heads = hs[:, first:ST, :, :].rearrange("p t h d -> p (t h) d")
                c = slice(first * H2, ST * H2)

                def spread(i):
                    return cols[:, i, c].rearrange("p (t o) -> p t o", o=1).broadcast_to([P, (ST - first) * H2, HEAD])

                nc.vector.tensor_reduce(cols[:, 0, c], heads, AX.X, ALU.add).then_inc(ln_v, 1)
                dve.wait_ge(ln_v, L * 6 + 1)
                nc.vector.tensor_scalar(cols[:, 0, c], cols[:, 0, c], -1.0 / HEAD, None, ALU.mult).then_inc(ln_v, 1)
                dve.wait_ge(ln_v, L * 6 + 2)
                nc.vector.tensor_tensor(heads, heads, spread(0), ALU.add).then_inc(ln_v, 1)
                dve.wait_ge(ln_a, L * 2 + 1)
                nc.vector.tensor_reduce(cols[:, 1, c], hq[:, first:ST, :, :].rearrange("p t h d -> p (t h) d"), AX.X, ALU.add).then_inc(ln_v, 1)
                dve.wait_ge(ln_a, L * 2 + 2)
                nc.vector.reciprocal(cols[:, 3, c], cols[:, 2, c]).then_inc(ln_v, 1)
                dve.wait_ge(ln_v, L * 6 + 5)
                nc.vector.tensor_tensor(heads, heads, spread(3), ALU.mult).then_inc(ln_v, 1)
                dve.wait_ge(om_half, (L + 1) * 4)
                lo = first * P

                def lower(f):
                    dve.wait_ge(yhi_ready, L * 4 + (f + 1))
                    nc.vector.tensor_tensor(ym_lo[:, f, lo:ALL], yu[:, f, lo:ALL], ym_hi[:, f, lo:ALL].bitcast(F), ALU.subtract).then_inc(ylo_ready, 1)

                for f in range(4):
                    g = vec[:, V_MN + L * 4 + f:V_MN + L * 4 + f + 1]
                    dve.wait_ge(yt_ready, L * 4 + (f + 1))
                    if first == 0:
                        nc.vector.scalar_tensor_tensor(yu[:, f, C], ps[:, 2 * f + 1, 0:CTX], g, om[:, f, C], ALU.mult, ALU.mult)
                    nc.vector.scalar_tensor_tensor(yu[:, f, X], ps[:, 2 * f, :], g, om[:, f, X], ALU.mult, ALU.mult).then_inc(yu_ready, 1)
                    if f >= 1:
                        lower(f - 1)
                lower(3)

            def add_to_stream(g, j, k, at, need_ctx):
                dve.wait_ge(chunk_used, g * RING + (j + 1))
                if need_ctx:
                    one = cx[:, ds(k, 1), :].rearrange("p o t -> p (o t)")
                    nc.vector.scalar_tensor_tensor(one, ps[:, 4 + j, 0:CTX], mod[:, 1, ds(k + at, 1)], one, ALU.mult, ALU.add)
                one = x[:, ds(k, 1), :].rearrange("p o t -> p (o t)")
                nc.vector.scalar_tensor_tensor(one, ps[:, j, :], mod[:, 0, ds(k + at, 1)], one, ALU.mult, ALU.add).then_inc(bank_read[j], 1)

            dve.wait_ge(ada_used, DEPTH * (ADA // 3) + 1)
            for v in range(2):
                nc.vector.tensor_tensor(mod[:, v, :], mod[:, v, :], vec[:, V_BADA:V_BADA + DEPTH * ADA], ALU.add).then_inc(mod_ready, 1)
            dve.wait_ge(mod_ready, 2)
            plain(FIRST_MOD, V_GF)
            dve.wait_ge(xf_done, KT)
            dve.wait_ge(c2_loaded, 16)
            dve.wait_ge(cx_loaded, 16)
            for L in range(DEPTH):
                need_ctx = L + 1 < DEPTH
                first = 0 if need_ctx else CT
                g0 = START_2 + L * G2
                modulated(FIRST_MOD + 1 + 2 * L, 0, FIRST_MOD + 2 * L, L, V_N1, 0)
                for j in range(RING):
                    tokens(g0 + G_VN, j, L * 8 + j, [vn[:, s, j * P:(j + 1) * P] for s in (slice(0, CT), slice(CT, ST))])
                dve.wait_ge(chunk_used, (g0 + G_GATE) * RING + 1)
                b = vec[:, V_BG + L:V_BG + L + 1]
                nc.vector.tensor_scalar(gates[:, C], ps[:, 4, 0:CTX], b, None, ALU.add)
                nc.vector.tensor_scalar(gates[:, X], ps[:, 0, :], b, None, ALU.add).then_inc(bank_read[0], 1)
                dve.wait_ge(bank_read[0], g0 + G_GATE + 3)
                gate_rows(L)
                neighborhood(L, need_ctx)
                gate_sums(L)
                for t, dst in enumerate((qm, km)):
                    for j in range(RING):
                        n, g = t * RING + j, g0 + t + G_QM
                        dve.wait_ge(z_ready, L * 16 + (5 + n))
                        if L or n:
                            dve.wait_ge(rope_2, L * 8 + n)
                        nc.vector.tensor_tensor(rope_a[:, :], zm[:, j % 2, X], rope_cos, ALU.mult).then_inc(rope_part, 1)
                        dve.wait_ge(zrot_ready, L * 8 + (n + 1))
                        nc.vector.tensor_tensor(rope_b[:, :], ps[:, j, :], rope_sin, ALU.mult).then_inc(bank_read[j], 1)
                        dve.wait_ge(rope_part, L * 8 + (n + 1))
                        dve.wait_ge(bank_read[j], g + 3)
                        nc.vector.tensor_tensor(dst[:, j, X], rope_a[:, :], rope_b[:, :], ALU.add).then_inc(rope_2, 1)
                nc.vector.memset(vm[:, :, :, HEAD:HEAD + 1], 1.0)
                for j in range(RING):
                    tokens(g0 + G_VM, j, L * 8 + 4 + j,
                           [vm[:, s, 2 * j:2 * j + 2, 0:HEAD].rearrange("p t h d -> p t h d") for s in (slice(0, CT), slice(CT, ST))])
                for j in range(RING):
                    dve.wait_ge(bank_read[j], g0 + G_OM + 3)
                    nc.vector.tensor_scalar(om[:, j, :], om[:, j, :], 0.5, 0.5, ALU.mult, ALU.add).then_inc(om_half, 1)
                mlstm(L, first)
                dve.wait_ge(reloaded, (L + 1) * 32)
                with dve.Fori(0, 2) as i:
                    for j in range(RING):
                        add_to_stream(g0 + i + G_OUT2, j, i * 4 + j, L * ADA + 2 * KT, need_ctx)
                modulated(FIRST_MOD + 2 + 2 * L, first, FIRST_MOD + 2 * L + 1, L, V_N2, 3 * KT)
                lo = first * P
                with dve.Fori(0, QUARTERS) as q:
                    with dve.Fori(0, 2) as i:
                        g = g0 + q * 4 + i + G_UP

                        def hidden_lower_2(j):
                            done = q * KT + i * 4 + ((DEPTH + L) * N_MLP + j + 1)
                            dve.wait_ge(uhi_ready, done)
                            one = (slice(None), ds(i * 4 + j, 1), slice(lo, ALL))
                            nc.vector.tensor_tensor(u2_lo[one].rearrange("p o t -> p (o t)"), hf_2[:, j % 2, lo:ALL],
                                                    u2_hi[one].rearrange("p o t -> p (o t)").bitcast(F), ALU.subtract).then_inc(ulo_ready, 1)

                        for j in range(RING):
                            dve.wait_ge(bank_read[j], g + 3)
                            if j >= 2:
                                dve.wait_ge(ulo_ready, q * KT + i * 4 + ((DEPTH + L) * N_MLP + j - 1))
                            nc.vector.tensor_tensor(hf_2[:, j % 2, lo:ALL], sq_2[:, j % 2, lo:ALL], sq_2[:, j % 2, lo:ALL], ALU.mult).then_inc(v2_ready, 1)
                            if j >= 1:
                                hidden_lower_2(j - 1)
                        hidden_lower_2(RING - 1)
                        dve.wait_ge(ulo_ready, q * KT + i * 4 + ((DEPTH + L) * N_MLP + RING))
                    with dve.Fori(0, 2) as i:
                        for j in range(RING):
                            add_to_stream(g0 + q * 4 + i + (G_UP + 2), j, i * 4 + j, L * ADA + 5 * KT, need_ctx)
            plain(FIRST_MOD + 1 + 2 * DEPTH, V_FIN)


def constants_2():
    import numpy as np
    f = np.float32
    p = np.arange(P)
    pos = np.arange(SEQ)
    inv = f(10000.0) ** (-np.arange(16, dtype=f) / f(16))
    d = p % 32
    ang = np.where((d < 16)[:, None], (pos // GRID_W).astype(f)[None, :], (pos % GRID_W).astype(f)[None, :]) * inv[d % 16][:, None]
    cos, sin = np.cos(ang), np.sin(ang) * np.where(p % HEAD < 32, -1, 1)[:, None]
    key, query = p[:, None], p[None, :]
    col = p % GRID_W
    start = np.clip(col - NA_COLS // 2, 0, GRID_W - NA_COLS)[:, None]
    c = np.arange(GRID_W)[None, :]
    window = np.where((c >= start) & (c < start + NA_COLS), 0.0, MASKED)
    causal = [np.where(seen, 0.0, -MASKED) for seen in (key <= query, key >= query)]
    return np.concatenate([cos, sin, *causal, window], axis=1).astype(f)


def bias_tiles(rpb):
    import numpy as np
    p, e, k = np.arange(P)[:, None, None], np.arange(1, 2 * NA_ROWS - 1)[None, :, None], np.arange(GRID_W)[None, None, :]
    dc = np.clip(k - p % GRID_W + NA_COLS - 1, 0, 2 * NA_COLS - 2)
    return np.ascontiguousarray(rpb[:, :, e - p // GRID_W, dc].reshape(*rpb.shape[:2], P, -1))


def gate_columns(b):
    import numpy as np
    out = np.zeros((P, b.shape[0]), np.float32)
    for g in range(4):
        out[32 * g:32 * g + H2] = b[:, g * H2:(g + 1) * H2].T
    return out


def kernel(x, g_mix, w_in, sinks, w_a, w_b, w_out, g_mlp, w_up, w_down, g_final, c_2, ctx_2, c_ctx_2,
           w_ada_2, b_ada_2, norm1_g_2, w_in_2, b_gate_2, mlstm_norm_g_2, rpb_2, w_out_2, norm2_g_2,
           w_mlp1_2, w_mlp2_2, final_g_2):
    import concourse.bacc as bacc
    import numpy as np
    from concourse import mybir
    from concourse.bass_utils import run_bass_kernel_spmd

    def host(a):
        return np.asarray(a)

    def by_feature(a):
        return np.ascontiguousarray(a.T.reshape(KT, P, -1).transpose(1, 0, 2))

    weights = weight_stream({n: host(a) for n, a in dict(
        w_in=w_in, w_a=w_a, w_b=w_b, w_out=w_out, w_up=w_up, w_down=w_down, w_in_2=w_in_2,
        w_out_2=w_out_2, w_mlp1_2=w_mlp1_2, w_mlp2_2=w_mlp2_2).items()})
    vectors = np.concatenate([*[columns(host(v)) for v in (g_mix, g_mlp, norm1_g_2, norm2_g_2, g_final, final_g_2,
                                                           b_ada_2, mlstm_norm_g_2)],
                              gate_columns(host(b_gate_2)),
                              np.broadcast_to(host(sinks).reshape(1, -1), (P, DEPTH * ATT_HEADS))], axis=1)
    arrays = {
        "x": by_feature(host(x)[0]), "ctx": by_feature(host(ctx_2)[0]), "w": weights, "vec": vectors,
        "c0": constants_0(), "c1": constants_1(), "c2": constants_2(), "rpb": bias_tiles(host(rpb_2)),
        "ada": np.ascontiguousarray(host(w_ada_2).transpose(0, 2, 1).reshape(DEPTH * ADA, P, D_MODEL)),
        "c": np.stack([host(c_2)[0], host(c_ctx_2)])[None],
    }
    nc = bacc.Bacc("TRN2", target_bir_lowering=False, num_devices=1)
    dram = {n: nc.dram_tensor(f"in_{n}", list(a.shape), mybir.dt.float32, kind="ExternalInput").ap() for n, a in arrays.items()}
    out = nc.dram_tensor("out", [P, KT, SEQ], mybir.dt.float32, kind="ExternalOutput").ap()
    hybrid_then_dit(nc, dram, out)
    results = run_bass_kernel_spmd(nc, [{f"in_{n}": a for n, a in arrays.items()}], core_ids=[0])
    got = results.results[0]["out"]
    return np.ascontiguousarray(got.transpose(1, 0, 2).reshape(D_MODEL, SEQ).T).reshape(1, SEQ, D_MODEL)
```

```python
P = 128
D_MODEL, SEQ, DEPTH = 1024, 512, 2
KT = D_MODEL // P
HALF_KT = KT // 2
TT = SEQ // P
D_FF = 4 * D_MODEL
QUARTERS = D_FF // D_MODEL
EPS = 1e-6
HEAD = 64
WINDOW = 128
ATT_HEADS, ATT_GROUPS = 8, 2
ATT_Q, ATT_KV = 512, 128
RET_HEADS, RET_QK, RET_V = 4, 128, 256
CTX = 256
ALL = CTX + SEQ
ST = ALL // P
CT = CTX // P
GRID_W, GRID_ROWS, NA_COLS, NA_ROWS = 64, 8, 16, 8
H2 = 8
NMOD = 6
RING, RAW = 4, 2
MASKED = -1e30

IN_1 = 48
WA_1 = 4
LAYER_1 = IN_1 + WA_1 + 2 * KT + QUARTERS * 2 * KT
LAYER_2 = 32 + KT + QUARTERS * 2 * KT
CHUNKS = DEPTH * (LAYER_1 + LAYER_2) + RING
ADA = NMOD * KT
V_GMIX, V_GMLP, V_N1, V_N2, V_GF, V_FIN, V_BADA, V_MN, V_BG, V_SINK, N_VEC = \
    0, 16, 32, 48, 64, 72, 80, 176, 184, 186, 202


def weight_stream(inp):
    import numpy as np

    def block(w, rows, cols):
        return w[np.asarray(rows)][:, np.asarray(cols)].reshape(-1, P, len(cols)).transpose(1, 0, 2)

    chunks = []
    every = np.arange(D_MODEL)

    def put(*blocks):
        chunks.append(np.concatenate([b.reshape(P, -1) for b in blocks], axis=1))

    def pad(n=1):
        for _ in range(n):
            chunks.append(np.zeros((P, KT * P), np.float32))

    def tile(w, start, width=P):
        put(block(w, every, np.arange(start, start + width)))

    def mlp(up, down):
        for q in range(QUARTERS):
            for m in range(KT):
                tile(up, q * D_MODEL + m * P)
            for m in range(KT):
                put(block(down, q * D_MODEL + every, np.arange(m * P, (m + 1) * P)))

    pair = [np.concatenate([np.arange(h * HEAD, (h + 1) * HEAD) for h in (t, t + 4)]) for t in range(4)]
    at = np.cumsum([0, ATT_Q, ATT_KV, ATT_KV, RET_HEADS * RET_QK, RET_HEADS * RET_QK,
                    RET_HEADS * RET_V, RET_HEADS * RET_V, D_MODEL])
    for l in range(DEPTH):
        w = inp["w_in"][l]
        for t in range(4):
            put(block(w, every, pair[t]))
        tile(w, at[1])
        tile(w, at[2])
        pad(2)
        for t in range(8):
            tile(w, at[3] + t * P)
        for t in range(8):
            tile(w, at[5] + t * P)
        for t in range(8):
            tile(w, at[6] + t * P)
        rows = np.concatenate(pair)
        for t in range(0, 8, 2):
            put(*[block(inp["w_a"][l], rows, np.arange(m * P, (m + 1) * P)) for m in (t, t + 1)])
        for m in range(8):
            tile(w, at[7] + m * P)
            tile(w, at[8] + m * P)
            tile(inp["w_b"][l], m * P)
        for m in range(8):
            tile(inp["w_out"][l], m * P)
        mlp(inp["w_up"][l], inp["w_down"][l])
    for l in range(DEPTH):
        w = inp["w_in_2"][l]
        for t in range(12):
            tile(w, 2048 + t * P)
        gates = np.zeros((D_MODEL, P), np.float32)
        for g, start in enumerate((0, 32, 64, 96)):
            gates[:, start:start + H2] = w[:, 3584 + g * H2:3584 + (g + 1) * H2]
        tile(gates, 0)
        pad(3)
        for t in range(16):
            tile(w, t * P)
        for m in range(8):
            tile(inp["w_out_2"][l], m * P)
        mlp(inp["w_mlp1_2"][l], inp["w_mlp2_2"][l])
    pad(RING)
    out = np.stack(chunks)
    assert out.shape[0] == CHUNKS
    return out


def columns(v):
    import numpy as np
    return np.ascontiguousarray(np.asarray(v).reshape(-1, P).T)


def constants_1():
    import numpy as np
    f = np.float32
    p = np.arange(P)
    pos = np.arange(SEQ, dtype=f)
    d = p % HEAD
    inv = f(10000.0) ** (-np.arange(32, dtype=f) / f(32))
    ang = pos[None, :] * inv[d % 32][:, None]
    att_cos, att_sin = np.cos(ang), np.sin(ang) * np.where(d < 32, -1, 1)[:, None]
    theta = f(1.0) / (f(10000.0) ** np.linspace(0.0, 1.0, 64, dtype=f))
    ang = pos[None, :] * theta[p // 2][:, None]
    ret_cos, ret_sin = np.cos(ang), np.sin(ang) * np.where(p % 2 == 0, -1, 1)[:, None]
    rel = p[:, None] + WINDOW - np.arange(2 * WINDOW)[None, :]
    mask = np.where((rel >= 0) & (rel < WINDOW), 0.0, MASKED)
    decay = []
    for h in range(RET_HEADS):
        log_g = np.log(f(1.0) - f(2.0) ** f(-5.0 - h))
        r = (np.arange(SEQ)[None, :] - p[:, None]).astype(f)
        decay.append(np.where(r >= 0, np.exp(log_g * np.maximum(r, 0)), 0) * f(RET_QK ** -0.5))
    swap_ret = np.eye(P)[p ^ 1]
    return np.concatenate([mask, mask, att_cos, att_sin, ret_cos, ret_sin, swap_ret, *decay], axis=1).astype(f)


def constants_0():
    import numpy as np
    p = np.arange(P)
    return np.concatenate([np.eye(P), np.ones((P, P)), np.eye(P)[p ^ 32]], axis=1).astype(np.float32)


def hybrid_then_dit(nc, dram, out):
    import concourse.bass as bass
    from concourse import mybir
    from contextlib import ExitStack

    F, R = mybir.dt.float32, mybir.dt.float32r
    ALU, ACT, AX = mybir.AluOpType, mybir.ActivationFunctionType, mybir.AxisListType
    ds = bass.ds

    KB = 1024
    BASE = 16512

    def sb(name, at, shape, dt=F):
        return nc.alloc_sbuf_tensor_at(name, [P, *shape], dt, offset=BASE + int(at))

    x = sb("x", 0, [KT, SEQ])
    w_raw = sb("w_raw", 24 * KB, [RAW, KT * P])
    w_hi = sb("w_hi", 32 * KB, [RING, KT * P], R)
    w_lo = sb("w_lo", 48 * KB, [RING, KT * P], R)
    h_hi = sb("h_hi", 64 * KB, [KT, SEQ], R)
    h_lo = sb("h_lo", 88 * KB, [KT, SEQ], R)
    CONST = 112 * KB
    c0 = sb("c0", CONST, [3 * P])
    ident, ones, swap_half = c0[:, 0:P], c0[:, P:2 * P], c0[:, 2 * P:3 * P]
    C1 = 4 * WINDOW + 4 * SEQ + P + RET_HEADS * SEQ
    c1 = sb("c1", CONST + 1536, [C1])
    att_mask = c1[:, 0:512].rearrange("p (h k) -> p h k", h=2)
    att_cos, att_sin = c1[:, 512:1024], c1[:, 1024:1536]
    ret_cos, ret_sin = c1[:, 1536:2048], c1[:, 2048:2560]
    swap_pair = c1[:, 2560:2688]
    decay = c1[:, 2688:C1].rearrange("p (h i) -> p h i", h=RET_HEADS)
    VECS = 132 * KB
    assert CONST + 1536 + 4 * C1 <= VECS
    vec = sb("vec", VECS, [N_VEC])
    SMALL = VECS + 4 * N_VEC + 24
    gain_now = sb("gain_now", SMALL, [KT])
    sink_now = sb("sink_now", SMALL + 32, [2, ATT_HEADS])
    eps = sb("eps", SMALL + 96, [1])
    rms = sb("rms", SMALL + 128, [2, 16])
    mod = sb("mod", SMALL + 256, [2, DEPTH * ADA])
    mod_3 = sb("mod_3", SMALL + 1056, [2, 3])
    tiny = sb("tiny", SMALL + 1088, [2, 16])
    DYN = 135 * KB
    assert SMALL + 1088 + 128 <= DYN
    stage = sb("stage", 80 * KB, [2, SEQ])
    stage_2 = sb("stage_2", 84 * KB, [2, SEQ])
    tmp = sb("tmp", 104 * KB, [2, SEQ])
    tmp_2 = sb("tmp_2", 108 * KB, [2, SEQ])
    tmp_3 = sb("tmp_3", 16 * KB, [2, SEQ])
    diag = sb("diag", 22 * KB, [TT, P])
    squares = [t[:, k, :] for t in (stage, stage_2, tmp_2, tmp_3) for k in range(2)]
    rqk = sb("rqk", DYN, [2 * RET_HEADS, SEQ])
    rv = sb("rv", DYN + 16 * KB, [TT, RET_HEADS * RET_V])
    r_hi = sb("r_hi", DYN, [KT, SEQ], R)
    r_lo = sb("r_lo", DYN + 16 * KB, [KT, SEQ], R)
    U = DYN + 32 * KB
    aq = sb("aq", U, [4, SEQ])
    ak = sb("ak", U + 8 * KB, [SEQ])
    av = sb("av", U + 10 * KB, [TT, ATT_KV])
    pt_sb = sb("pt_sb", U + 12 * KB, [2, 2, 2, P])
    s_sb = sb("s_sb", 16 * KB, [2, 2, 2 * WINDOW])
    p_sb = sb("p_sb", U + 32 * KB, [2, 2, 2 * WINDOW])
    o_hi = sb("o_hi", U + 16 * KB, [4, SEQ], R)
    o_lo = sb("o_lo", U + 24 * KB, [4, SEQ], R)
    r_raw = sb("r_raw", U, [KT, SEQ])
    a_sb = [sb("a_sb0", U + 32 * KB, [1280]), sb("a_sb1", 16 * KB, [1280])]
    y_a = sb("y_a", U, [KT, SEQ])
    mix_hi = sb("mix_hi", U + 16 * KB, [KT, SEQ], R)
    mix_lo = sb("mix_lo", U, [KT, SEQ], R)
    u_hi = sb("u_hi", DYN, [KT, SEQ], R)
    u_lo = sb("u_lo", DYN + 16 * KB, [KT, SEQ], R)
    ada_w = sb("ada_w", U, [3, D_MODEL])
    ada_junk = sb("ada_junk", U + 12 * KB, [D_MODEL])
    c_silu = sb("c_silu", U + 16 * KB, [2, D_MODEL])
    c_raw = sb("c_raw", U + 24 * KB, [2, D_MODEL])

    cx = sb("cx", 16 * KB, [KT, CTX])
    c_hi = sb("c_hi", 64 * KB, [KT, ALL], R)
    c_lo = sb("c_lo", 88 * KB, [KT, ALL], R)
    C2 = 2 * SEQ + 2 * P + GRID_W
    c2 = sb("c2", CONST + 1536, [C2])
    rope_cos, rope_sin = c2[:, 0:SEQ], c2[:, SEQ:2 * SEQ]
    causal = [c2[:, 2 * SEQ:2 * SEQ + P], c2[:, 2 * SEQ + P:2 * SEQ + 2 * P]]
    col_mask = c2[:, 2 * SEQ + 2 * P:C2]
    GATE = CONST + 1536 + 4 * C2
    gates = sb("gates", GATE, [ALL])
    cum_f = sb("cum_f", GATE + 3 * KB, [ALL])
    run_m = sb("run_m", GATE + 6 * KB, [ALL])
    key_w = sb("key_w", GATE + 9 * KB, [ALL])
    key_t = sb("key_t", GATE, [ST, P])
    cols = sb("cols", GATE + 12 * KB, [4, ST * H2])
    assert GATE + 12 * KB + 16 * ST * H2 <= VECS
    gain_2 = sb("gain_2", SMALL + 1088 + 128, [2, KT])
    assert SMALL + 1088 + 128 + 64 <= DYN
    sq_2 = sb("sq_2", DYN + 48 * KB, [2, ALL])
    hf_2 = sb("hf_2", DYN + 54 * KB, [2, ALL])
    diag_2 = sb("diag_2", DYN + 60 * KB, [ST, P])
    squares_2 = [sq_2[:, k, :] for k in range(2)] + [sb(f"squares{k}", at, [ALL])[:, :] for k, at in enumerate(
        [GATE + 3 * KB * i for i in range(4)] + [DYN + 63 * KB, DYN + 66 * KB])]
    qn = sb("qn", DYN, [4, ALL])
    kn = sb("kn", DYN + 12 * KB, [4, ALL])
    yn_hi = sb("yn_hi", DYN, [4, ALL], R)
    yn_lo = sb("yn_lo", DYN + 12 * KB, [4, ALL], R)
    vn = sb("vn", DYN + 24 * KB, [ST, H2 * HEAD])
    vm = sb("vm", DYN + 36 * KB, [ST, H2, HEAD + 1])
    OM = DYN + 36 * KB + 4 * ST * H2 * (HEAD + 1)
    AFTER = OM + 12 * KB
    bias = sb("bias", OM + 10 * KB, [2, (2 * NA_ROWS - 2) * GRID_W])
    sn = sb("sn", GATE + 3 * KB, [3, ALL])
    pn = sb("pn", OM + 17 * KB, [2, ALL])
    zm = sb("zm", OM, [2, ALL])
    rope_a = sb("rope_a", OM + 6 * KB, [SEQ])
    rope_b = sb("rope_b", OM + 8 * KB, [SEQ])
    qm = sb("qm", 0, [4, ALL])
    km = sb("km", 12 * KB, [4, ALL])
    om = sb("om", OM, [4, ALL])
    hs = sb("hs", DYN + 24 * KB, [ST, H2, HEAD])
    m_row = sb("m_row", AFTER, [2, 2, ALL])
    hq = sb("hq", AFTER, [ST, H2, HEAD])
    assert AFTER + 12 * KB <= 207 * KB + 512
    PAIRS = 42
    gw = sb("gw", 64 * KB, [2, PAIRS * P])
    num = sb("num", GATE + 3 * KB, [2, ALL])
    hb = sb("hb", 106 * KB, [ST, HEAD])
    yu = sb("yu", 64 * KB, [4, ALL])
    ym_hi = sb("ym_hi", 76 * KB, [4, ALL], R)
    ym_lo = sb("ym_lo", 88 * KB, [4, ALL], R)
    u2_hi = sb("u2_hi", DYN, [KT, ALL], R)
    u2_lo = sb("u2_lo", DYN + 24 * KB, [KT, ALL], R)
    x_spill = nc.dram_tensor("x_spill", [P, KT, SEQ], F, kind="Internal").ap()
    cx_spill = nc.dram_tensor("cx_spill", [P, KT, CTX], F, kind="Internal").ap()
    m_spill = nc.dram_tensor("m_spill", [2, H2, ALL], F, kind="Internal").ap()

    RET_COL = [0, 512, 896, 1152, 1280]

    ctx = ExitStack()
    with ctx:
        ps = ctx.enter_context(nc.psum_tensor("ps", [P, 8, SEQ], F))

        def sem(name):
            return ctx.enter_context(nc.semaphore(name))

        x_loaded, vec_loaded, c0_loaded, c1_loaded = sem("x_loaded"), sem("vec_loaded"), sem("c0_loaded"), sem("c1_loaded")
        raw_ready = [sem(f"raw_ready{j}") for j in range(RAW)]
        c_loaded = sem("c_loaded")
        ada_ready = [sem(f"ada_ready{j}") for j in range(3)]
        stored = sem("stored")
        hi_ready, lo_ready, chunk_used = sem("hi_ready"), sem("lo_ready"), sem("chunk_used")
        bank_read = [sem(f"bank_read{j}") for j in range(RING)]
        sq_ready, sq_added, sq_used, std_ready = sem("sq_ready"), sem("sq_added"), sem("sq_used"), sem("std_ready")
        rinv_ready, diag_ready, rb_ready = sem("rinv_ready"), sem("diag_ready"), sem("rb_ready")
        hf_ready, hhi_ready, hlo_ready = sem("hf_ready"), sem("hhi_ready"), sem("hlo_ready")
        eps_set = sem("eps_set")
        rot_ready, rope_half_done, rope_done = sem("rot_ready"), sem("rope_half_done"), sem("rope_done")
        vt_ready, v_done = sem("vt_ready"), sem("v_done")
        rz_ready, rturn_ready, rcos_done, rrope_done = sem("rz_ready"), sem("rturn_ready"), sem("rcos_done"), sem("rrope_done")
        layer_vec = sem("layer_vec")
        sc_ready, s_done, mx_done, nm_ready = sem("sc_ready"), sem("s_done"), sem("mx_done"), sem("nm_ready")
        exp_done, den_done, p_ready, pt_ready = sem("exp_done"), sem("den_done"), sem("p_ready"), sem("pt_ready")
        pt_copied, pv_ready, ohi_ready, olo_ready = sem("pt_copied"), sem("pv_ready"), sem("ohi_ready"), sem("olo_ready")
        rs_ready, a_ready, inner_ready, rcopy_done = sem("rs_ready"), sem("a_ready"), sem("inner_ready"), sem("rcopy_done")
        rsq_used, rstd_ready, rrinv_ready = sem("rsq_used"), sem("rstd_ready"), sem("rrinv_ready")
        rdiag_ready, rrb_ready = sem("rdiag_ready"), sem("rrb_ready")
        tanh_ready, sl_ready, rr_ready, rhi_ready, rlo_ready = sem("tanh_ready"), sem("sl_ready"), sem("rr_ready"), sem("rhi_ready"), sem("rlo_ready")
        ya_ready, ta_ready, t12_ready, mx_ready, mhi_ready, mlo_ready = \
            sem("ya_ready"), sem("ta_ready"), sem("t12_ready"), sem("mx_ready"), sem("mhi_ready"), sem("mlo_ready")
        relu_ready, v2_ready, uhi_ready, ulo_ready = sem("relu_ready"), sem("v2_ready"), sem("uhi_ready"), sem("ulo_ready")
        ct_ready, cs_ready, ada_sum, ada_used = sem("ct_ready"), sem("cs_ready"), sem("ada_sum"), sem("ada_used")

        N_ROPE, N_ATT, N_MLP = 4 + 1, 16, QUARTERS * KT
        G1 = LAYER_1 // RING
        G_KV, G_RET, G_RV, G_RG, G_WA, G_MIX, G_OUT, G_MLP = 1, 2, 4, 6, 8, 9, 15, 17
        units = [(n, g, i) for n in range(TT) for g in range(ATT_GROUPS) for i in range(2)]

        cx_loaded, c2_loaded, xf_done, spilled, reloaded = sem("cx_loaded"), sem("c2_loaded"), sem("xf_done"), sem("spilled"), sem("reloaded")
        mod_ready, gain_ready = sem("mod_ready"), sem("gain_ready")
        z_ready, zrot_ready, ztok_ready, rope_part, rope_2 = sem("z_ready"), sem("zrot_ready"), sem("ztok_ready"), sem("rope_part"), sem("rope_2")
        om_half = sem("om_half")
        bias_loaded = [sem(f"bias_loaded{j}") for j in range(2)]
        bias_ready = sem("bias_ready")
        ns_ready, nsx_done, nsc_done, nmx_done, nneg_ready = sem("ns_ready"), sem("nsx_done"), sem("nsc_done"), sem("nmx_done"), sem("nneg_ready")
        nexp_done, nrec_done, np_ready, npt_ready = sem("nexp_done"), sem("nrec_done"), sem("np_ready"), sem("npt_ready")
        npt_copied, npv_ready, nhi_ready, nlo_ready = sem("npt_copied"), sem("npv_ready"), sem("nhi_ready"), sem("nlo_ready")
        gate_v, gate_a, m_stored, key_ready, key_copied = sem("gate_v"), sem("gate_a"), sem("m_stored"), sem("key_ready"), sem("key_copied")
        m_loaded = [sem(f"m_loaded{j}") for j in range(2)]
        ms_ready, mw_ready, mdiag_ready, mg_ready, mpv_ready = sem("ms_ready"), sem("mw_ready"), sem("mdiag_ready"), sem("mg_ready"), sem("mpv_ready")
        num_ready, num_token = sem("num_ready"), sem("num_token")
        post_v, head_done, ln_v, ln_a, yt_ready, yu_ready = sem("post_v"), sem("head_done"), sem("ln_v"), sem("ln_a"), sem("yt_ready"), sem("yu_ready")
        yhi_ready, ylo_ready = sem("yhi_ready"), sem("ylo_ready")

        G2 = LAYER_2 // RING
        G_VN, G_GATE, G_QM, G_VM, G_OM, G_OUT2, G_UP = 2, 3, 4, 6, 7, 8, 10
        START_2 = DEPTH * G1
        X, C = slice(CTX, ALL), slice(0, CTX)
        FIRST_MOD = 2 * DEPTH
        N_UNITS = H2 * ST

        def natt_units(need_ctx):
            return [(h, c, t) for c, n in ((0, TT), (1, CT if need_ctx else 0)) for h in range(H2) for t in range(n)]

        M_TILES = 12

        def place(u, need_ctx):
            return u if need_ctx else 3 * (u // 2) + u % 2

        def tiles_after(u, units, need_ctx, late):
            last = [max(v for v in range(len(units)) if place(v, need_ctx) <= 4 * c + 3 + late) for c in range(M_TILES - 1)]
            return [c for c, v in enumerate(last) if v + 1 == u]

        N_FILLS = 2 * H2 * TT + H2 * CT

        def fills_before(u, units):
            return sum(1 if c else 2 for h, c, t in units[:u])

        def group_end(u, units):
            h, c, t = units[u]
            return c * H2 + h if t + 1 == (CT if c else TT) else None

        def key_tiles(d, t):
            if d == 0:
                return list(range(t + 1))
            return list(range(t, CT)) if t < CT else list(range(CT)) + list(range(t, ST))

        def gw_layout(first):
            at, runs, where = 0, [[] for _ in range(ST)], {}
            for s in range(ST):
                for d in range(2):
                    seen = [t for t in range(first, ST) if s in key_tiles(d, t)]
                    while seen:
                        n = 1
                        while n < len(seen) and seen[n] == seen[0] + n:
                            n += 1
                        runs[s].append((d, seen[0], seen[0] + n, at))
                        for t in seen[:n]:
                            where[d, s, t] = at + (t - seen[0]) * P
                        at, seen = at + n * P, seen[n:]
            assert at <= PAIRS * P
            return runs, where

        block = ctx.enter_context(nc.Block())

        @block.sync
        def _(sp):
            sp.dma_start(x[:, :, :], dram["x"]).then_inc(x_loaded, 16)
            sp.dma_start(c0[:, :], dram["c0"]).then_inc(c0_loaded, 16)
            sp.dma_start(vec[:, :], dram["vec"]).then_inc(vec_loaded, 16)
            for j in range(RAW):
                sp.dma_start(w_raw[:, j, :], dram["w"][j, :, :]).then_inc(raw_ready[j], 16)
            sp.dma_start(c1[:, :], dram["c1"]).then_inc(c1_loaded, 16)
            with sp.Fori(1, CHUNKS // RAW) as g:
                for j in range(RAW):
                    sp.wait_ge(lo_ready, g * RAW + (j + 1 - RAW))
                    sp.dma_start(w_raw[:, j, :], dram["w"][g * RAW + j, :, :]).then_inc(raw_ready[j], 16)
            for k in range(KT):
                sp.wait_ge(xf_done, KT + (k + 1))
                sp.dma_start(out[:, k, :], x[:, k, :]).then_inc(stored, 16)
            sp.wait_ge(stored, KT * 16)

        @block.gpsimd
        def _(pool):
            with pool.Fori(0, CHUNKS // RING) as g:
                for j in range(RING):
                    pool.wait_ge(hi_ready, g * RING + (j + 1))
                    nc.gpsimd.tensor_tensor(w_lo[:, j, :], w_raw[:, j % RAW, :], w_hi[:, j, :].bitcast(F),
                                            ALU.subtract).then_inc(lo_ready, 1)

        @block.tensor
        def _(pe):
            def product(g, j, bank, rhs_hi, rhs_lo, blocks=range(KT)):
                n = len(blocks)
                for k, b in enumerate(blocks):
                    w = slice(b * P, (b + 1) * P)
                    nc.tensor.matmul(bank, w_hi[:, j, w], rhs_hi[:, k, :], start=(k == 0), stop=False)
                    nc.tensor.matmul(bank, w_hi[:, j, w], rhs_lo[:, k, :], start=False, stop=False)
                    last = nc.tensor.matmul(bank, w_lo[:, j, w], rhs_hi[:, k, :], start=False, stop=(k == n - 1))
                return last

            def arrive(g, j, more=0):
                pe.wait_ge(lo_ready, g * RING + (j + 1 + more))
                pe.wait_ge(bank_read[j], g + 2)

            def first_chunk(g, j, n):
                arrive(g, j)
                for k in range(KT):
                    pe.wait_ge(hlo_ready, n * KT + (k + 1))
                    w = slice(k * P, (k + 1) * P)
                    nc.tensor.matmul(ps[:, j, :], w_hi[:, j, w], h_hi[:, k, :], start=(k == 0), stop=False)
                    nc.tensor.matmul(ps[:, j, :], w_hi[:, j, w], h_lo[:, k, :], start=False, stop=False)
                    last = nc.tensor.matmul(ps[:, j, :], w_lo[:, j, w], h_hi[:, k, :], start=False, stop=(k == KT - 1))
                last.then_inc(chunk_used, 1)

            def half(j, e):
                for k in range(e * KT // 2, (e + 1) * KT // 2):
                    w = slice(k * P, (k + 1) * P)
                    nc.tensor.matmul(ps[:, j, :], w_hi[:, j, w], h_hi[:, k, :], start=(k == 0), stop=False)
                    nc.tensor.matmul(ps[:, j, :], w_hi[:, j, w], h_lo[:, k, :], start=False, stop=False)
                    last = nc.tensor.matmul(ps[:, j, :], w_lo[:, j, w], h_hi[:, k, :], start=False, stop=(k == KT - 1))
                return last

            def chunk(g, j, rhs_hi, rhs_lo, pads=0):
                arrive(g, j, pads)
                product(g, j, ps[:, j, :], rhs_hi, rhs_lo).then_inc(chunk_used, 1 + pads)

            def norm(n):
                for k in range(HALF_KT + 1):
                    if k < HALF_KT:
                        pe.wait_ge(sq_ready, n * KT + (k + 1))
                    else:
                        pe.wait_ge(sq_added, (n + 1) * (KT - HALF_KT - 1))
                    for t in range(TT):
                        last = nc.tensor.matmul(ps[:, 4, t:t + 1], squares[k][:, t * P:(t + 1) * P], ones[:, 0:1],
                                                start=(k == 0 and t == 0), stop=(k == HALF_KT), skip_group_check=True)
                last.then_inc(sq_used, 1)
                pe.wait_ge(diag_ready, n + 1)
                nc.tensor.matmul(ps[:, 5, :], ones, diag[:, :, :].rearrange("p t q -> p (t q)"),
                                 start=True, stop=True).then_inc(rb_ready, 1)

            def rotate(l, n, g, j, swap):
                pe.wait_ge(bank_read[j], g + 3)
                if not isinstance(n, int) or n >= 2:
                    pe.wait_ge(rope_half_done, l * (2 * N_ROPE) + n * 2 - 2)
                nc.tensor.matmul(ps[:, 4 + j % 2, :], swap, stage[:, j % 2, :], start=True, stop=True).then_inc(rot_ready, 1)

            def transposed(g, j):
                pe.wait_ge(bank_read[j], g + 3)
                for t in range(TT):
                    last = nc.tensor.transpose(ps[:, 6, t * P:(t + 1) * P], stage[:, j % 2, t * P:(t + 1) * P], ident)
                last.then_inc(vt_ready, 1)

            pe.wait_ge(c0_loaded, 16)
            with pe.Fori(0, DEPTH) as l:
                g0 = l * G1
                norm(2 * l)

                first_chunk(g0, 0, 2 * l)
                for j in range(RING):
                    if j > 0:
                        chunk(g0, j, h_hi, h_lo)
                        rotate(l, j - 1, g0, j - 1, swap_half)
                rotate(l, 3, g0, 3, swap_half)
                chunk(g0 + G_KV, 0, h_hi, h_lo)
                chunk(g0 + G_KV, 1, h_hi, h_lo, pads=2)
                rotate(l, 4, g0 + G_KV, 0, swap_half)
                transposed(g0 + G_KV, 1)

                pe.wait_ge(rope_done, l * N_ROPE + N_ROPE)
                pe.wait_ge(v_done, l + 1)

                def scores(u):
                    n, g, i = units[u]
                    rows = slice(g * HEAD, (g + 1) * HEAD)
                    keys = slice(max(n - 1, 0) * P, (n + 1) * P)
                    wide = keys.stop - keys.start
                    for e in range(2):
                        last = nc.tensor.matmul(ps[:, 4 + u % 2, e * 2 * P:e * 2 * P + wide], aq[rows, 2 * i + e, n * P:(n + 1) * P],
                                                ak[rows, keys], start=True, stop=True)
                    last.then_inc(sc_ready, 1)

                def weighted(u):
                    n, g, i = units[u]
                    pe.wait_ge(pt_copied, l * N_ATT + (u + 1))
                    if u >= 1:
                        pe.wait_ge(olo_ready, l * N_ATT + u)
                    first = 0 if n else 1
                    for b in range(first, 2):
                        last = nc.tensor.matmul(ps[g * HEAD:(g + 1) * HEAD, 7, 0:2 * P],
                                                av[:, n - 1 + b, g * HEAD:(g + 1) * HEAD], pt_sb[:, u % 2, b, :, :],
                                                start=(b == first), stop=(b == 1))
                    last.then_inc(pv_ready, 1)

                def finish(c):
                    pe.wait_ge(rz_ready, l * N_ATT + (c + 1))
                    if c < 2 * RET_HEADS:
                        nc.tensor.matmul(ps[:, c % RING, :], swap_pair, stage[:, c % 2, :], start=True, stop=True).then_inc(rturn_ready, 1)
                        return
                    for t in range(TT):
                        last = nc.tensor.transpose(ps[:, c % RING, t * P:(t + 1) * P], stage[:, c % 2, t * P:(t + 1) * P], ident)
                    last.then_inc(rturn_ready, 1)

                pe.wait_ge(c1_loaded, 16)
                scores(0)
                scores(1)
                for u in range(N_ATT):
                    n, g, i = units[u]
                    c, j = u, u % RING
                    arrive(g0 + (G_RET + c // RING), j)
                    half(j, 0)
                    if c >= 1:
                        finish(c - 1)
                    pe.wait_ge(p_ready, l * N_ATT + (u + 1))
                    if u >= 1:
                        pe.wait_ge(pt_copied, l * N_ATT + u)
                    for b in range(0 if n else 1, 2):
                        for e in range(2):
                            at = (b if n else 0) * P
                            last = nc.tensor.transpose(ps[:, 6, (b * 2 + e) * P:(b * 2 + e + 1) * P],
                                                       p_sb[:, u % 2, e, at:at + P], ident)
                    last.then_inc(pt_ready, 1)
                    if u + 2 < N_ATT:
                        scores(u + 2)
                    half(j, 1).then_inc(chunk_used, 1)
                    if u >= 1:
                        weighted(u - 1)
                weighted(N_ATT - 1)
                finish(N_ATT - 1)

                pe.wait_ge(rrope_done, l * 2 * RET_HEADS + 2 * RET_HEADS)
                for j in range(RING):
                    pe.wait_ge(bank_read[j], g0 + (G_RV + 4))
                pe.wait_ge(olo_ready, l * N_ATT + N_ATT)

                def ret_scores(h):
                    for t in range(TT):
                        if h >= 1:
                            pe.wait_ge(a_ready, l * 16 + (4 * (h - 1) + (t + 1 if t < 2 else 4)))
                        bank = ps[:, t, 0:SEQ - t * P] if t < 3 else ps[:, 2, 256:384]
                        nc.tensor.matmul(bank, rqk[:, RET_HEADS + h, t * P:(t + 1) * P], rqk[:, h, t * P:SEQ],
                                         start=True, stop=True).then_inc(rs_ready, 1)

                def ret_inner(h):
                    b = 4 + 2 * (h % 2)
                    if h >= 2:
                        pe.wait_ge(rcopy_done, l * 16 + 4 * (h - 1))
                    for t in range(TT):
                        pe.wait_ge(a_ready, l * 16 + (4 * h + t + 1))
                        for e in range(2):
                            last = nc.tensor.matmul(ps[:, b + e, t * P:SEQ], rv[:, t, h * RET_V + e * P:h * RET_V + (e + 1) * P],
                                                    a_sb[h % 2][:, RET_COL[t]:RET_COL[t + 1]], start=(t == 0), stop=(t == TT - 1))
                    last.then_inc(inner_ready, 1)

                def ret_squares(h):
                    pe.wait_ge(rcopy_done, l * 16 + 4 * (h + 1))
                    for t in range(TT):
                        for e in range(2):
                            last = nc.tensor.matmul(ps[:, 3, 4 * h + t:4 * h + t + 1], stage_2[:, e, t * P:(t + 1) * P], ones[:, 0:1],
                                                    start=(h == 0 and t == 0 and e == 0), stop=(e == 1), skip_group_check=True)
                    last.then_inc(rsq_used, 1)

                ret_scores(0)
                for h in range(RET_HEADS):
                    if h + 1 < RET_HEADS:
                        ret_scores(h + 1)
                    ret_inner(h)
                    if h >= 1:
                        ret_squares(h - 1)
                ret_squares(RET_HEADS - 1)
                for h in range(RET_HEADS):
                    pe.wait_ge(rdiag_ready, l * 4 + (h + 1))
                    nc.tensor.matmul(ps[:, 4 + h, :], ones, diag[:, :, :].rearrange("p t q -> p (t q)"),
                                     start=True, stop=True).then_inc(rrb_ready, 1)

                with pe.Fori(0, 2) as i:
                    for j in range(RING):
                        chunk(g0 + i + G_RG, j, h_hi, h_lo)
                pe.wait_ge(rr_ready, l * 8 + 8)
                for j in range(RING):
                    arrive(g0 + G_WA, j)
                    product(g0 + G_WA, j, ps[:, j, :], o_hi, o_lo, range(0, 4))
                    product(g0 + G_WA, j, ps[:, 4 + j, :], o_hi, o_lo, range(4, 8)).then_inc(chunk_used, 1)
                with pe.Fori(0, 2) as i:
                    pe.wait_ge(rlo_ready, l * 8 + 8)
                    for c in range(12):
                        src = (r_hi, r_lo) if c % 3 == 2 else (h_hi, h_lo)
                        chunk(g0 + i * 3 + (G_MIX + c // RING), c % RING, *src)
                with pe.Fori(0, 2) as i:
                    pe.wait_ge(mlo_ready, l * 8 + 8)
                    for j in range(RING):
                        chunk(g0 + i + G_OUT, j, mix_hi, mix_lo)
                norm(2 * l + 1)
                with pe.Fori(0, QUARTERS) as q:
                    with pe.Fori(0, 2) as i:
                        first_chunk(g0 + q * 4 + i + G_MLP, 0, 2 * l + 1)
                        for j in range(1, RING):
                            chunk(g0 + q * 4 + i + G_MLP, j, h_hi, h_lo)
                    with pe.Fori(0, 2) as i:
                        for j in range(RING):
                            arrive(g0 + q * 4 + i + (G_MLP + 2), j)
                            for k in range(KT):
                                pe.wait_ge(ulo_ready, l * N_MLP + q * KT + (k + 1))
                                w = slice(k * P, (k + 1) * P)
                                nc.tensor.matmul(ps[:, j, :], w_hi[:, j, w], u_hi[:, k, :], start=(k == 0), stop=False)
                                nc.tensor.matmul(ps[:, j, :], w_hi[:, j, w], u_lo[:, k, :], start=False, stop=False)
                                last = nc.tensor.matmul(ps[:, j, :], w_lo[:, j, w], u_hi[:, k, :], start=False, stop=(k == KT - 1))
                            last.then_inc(chunk_used, 1)

            def norm_2(n, first, read=None):
                if read is not None:
                    pe.wait_ge(bank_read[0], read + 3)
                for k in range(HALF_KT + 1):
                    if k < HALF_KT:
                        pe.wait_ge(sq_ready, n * KT + (k + 1))
                    else:
                        pe.wait_ge(sq_added, (n + 1) * (KT - HALF_KT - 1))
                    for t in range(first, ST):
                        last = nc.tensor.matmul(ps[:, 4, t:t + 1], squares_2[k][:, t * P:(t + 1) * P], ones[:, 0:1],
                                                start=(k == 0 and t == first), stop=(k == HALF_KT), skip_group_check=True)
                last.then_inc(sq_used, 1)
                pe.wait_ge(diag_ready, n + 1)
                if first == 0:
                    nc.tensor.matmul(ps[:, 6, 0:CTX], ones, diag_2[:, 0:CT, :].rearrange("p t q -> p (t q)"), start=True, stop=True)
                nc.tensor.matmul(ps[:, 5, :], ones, diag_2[:, CT:ST, :].rearrange("p t q -> p (t q)"),
                                 start=True, stop=True).then_inc(rb_ready, 1)

            def blocks_2(j, k, hi, lo, need_ctx):
                w = slice(k * P, (k + 1) * P)
                for part, bank in ((X, ps[:, j, :]), (C, ps[:, 4 + j, 0:CTX]))[:2 if need_ctx else 1]:
                    nc.tensor.matmul(bank, w_hi[:, j, w], hi[:, part], start=(k == 0), stop=False)
                    nc.tensor.matmul(bank, w_hi[:, j, w], lo[:, part], start=False, stop=False)
                    last = nc.tensor.matmul(bank, w_lo[:, j, w], hi[:, part], start=False, stop=(k == KT - 1))
                return last

            def chunk_2(g, j, hi, lo, need_ctx=True, pads=0, norm=None):
                arrive(g, j, pads)
                for k in range(KT):
                    if norm is not None:
                        pe.wait_ge(hlo_ready, norm * KT + k + 1)
                    last = blocks_2(j, k, hi(k), lo(k), need_ctx)
                last.then_inc(chunk_used, 1 + pads)

            def normed(g, j, need_ctx=True, pads=0, norm=None):
                chunk_2(g, j, lambda k: c_hi[:, k, :], lambda k: c_lo[:, k, :], need_ctx, pads, norm)

            def to_tokens(j, n, x_bank, c_bank):
                pe.wait_ge(z_ready, n + 1)
                for t in range(ST):
                    bank = ps[:, c_bank, t * P:(t + 1) * P] if t < CT else ps[:, x_bank, (t - CT) * P:(t - CT + 1) * P]
                    last = nc.tensor.transpose(bank, zm[:, j % 2, t * P:(t + 1) * P], ident)
                last.then_inc(ztok_ready, 1)

            def neighborhood(L, need_ctx, g0):
                units, base, nz = natt_units(need_ctx), L * N_UNITS, L * 16 + 4

                def scores(u):
                    h, c, t = units[u]
                    rows = slice(h % 2 * HEAD, h % 2 * HEAD + HEAD)
                    if u >= 2:
                        pe.wait_ge(nneg_ready, base + (u - 1))
                    if u >= 1:
                        pe.wait_ge(nsc_done, base + u)
                    at = (0 if c else CTX) + t * P
                    query = qn[rows, h // 2, at:at + P]
                    if not c:
                        nc.tensor.matmul(ps[:, 3 + u % 2, :], query, kn[rows, h // 2, X], start=True, stop=True)
                    nc.tensor.matmul(ps[:, 5, 0:CTX], query, kn[rows, h // 2, C], start=True, stop=True).then_inc(ns_ready, 1)

                def by_key(u, part):
                    h, c, t = units[u]
                    if part == 1 and c:
                        return
                    fills = fills_before(u, units) + part
                    pe.wait_ge(np_ready, base + (u + 1))
                    if fills:
                        pe.wait_ge(npt_copied, L * N_FILLS + fills)
                    of_x = part == 0 and not c
                    for s in range(TT if of_x else CT):
                        at = s * P + (CTX if of_x else 0)
                        last = nc.tensor.transpose(ps[:, 6, s * P:(s + 1) * P], sn[:, u % 3, at:at + P], ident)
                    last.then_inc(npt_ready, 1)

                def weighted(u):
                    h, c, t = units[u]
                    rows = slice(h % 2 * HEAD, h % 2 * HEAD + HEAD)
                    pe.wait_ge(npt_copied, L * N_FILLS + fills_before(u + 1, units))
                    if c * H2 + h >= 2 and t == 0:
                        pe.wait_ge(nlo_ready, L * (2 * H2) + c * H2 + h - 1)
                    keys = CT if c else ST
                    for s in range(keys):
                        last = nc.tensor.matmul(ps[rows, 7, t * P:(t + 1) * P], vn[:, s, h * HEAD:(h + 1) * HEAD],
                                                pn[:, u % 2, s * P:(s + 1) * P], start=(s == 0), stop=(s == keys - 1))
                    last.then_inc(npv_ready, 1)

                def parts(c, a, b):
                    g, j = g0 + G_QM + c // RING, c % RING
                    if a == 0:
                        pe.wait_ge(lo_ready, g * RING + j + 1)
                        pe.wait_ge(bank_read[(j + 2) % RING], g + (3 if j >= 2 else 2))
                    if a == KT:
                        pe.wait_ge(bank_read[(j + 3) % RING], g + (3 if j >= 1 else 2))
                    for i in range(a, b):
                        k = i % KT
                        w = slice(k * P, (k + 1) * P)
                        part, bank = (X, ps[:, c % 2, :]) if i < KT else (C, ps[:, 2, 0:CTX])
                        nc.tensor.matmul(bank, w_hi[:, j, w], c_hi[:, k, part], start=(k == 0), stop=False)
                        nc.tensor.matmul(bank, w_hi[:, j, w], c_lo[:, k, part], start=False, stop=False)
                        last = nc.tensor.matmul(bank, w_lo[:, j, w], c_hi[:, k, part], start=False, stop=(k == KT - 1))
                    if b == 2 * KT:
                        last.then_inc(chunk_used, 1)

                def finish(c):
                    if c < 2 * RING:
                        pe.wait_ge(z_ready, nz + c + 1)
                        nc.tensor.matmul(ps[:, c % 2, :], swap_half, zm[:, c % 2, X], start=True, stop=True).then_inc(zrot_ready, 1)
                    else:
                        to_tokens(c, nz + c, c % 2, 2)

                scores(0)
                scores(1)
                at = {place(u, need_ctx): u for u in range(len(units))}
                for c in range(M_TILES):
                    for q in range(4):
                        u = at.get(4 * c + q)
                        if u is not None and u >= 1:
                            by_key(u - 1, 1)
                        parts(c, 4 * q, 4 * q + 2)
                        if u is not None:
                            if u + 2 < len(units):
                                scores(u + 2)
                            by_key(u, 0)
                        parts(c, 4 * q + 2, 4 * q + 4)
                        if u is not None and u >= 1:
                            weighted(u - 1)
                        if q == 0 and c:
                            finish(c - 1)
                by_key(len(units) - 1, 1)
                weighted(len(units) - 1)
                finish(M_TILES - 1)
                pe.wait_ge(nlo_ready, L * (2 * H2) + group_end(len(units) - 1, units) + 1)
                for j in range(RING):
                    pe.wait_ge(bank_read[j], g0 + G_VM + 3)

            def mlstm(L, first):
                runs, where = gw_layout(first)
                pe.wait_ge(gate_a, L * 3 + 3)
                for t in range(ST):
                    bank = ps[:, 0, t * P:(t + 1) * P] if t < TT else ps[:, 1, (t - TT) * P:(t - TT + 1) * P]
                    last = nc.tensor.transpose(bank, key_w[:, t * P:(t + 1) * P], ident)
                last.then_inc(key_ready, 1)
                pe.wait_ge(key_copied, L + 1)

                def scores(h):
                    rows = slice(h % 2 * HEAD, h % 2 * HEAD + HEAD)
                    for s in range(ST):
                        n = h * ST + s
                        b = 2 * (n % 2)
                        t0 = max(first, CT if s >= CT else 0)
                        if s == 0 and h >= 2 and h % 2 == 0:
                            pe.wait_ge(head_done, L * H2 + h - 1)
                        if n >= 2:
                            pe.wait_ge(mg_ready, L * N_UNITS + (n - 1))
                        key = km[rows, h // 2, s * P:(s + 1) * P]
                        nc.tensor.matmul(ps[:, b, t0 * P:SEQ], key, qm[rows, h // 2, t0 * P:SEQ], start=True, stop=True)
                        nc.tensor.matmul(ps[:, b + 1, 0:ALL - SEQ], key, qm[rows, h // 2, SEQ:ALL],
                                         start=True, stop=True).then_inc(ms_ready, 1)

                def results(h, d):
                    b = 4 + 2 * d
                    pe.wait_ge(mg_ready, L * N_UNITS + (h + 1) * ST)
                    if h % 2:
                        pe.wait_ge(num_ready, 2 * (L * H2 + h - 1) + d + 1)
                    elif h:
                        pe.wait_ge(head_done, L * H2 + h)
                    order = [d] + [s for s in range(ST) if s != d]
                    pieces = [(s, max(t0 * P, e0), min(t1 * P, e1), e, at + max(0, e0 - t0 * P)) for s in order for d1, t0, t1, at in runs[s]
                              for e, (e0, e1) in enumerate(((0, SEQ), (SEQ, ALL))) if d1 == d and max(t0 * P, e0) < min(t1 * P, e1)]
                    for i, (s, a0, a1, e, at) in enumerate(pieces):
                        rest, before = [p[3] for p in pieces[i + 1:]], [p[3] for p in pieces[:i]]
                        last = nc.tensor.matmul(ps[0:HEAD + 1, b + e, a0 - e * SEQ:a1 - e * SEQ], vm[:, s, h, :], gw[:, h % 2, at:at + a1 - a0],
                                                start=(e not in before), stop=(e not in rest), skip_group_check=True)
                    last.then_inc(mpv_ready, 1)

                def by_token(h, d):
                    n = 2 * (L * H2 + h) + d
                    pe.wait_ge(num_ready, n + 1)
                    if h % 2 == 0:
                        pe.wait_ge(mg_ready, L * N_UNITS + (h + 2) * ST)
                    for t in range(first, ST):
                        last = nc.tensor.transpose(ps[:, 4 * (h % 2) + 2 * d, t * (HEAD + 1):(t + 1) * (HEAD + 1)],
                                                   num[0:HEAD + 1, d, t * P:(t + 1) * P], ident[0:HEAD + 1, 0:HEAD + 1])
                    last.then_inc(num_token, 1)

                for h in range(0, H2, 2):
                    scores(h)
                    scores(h + 1)
                    results(h, 0)
                    results(h, 1)
                    by_token(h, 0)
                    results(h + 1, 0)
                    by_token(h, 1)
                    results(h + 1, 1)
                    by_token(h + 1, 0)
                    by_token(h + 1, 1)
                pe.wait_ge(ln_v, L * 6 + 6)
                for f in range(4):
                    for t in range(first, ST):
                        bank = ps[:, 2 * f + 1, t * P:(t + 1) * P] if t < CT else ps[:, 2 * f, (t - CT) * P:(t - CT + 1) * P]
                        last = nc.tensor.transpose(bank, hs[:, t, 2 * f:2 * f + 2, :].rearrange("p h d -> p (h d)"), ident)
                    last.then_inc(yt_ready, 1)

            norm(FIRST_MOD)
            for L in range(DEPTH):
                need_ctx = L + 1 < DEPTH
                first = 0 if need_ctx else CT
                g0 = START_2 + L * G2
                nz = L * 16
                norm_2(FIRST_MOD + 1 + 2 * L, 0, g0 - 1 if L else None)
                pe.wait_ge(c2_loaded, 16)
                with pe.Fori(0, G_VN) as i:
                    normed(g0 + i, 0, norm=FIRST_MOD + 2 * L)
                    for j in range(1, RING):
                        normed(g0 + i, j)
                for j in range(RING):
                    normed(g0 + G_VN, j)
                    if j > 0:
                        to_tokens(j - 1, nz + j - 1, j - 1, 4 + j - 1)
                to_tokens(3, nz + 3, 3, 7)
                normed(g0 + G_GATE, 0, pads=3)
                for j in range(RING):
                    pe.wait_ge(bank_read[j], g0 + G_GATE + 3)
                neighborhood(L, need_ctx, g0)
                for j in range(RING):
                    normed(g0 + G_OM, j)
                for j in range(RING):
                    pe.wait_ge(bank_read[j], g0 + G_OM + 3)
                mlstm(L, first)
                pe.wait_ge(ylo_ready, L * 4 + 4)
                y_hi = lambda k: ym_hi[:, k, :] if k < 4 else yn_hi[:, k - 4, :]
                y_lo = lambda k: ym_lo[:, k, :] if k < 4 else yn_lo[:, k - 4, :]
                with pe.Fori(0, 2) as i:
                    for j in range(RING):
                        chunk_2(g0 + i + G_OUT2, j, y_hi, y_lo, need_ctx)
                norm_2(FIRST_MOD + 2 + 2 * L, first, g0 + G_OUT2 + 1)
                with pe.Fori(0, QUARTERS) as q:
                    with pe.Fori(0, 2) as i:
                        normed(g0 + q * 4 + i + G_UP, 0, need_ctx, norm=FIRST_MOD + 2 * L + 1)
                        for j in range(1, RING):
                            normed(g0 + q * 4 + i + G_UP, j, need_ctx)
                    with pe.Fori(0, 2) as i:
                        for j in range(RING):
                            arrive(g0 + q * 4 + i + (G_UP + 2), j)
                            for k in range(KT):
                                pe.wait_ge(ulo_ready, q * KT + ((DEPTH + L) * N_MLP + k + 1))
                                last = blocks_2(j, k, u2_hi[:, k, :], u2_lo[:, k, :], need_ctx)
                            last.then_inc(chunk_used, 1)
            norm_2(FIRST_MOD + 1 + 2 * DEPTH, CT)

        @block.scalar
        def _(act):
            def split(g, j):
                act.wait_ge(chunk_used, g * RING + (j + 1))
                act.wait_ge(raw_ready[j % RAW], g * 32 + 16 * (RING // RAW + 1 + j // RAW))
                nc.scalar.activation(w_hi[:, j, :], w_raw[:, j % RAW, :], ACT.Copy).then_inc(hi_ready, 1)

            def square(k, read):
                act.wait_ge(bank_read[k % RING], read + (k // RING + 3))
                nc.scalar.activation(squares[k], x[:, k, :], ACT.Square).then_inc(sq_ready, 1)

            def root(n):
                act.wait_ge(sq_used, n + 1)
                nc.scalar.activation(rms[:, 0, 0:TT], ps[:, 4, 0:TT], ACT.Sqrt, bias=eps[:, 0:1], scale=1.0 / D_MODEL).then_inc(std_ready, 1)

            def norm(n):
                root(n)
                for k in range(KT):
                    act.wait_ge(hf_ready, n * KT + (k + 1))
                    nc.scalar.activation(h_hi[:, k, :], tmp[:, k % 2, :], ACT.Copy).then_inc(hhi_ready, 1)

            for j in range(RING):
                act.wait_ge(raw_ready[j % RAW], 16 * (1 + j // RAW))
                nc.scalar.activation(w_hi[:, j, :], w_raw[:, j % RAW, :], ACT.Copy).then_inc(hi_ready, 1)

            for k in range(KT):
                square(k, -2)
            with act.Fori(0, DEPTH) as l:
                g0 = l * G1

                def to_stage(g, j):
                    act.wait_ge(chunk_used, g * RING + (j + 1))
                    nc.scalar.activation(stage[:, j % 2, :], ps[:, j, :], ACT.Copy).then_inc(bank_read[j], 1)

                norm(2 * l)
                for j in range(RING):
                    if j >= 2:
                        act.wait_ge(rope_half_done, l * (2 * N_ROPE) + 2 * (j - 1))
                    to_stage(g0, j)
                    split(g0, j)
                for j in range(2):
                    act.wait_ge(rope_half_done, l * (2 * N_ROPE) + 2 * (3 + j))
                    to_stage(g0 + G_KV, j)
                    split(g0 + G_KV, j)
                for j in range(2, RING):
                    act.sem_inc(bank_read[j], 1)
                    split(g0 + G_KV, j)

                def probabilities_by_key(u):
                    n = units[u][0]
                    act.wait_ge(pt_ready, l * N_ATT + (u + 1))
                    if u >= 2:
                        act.wait_ge(pv_ready, l * N_ATT + (u - 1))
                    b = slice(0 if n else 1, 2)
                    nc.scalar.activation(pt_sb[:, u % 2, b, :, :],
                                         ps[:, 6, :].rearrange("p (b e q) -> p b e q", b=2, e=2)[:, b, :, :],
                                         ACT.Copy).then_inc(pt_copied, 1)

                def output_upper(u):
                    n, g, i = units[u]
                    rows = slice(g * HEAD, (g + 1) * HEAD)
                    act.wait_ge(pv_ready, l * N_ATT + (u + 1))
                    nc.scalar.activation(o_hi[rows, 2 * i:2 * i + 2, n * P:(n + 1) * P],
                                         ps[rows, 7, 0:2 * P].rearrange("p (e q) -> p e q", e=2), ACT.Copy).then_inc(ohi_ready, 1)

                def take(c):
                    g, j = g0 + (G_RET + c // RING), c % RING
                    act.wait_ge(chunk_used, g * RING + (j + 1))
                    if c >= 2:
                        act.wait_ge(bank_read[(j + 2) % RING], g + (3 if j >= 2 else 2))
                    nc.scalar.activation(stage[:, c % 2, :], ps[:, j, :], ACT.Copy).then_inc(rz_ready, 1)
                    split(g, j)

                act.wait_ge(rope_done, l * N_ROPE + N_ROPE)
                act.wait_ge(v_done, l + 1)
                for u in range(N_ATT):
                    wide = 2 * P if units[u][0] else P
                    act.wait_ge(nm_ready, l * N_ATT + (u + 1))
                    for e in range(2):
                        nc.scalar.activation(p_sb[:, u % 2, e, 0:wide], s_sb[:, u % 2, e, 0:wide], ACT.Exp,
                                             bias=tiny[:, u % 2, e:e + 1], accum_out=tiny[:, u % 2, 4 + e:5 + e])
                    nc.scalar.activation(tiny[:, u % 2, 6:8], tiny[:, u % 2, 2:4], ACT.Exp).then_inc(exp_done, 1)
                    if u >= 1:
                        probabilities_by_key(u - 1)
                    if u >= 2:
                        output_upper(u - 2)
                    if u >= 1:
                        take(u - 1)
                probabilities_by_key(N_ATT - 1)
                output_upper(N_ATT - 2)
                take(N_ATT - 1)
                output_upper(N_ATT - 1)

                for h in range(RET_HEADS):
                    act.wait_ge(inner_ready, l * RET_HEADS + (h + 1))
                    b = 4 + 2 * (h % 2)
                    for e in range(2):
                        nc.scalar.activation(r_raw[:, 2 * h + e, :], ps[:, b + e, :], ACT.Copy).then_inc(rcopy_done, 1)
                    if h >= 1:
                        act.wait_ge(rsq_used, l * RET_HEADS + h)
                    for e in range(2):
                        nc.scalar.activation(stage_2[:, e, :], ps[:, b + e, :], ACT.Square).then_inc(rcopy_done, 1)
                act.wait_ge(rsq_used, l * RET_HEADS + RET_HEADS)
                nc.scalar.activation(rms[:, 0, 0:16], ps[:, 3, 0:16], ACT.Sqrt, bias=eps[:, 0:1], scale=1.0 / RET_V).then_inc(rstd_ready, 1)
                with act.Fori(0, 2) as i:
                    g = g0 + i + G_RG
                    for j in range(RING):
                        act.wait_ge(chunk_used, g * RING + (j + 1))
                        act.wait_ge(bank_read[(j + 2) % RING], g + (3 if j >= 2 else 2))
                        nc.scalar.activation(stage[:, j % 2, :], ps[:, j, :], ACT.Tanh, scale=0.5).then_inc(tanh_ready, 1)
                        split(g, j)
                        act.wait_ge(rr_ready, l * KT + i * 4 + (j + 1))
                        nc.scalar.activation(r_hi[:, ds(i * 4 + j, 1), :].rearrange("p o t -> p (o t)"), tmp_2[:, j % 2, :], ACT.Copy).then_inc(rhi_ready, 1)
                for j in range(RING):
                    act.wait_ge(chunk_used, (g0 + G_WA) * RING + (j + 1))
                    nc.scalar.activation(y_a[:, 2 * j, :], ps[:, j, :], ACT.Copy)
                    nc.scalar.activation(y_a[:, 2 * j + 1, :], ps[:, 4 + j, :], ACT.Copy).then_inc(bank_read[j], 1)
                    split(g0 + G_WA, j)
                with act.Fori(0, 2) as i:
                    for m in range(RING):
                        for c in range(3 * m, 3 * m + 3):
                            g, j = g0 + i * 3 + (G_MIX + c // RING), c % RING
                            if c % 3 < 2:
                                act.wait_ge(chunk_used, g * RING + (j + 1))
                                nc.scalar.activation((stage, stage_2)[c % 3][:, m % 2, :], ps[:, j, :], ACT.Tanh, scale=0.5).then_inc(bank_read[j], 1)
                            split(g, j)
                        act.wait_ge(mx_ready, l * KT + i * 4 + (m + 1))
                        nc.scalar.activation(mix_hi[:, ds(i * 4 + m, 1), :].rearrange("p o t -> p (o t)"), tmp_2[:, m % 2, :], ACT.Copy).then_inc(mhi_ready, 1)
                for k in range(KT):
                    split(g0 + (G_OUT + k // RING), k % RING)
                    if k:
                        square(k - 1, g0 + G_OUT)
                square(KT - 1, g0 + G_OUT)
                norm(2 * l + 1)
                act.dma_start(c_raw[:, :, :], dram["c"].broadcast_to([P, 2, D_MODEL])).then_inc(c_loaded, 16)
                act.wait_ge(c_loaded, l * 16 + 16)
                nc.scalar.activation(c_silu[:, :, :], c_raw[:, :, :], ACT.Tanh, scale=0.5).then_inc(ct_ready, 1)

                def ada_load(n):
                    act.wait_ge(ada_used, n + 1)
                    for s in range(3):
                        act.dma_start(ada_w[:, s, :], dram["ada"][ds(n * 3 + s, 1), :, :].rearrange("o p k -> p (o k)")).then_inc(ada_ready[s], 16)

                def up(q):
                    with act.Fori(0, 2) as i:
                        g = g0 + q * 4 + i + G_MLP
                        ada_load(l * 16 + q * 4 + i)
                        for j in range(RING):
                            act.wait_ge(chunk_used, g * RING + (j + 1))
                            nc.scalar.activation(stage[:, j % 2, :], ps[:, j, :], ACT.Relu).then_inc(bank_read[j], 1)
                            split(g, j)
                            act.wait_ge(v2_ready, l * N_MLP + q * KT + i * 4 + (j + 1))
                            nc.scalar.activation(u_hi[:, ds(i * 4 + j, 1), :].rearrange("p o t -> p (o t)"), tmp[:, j % 2, :], ACT.Copy).then_inc(uhi_ready, 1)

                with act.Fori(0, QUARTERS - 1) as q:
                    up(q)
                    with act.Fori(0, 2) as i:
                        ada_load(l * 16 + q * 4 + i + 2)
                        for j in range(RING):
                            split(g0 + q * 4 + i + (G_MLP + 2), j)
                up(QUARTERS - 1)
                last = G_MLP + 4 * QUARTERS - 2
                for k in range(KT):
                    if k % RING == 0:
                        ada_load(l * 16 + (4 * QUARTERS - 2 + k // RING))
                    split(g0 + (last + k // RING), k % RING)
                    if k:
                        square(k - 1, g0 + last)
                square(KT - 1, g0 + last)

            def square_2(k, first, read=None):
                if read is not None:
                    act.wait_ge(bank_read[k % RING], read + k // RING + 3)
                if first == 0:
                    nc.scalar.activation(squares_2[k][:, C], cx[:, k, :], ACT.Square)
                nc.scalar.activation(squares_2[k][:, X], x[:, k, :], ACT.Square).then_inc(sq_ready, 1)

            def norm_2(n, first, m, L, col):
                act.wait_ge(sq_used, n + 1)
                nc.scalar.activation(rms[:, 0, first:ST], ps[:, 4, first:ST], ACT.Sqrt, bias=eps[:, 0:1], scale=1.0 / D_MODEL).then_inc(std_ready, 1)
                if m is None:
                    return
                for k in range(KT):
                    act.wait_ge(hf_ready, m * KT + (k + 1))
                    at = L * ADA + col + k
                    if first == 0:
                        nc.scalar.activation(c_hi[:, k, C], hf_2[:, k % 2, C], ACT.Identity, bias=mod[:, 1, at:at + 1])
                    nc.scalar.activation(c_hi[:, k, X], hf_2[:, k % 2, X], ACT.Identity, bias=mod[:, 0, at:at + 1]).then_inc(hhi_ready, 1)

            def z_slot(g, j):
                act.wait_ge(chunk_used, g * RING + (j + 1))
                act.wait_ge(bank_read[(j + 2) % RING], g + (3 if j >= 2 else 2))

            def copy_out(g, j, x_bank, c_bank):
                z_slot(g, j)
                nc.scalar.activation(zm[:, j % 2, C], ps[:, c_bank, 0:CTX], ACT.Copy)
                nc.scalar.activation(zm[:, j % 2, X], ps[:, x_bank, :], ACT.Copy).then_inc(z_ready, 1)
                split(g, j)

            def load_bias(L, h):
                act.dma_start(bias[:, h % 2, :], dram["rpb"][L, h, :, :]).then_inc(bias_loaded[h % 2], 16)

            def neighborhood(L, need_ctx, g0):
                units, base = natt_units(need_ctx), L * N_UNITS

                def context_scores(u):
                    act.wait_ge(ns_ready, base + (u + 1))
                    if u >= 3:
                        act.wait_ge(npt_ready, L * N_FILLS + fills_before(u - 2, units))
                    nc.scalar.activation(sn[:, u % 3, C], ps[:, 5, 0:CTX], ACT.Copy, scale=HEAD ** -0.5).then_inc(nsc_done, 1)

                def by_key(u, part):
                    if part == 1 and units[u][1]:
                        return
                    if u >= 2:
                        act.wait_ge(npv_ready, base + (u - 1))
                    act.wait_ge(npt_ready, L * N_FILLS + fills_before(u, units) + part + 1)
                    if part == 0 and not units[u][1]:
                        nc.scalar.activation(pn[:, u % 2, X], ps[:, 6, :], ACT.Copy).then_inc(npt_copied, 1)
                        return
                    nc.scalar.activation(pn[:, u % 2, C], ps[:, 6, 0:CTX], ACT.Copy).then_inc(npt_copied, 1)

                def upper(u):
                    h, c, t = units[u]
                    rows = slice(h % 2 * HEAD, h % 2 * HEAD + HEAD)
                    act.wait_ge(npv_ready, base + (u + 1))
                    part = C if c else X
                    nc.scalar.activation(yn_hi[rows, h // 2, part], ps[rows, 7, 0:part.stop - part.start], ACT.Copy).then_inc(nhi_ready, 1)
                    if not c and h + 2 < H2:
                        load_bias(L, h + 2)

                def take(c):
                    g, j = g0 + G_QM + c // RING, c % RING
                    if c >= 2 * RING:
                        copy_out(g, j, c % 2, 2)
                        return
                    z_slot(g, j)
                    nc.scalar.activation((qm, km)[c // RING][:, j, C], ps[:, 2, 0:CTX], ACT.Copy)
                    nc.scalar.activation(zm[:, j % 2, X], ps[:, c % 2, :], ACT.Copy).then_inc(z_ready, 1)
                    split(g, j)

                act.wait_ge(spilled, (L + 1) * 32)
                context_scores(0)
                for u in range(len(units)):
                    wide = CTX if units[u][1] else ALL
                    if u >= 2:
                        by_key(u - 2, 1)
                    if u >= 3 and group_end(u - 3, units) is not None:
                        upper(u - 3)
                    act.wait_ge(nneg_ready, base + (u + 1))
                    nc.scalar.activation(sn[:, u % 3, 0:wide], sn[:, u % 3, 0:wide], ACT.Exp, bias=tiny[:, u % 2, 0:1],
                                         accum_out=tiny[:, u % 2, 1:2]).then_inc(nexp_done, 1)
                    if u + 1 < len(units):
                        context_scores(u + 1)
                    if u >= 1:
                        by_key(u - 1, 0)
                    for c in tiles_after(u, units, need_ctx, 0):
                        take(c)
                by_key(len(units) - 2, 1)
                by_key(len(units) - 1, 0)
                take(M_TILES - 1)
                by_key(len(units) - 1, 1)
                for u in range(len(units) - 3, len(units)):
                    if group_end(u, units) is not None:
                        upper(u)

            def gate_rows(L):
                f = slice(64, P)
                act.wait_ge(gate_v, L * 9 + 2)
                nc.scalar.activation(cum_f[f, :], cum_f[f, :], ACT.Exp).then_inc(gate_a, 1)
                act.wait_ge(gate_a, L * 3 + 1)
                nc.scalar.activation(cum_f[f, :], cum_f[f, :], ACT.Ln, bias=ones[f, 0:1]).then_inc(gate_a, 1)

            def gate_rows_end(L):
                act.wait_ge(gate_v, L * 9 + 9)
                for d in range(2):
                    act.dma_start(m_spill[d, :, :], run_m[32 * d:32 * d + H2, :]).then_inc(m_stored, 16)
                nc.scalar.activation(key_w[64:P, :], key_w[64:P, :], ACT.Exp, scale=-1.0).then_inc(gate_a, 1)

            def mlstm(L, first):
                runs, where = gw_layout(first)
                last_row = first * P

                def load_maxima(h):
                    act.dma_start(m_row[:, h % 2, :, :], m_spill[:, h, :].rearrange("d (o t) -> o d t", o=1).broadcast_to([P, 2, ALL])).then_inc(m_loaded[h % 2], 16)

                act.wait_ge(m_stored, (L + 1) * 32)
                load_maxima(0)
                load_maxima(1)
                act.wait_ge(key_ready, L + 1)
                nc.scalar.activation(key_t[:, 0:TT, :], ps[:, 0, :].rearrange("p (t c) -> p t c", t=TT), ACT.Copy)
                nc.scalar.activation(key_t[:, TT:ST, :], ps[:, 1, 0:CTX].rearrange("p (t c) -> p t c", t=CT), ACT.Copy).then_inc(key_copied, 1)
                act.wait_ge(key_copied, L + 1)
                def weights(h):
                    act.wait_ge(m_loaded[h % 2], (L * 4 + h // 2 + 1) * 16)
                    act.wait_ge(mdiag_ready, L * H2 + h + 1)
                    for s in range(ST):
                        for d, t0, t1, at in runs[s]:
                            for a, b in ((t0, s), (s + 1, t1)) if t0 <= s < t1 else ((t0, t1),):
                                if a < b:
                                    last = nc.scalar.activation(gw[:, h % 2, at + (a - t0) * P:at + (b - t0) * P], m_row[:, h % 2, d, a * P:b * P], ACT.Exp,
                                                                bias=key_t[:, s, 32 * d + h:32 * d + h + 1], scale=-1.0)
                            if t0 <= s < t1:
                                one = gw[:, h % 2, at + (s - t0) * P:at + (s - t0 + 1) * P]
                                last = nc.scalar.activation(one, one, ACT.Exp, scale=-1.0)
                        last.then_inc(mw_ready, 1)
                    if h + 2 < H2:
                        act.wait_ge(mw_ready, L * N_UNITS + (h + 1) * ST)
                        load_maxima(h + 2)

                weights(0)
                weights(1)
                for h in range(H2):
                    for d in range(2):
                        n = 2 * (L * H2 + h) + d
                        act.wait_ge(mpv_ready, n + 1)
                        if h >= 1:
                            act.wait_ge(num_token, n - 1)
                        both = ps[0:HEAD + 1, 4 + 2 * d:6 + 2 * d, :].rearrange("p b t -> p (b t)")
                        nc.scalar.activation(num[0:HEAD + 1, d, last_row:ALL], both[:, last_row:ALL], ACT.Copy).then_inc(num_ready, 1)
                    if h + 2 < H2:
                        weights(h + 2)
                act.wait_ge(ln_v, L * 6 + 3)
                nc.scalar.activation(hq[:, first:ST, :, :], hs[:, first:ST, :, :], ACT.Square).then_inc(ln_a, 1)
                act.wait_ge(ln_v, L * 6 + 4)
                nc.scalar.activation(cols[:, 2, first * H2:ST * H2], cols[:, 1, first * H2:ST * H2], ACT.Sqrt, bias=eps[:, 0:1], scale=1.0 / HEAD).then_inc(ln_a, 1)
                act.wait_ge(yt_ready, L * 4 + 4)
                act.dma_start(x[:, :, :], x_spill).then_inc(reloaded, 16)
                act.dma_start(cx[:, :, :], cx_spill).then_inc(reloaded, 16)
                for f in range(4):
                    act.wait_ge(yu_ready, L * 4 + (f + 1))
                    nc.scalar.activation(ym_hi[:, f, last_row:ALL], yu[:, f, last_row:ALL], ACT.Copy).then_inc(yhi_ready, 1)

            act.wait_ge(hlo_ready, FIRST_MOD * KT)
            act.dma_start(c2[:, :], dram["c2"]).then_inc(c2_loaded, 16)
            root(FIRST_MOD)
            act.wait_ge(rb_ready, FIRST_MOD + 1)
            act.dma_start(cx[:, :, :], dram["ctx"]).then_inc(cx_loaded, 16)
            act.wait_ge(ada_used, DEPTH * (ADA // 3) + 1)
            act.wait_ge(cx_loaded, 16)
            for k in range(KT):
                act.wait_ge(xf_done, k + 1)
                square_2(k, 0)
            for L in range(DEPTH):
                need_ctx = L + 1 < DEPTH
                first = 0 if need_ctx else CT
                g0 = START_2 + L * G2
                norm_2(FIRST_MOD + 1 + 2 * L, 0, FIRST_MOD + 2 * L, L, 0)
                act.wait_ge(hlo_ready, (FIRST_MOD + 2 * L + 1) * KT)
                act.dma_start(x_spill, x[:, :, :]).then_inc(spilled, 16)
                act.dma_start(cx_spill, cx[:, :, :]).then_inc(spilled, 16)
                for t, dst in enumerate((qn, kn)):
                    for j in range(RING):
                        act.wait_ge(chunk_used, (g0 + t) * RING + (j + 1))
                        nc.scalar.activation(dst[:, j, C], ps[:, 4 + j, 0:CTX], ACT.Copy)
                        nc.scalar.activation(dst[:, j, X], ps[:, j, :], ACT.Copy).then_inc(bank_read[j], 1)
                        split(g0 + t, j)
                load_bias(L, 0)
                load_bias(L, 1)
                for j in range(RING):
                    copy_out(g0 + G_VN, j, j, 4 + j)
                split(g0 + G_GATE, 0)
                for j in range(1, RING):
                    act.sem_inc(bank_read[j], 1)
                    split(g0 + G_GATE, j)
                neighborhood(L, need_ctx, g0)
                gate_rows(L)
                gate_rows_end(L)
                act.wait_ge(bank_read[3], g0 + G_VM + 3)
                for j in range(RING):
                    act.wait_ge(chunk_used, (g0 + G_OM) * RING + (j + 1))
                    nc.scalar.activation(om[:, j, C], ps[:, 4 + j, 0:CTX], ACT.Tanh, scale=0.5)
                    nc.scalar.activation(om[:, j, X], ps[:, j, :], ACT.Tanh, scale=0.5).then_inc(bank_read[j], 1)
                    split(g0 + G_OM, j)
                mlstm(L, first)
                for k in range(KT):
                    split(g0 + G_OUT2 + k // RING, k % RING)
                    if k:
                        square_2(k - 1, first, g0 + G_OUT2)
                square_2(KT - 1, first, g0 + G_OUT2)
                norm_2(FIRST_MOD + 2 + 2 * L, first, FIRST_MOD + 2 * L + 1, L, 3 * KT)
                lo = first * P

                def up_2(q):
                    with act.Fori(0, 2) as i:
                        g = g0 + q * 4 + i + G_UP
                        for j in range(RING):
                            act.wait_ge(chunk_used, g * RING + (j + 1))
                            if need_ctx:
                                nc.scalar.activation(sq_2[:, j % 2, C], ps[:, 4 + j, 0:CTX], ACT.Relu)
                            nc.scalar.activation(sq_2[:, j % 2, X], ps[:, j, :], ACT.Relu).then_inc(bank_read[j], 1)
                            split(g, j)
                            act.wait_ge(v2_ready, q * KT + i * 4 + ((DEPTH + L) * N_MLP + j + 1))
                            nc.scalar.activation(u2_hi[:, ds(i * 4 + j, 1), lo:ALL].rearrange("p o t -> p (o t)"), hf_2[:, j % 2, lo:ALL], ACT.Copy).then_inc(uhi_ready, 1)

                with act.Fori(0, QUARTERS - 1) as q:
                    up_2(q)
                    with act.Fori(0, 2) as i:
                        for j in range(RING):
                            split(g0 + q * 4 + i + (G_UP + 2), j)
                up_2(QUARTERS - 1)
                done = g0 + G_UP + 4 * QUARTERS - 2
                for k in range(KT):
                    split(done + k // RING, k % RING)
                    if k:
                        square_2(k - 1, 0 if need_ctx else CT, done)
                square_2(KT - 1, 0 if need_ctx else CT, done)
            norm_2(FIRST_MOD + 1 + 2 * DEPTH, CT, None, None, None)

        @block.vector
        def _(dve):
            def spread(col):
                return (diag[:, :, :], ident.rearrange("p (o q) -> p o q", o=1).broadcast_to([P, TT, P]),
                        rms[:, 1, col:col + TT].rearrange("p (t o) -> p t o", o=1).broadcast_to([P, TT, P]), ALU.mult)

            def add_squares(n, tiles):
                for a in range(1, len(tiles)):
                    dve.wait_ge(sq_ready, n * KT + (KT - len(tiles) + a + 1))
                    if a >= 2:
                        dve.wait_ge(sq_added, n * (len(tiles) - 1) + (a - 1))
                    nc.vector.tensor_tensor(tiles[0], tiles[0], tiles[a], ALU.add).then_inc(sq_added, 1)

            def root(n):
                add_squares(n, squares[HALF_KT:])
                dve.wait_ge(std_ready, n + 1)
                nc.vector.reciprocal(rms[:, 1, 0:TT], rms[:, 0, 0:TT]).then_inc(rinv_ready, 1)
                dve.wait_ge(rinv_ready, n + 1)
                nc.vector.tensor_tensor(*spread(0)).then_inc(diag_ready, 1)
                dve.wait_ge(rb_ready, n + 1)

            def norm(n):
                root(n)

                def lower(k):
                    dve.wait_ge(hhi_ready, n * KT + (k + 1))
                    nc.vector.tensor_tensor(h_lo[:, k, :], tmp[:, k % 2, :], h_hi[:, k, :].bitcast(F), ALU.subtract).then_inc(hlo_ready, 1)

                for k in range(KT):
                    if k >= 2:
                        dve.wait_ge(hlo_ready, n * KT + (k - 1))
                    nc.vector.scalar_tensor_tensor(tmp[:, k % 2, :], x[:, k, :], gain_now[:, k:k + 1], ps[:, 5, :],
                                                   ALU.mult, ALU.mult).then_inc(hf_ready, 1)
                    if k >= 1:
                        lower(k - 1)
                lower(KT - 1)

            nc.vector.memset(eps[:, :], EPS).then_inc(eps_set, 1)
            dve.wait_ge(eps_set, 1)
            dve.wait_ge(x_loaded, 16)
            dve.wait_ge(vec_loaded, 16)
            for j in range(RING):
                dve.sem_inc(bank_read[j], 2)
            dve.sem_inc(ada_used, 1)
            dve.wait_ge(c0_loaded, 16)
            dve.wait_ge(c1_loaded, 16)

            with dve.Fori(0, DEPTH) as l:
                g0 = l * G1
                nc.vector.tensor_copy(gain_now[:, :], vec[:, ds(l * KT + V_GMIX, KT)]).then_inc(layer_vec, 1)
                nc.vector.tensor_copy(sink_now[:, 0, :], vec[:, ds(l * ATT_HEADS + V_SINK, ATT_HEADS)]).then_inc(layer_vec, 1)
                dve.wait_ge(layer_vec, l * 4 + 2)
                nc.vector.tensor_scalar(sink_now[:, 1, :], sink_now[:, 0, :], -1.0, None, ALU.mult).then_inc(layer_vec, 1)
                norm(2 * l)

                def rope(n, g, j, cos, sin, dst):
                    dve.wait_ge(bank_read[j], g + 3)
                    if not isinstance(n, int) or n:
                        dve.wait_ge(rope_done, l * N_ROPE + n)
                    nc.vector.tensor_tensor(tmp[:, j % 2, :], stage[:, j % 2, :], cos, ALU.mult).then_inc(rope_half_done, 1)
                    dve.wait_ge(rot_ready, l * N_ROPE + n + 1)
                    nc.vector.tensor_tensor(tmp_2[:, j % 2, :], ps[:, 4 + j % 2, :], sin, ALU.mult).then_inc(rope_half_done, 1)
                    dve.wait_ge(rope_half_done, l * (2 * N_ROPE) + n * 2 + 2)
                    nc.vector.tensor_tensor(dst, tmp[:, j % 2, :], tmp_2[:, j % 2, :], ALU.add).then_inc(rope_done, 1)

                for j in range(RING):
                    rope(j, g0, j, att_cos, att_sin, aq[:, j, :])
                rope(RING, g0 + G_KV, 0, att_cos, att_sin, ak[:, :])
                dve.wait_ge(vt_ready, l + 1)
                nc.vector.tensor_copy(av[:, :, :], ps[:, 6, :].rearrange("p (t d) -> p t d", t=TT)).then_inc(v_done, 1)

                def normalised(u):
                    wide = 2 * P if units[u][0] else P
                    c = tiny[:, u % 2, :]
                    dve.wait_ge(exp_done, l * N_ATT + (u + 1))
                    nc.vector.tensor_tensor(c[:, 8:10], c[:, 4:6], c[:, 6:8], ALU.add).then_inc(den_done, 1)
                    dve.wait_ge(den_done, l * (2 * N_ATT) + (2 * u + 1))
                    nc.vector.reciprocal(c[:, 10:12], c[:, 8:10]).then_inc(den_done, 1)
                    dve.wait_ge(den_done, l * (2 * N_ATT) + (2 * u + 2))
                    for e in range(2):
                        last = nc.vector.tensor_scalar(p_sb[:, u % 2, e, 0:wide], p_sb[:, u % 2, e, 0:wide], c[:, 10 + e:11 + e], None, ALU.mult)
                    last.then_inc(p_ready, 1)

                def output_lower(u):
                    n, g, i = units[u]
                    rows = slice(g * HEAD, (g + 1) * HEAD)
                    at = (rows, slice(2 * i, 2 * i + 2), slice(n * P, (n + 1) * P))
                    dve.wait_ge(ohi_ready, l * N_ATT + (u + 1))
                    nc.vector.tensor_tensor(o_lo[at], ps[rows, 7, 0:2 * P].rearrange("p (e q) -> p e q", e=2),
                                            o_hi[at].bitcast(F), ALU.subtract).then_inc(olo_ready, 1)

                def take(i):
                    g, j, n = g0 + (G_RET + i // RING), i % RING, l * 2 * RET_HEADS + i
                    if i >= 2 * RET_HEADS:
                        v = i - 2 * RET_HEADS
                        dve.wait_ge(rturn_ready, l * N_ATT + (i + 1))
                        nc.vector.tensor_copy(rv[:, :, v * P:(v + 1) * P], ps[:, j, :].rearrange("p (t d) -> p t d", t=TT)).then_inc(bank_read[j], 1)
                        return
                    dve.wait_ge(rz_ready, l * N_ATT + (i + 1))
                    if i:
                        dve.wait_ge(rrope_done, n)
                    nc.vector.tensor_tensor(tmp[:, j % 2, :], stage[:, j % 2, :], ret_cos, ALU.mult).then_inc(rcos_done, 1)
                    dve.wait_ge(rturn_ready, l * N_ATT + (i + 1))
                    nc.vector.tensor_tensor(tmp_2[:, j % 2, :], ps[:, j, :], ret_sin, ALU.mult).then_inc(bank_read[j], 1)
                    dve.wait_ge(rcos_done, n + 1)
                    dve.wait_ge(bank_read[j], g + 3)
                    nc.vector.tensor_tensor(rqk[:, i, :], tmp[:, j % 2, :], tmp_2[:, j % 2, :], ALU.add).then_inc(rrope_done, 1)

                for u in range(N_ATT):
                    n, g, i = units[u]
                    wide = 2 * P if n else P
                    c, h = tiny[:, u % 2, :], 4 * g + 2 * i
                    dve.wait_ge(sc_ready, l * N_ATT + (u + 1))
                    if u >= 2:
                        dve.wait_ge(exp_done, l * N_ATT + (u - 1))
                    nc.vector.scalar_tensor_tensor(s_sb[:, u % 2, :, 0:wide], ps[:, 4 + u % 2, :].rearrange("p (e k) -> p e k", e=2)[:, :, 0:wide],
                                                   HEAD ** -0.5, att_mask[:, :, 2 * P - wide:2 * P], ALU.mult, ALU.add).then_inc(s_done, 1)
                    dve.wait_ge(s_done, l * N_ATT + (u + 1))
                    nc.vector.tensor_reduce(c[:, 12:14], s_sb[:, u % 2, :, 0:wide], AX.X, ALU.max).then_inc(mx_done, 1)
                    dve.wait_ge(mx_done, l * (2 * N_ATT) + (2 * u + 1))
                    nc.vector.scalar_tensor_tensor(c[:, 0:2], c[:, 12:14], -1.0, sink_now[:, 1, h:h + 2], ALU.mult, ALU.min).then_inc(mx_done, 1)
                    dve.wait_ge(mx_done, l * (2 * N_ATT) + (2 * u + 2))
                    nc.vector.tensor_tensor(c[:, 2:4], c[:, 0:2], sink_now[:, 0, h:h + 2], ALU.add).then_inc(nm_ready, 1)
                    if u >= 1:
                        normalised(u - 1)
                    if u >= 3:
                        output_lower(u - 3)
                    if u >= 2:
                        take(u - 2)
                normalised(N_ATT - 1)
                output_lower(N_ATT - 3)
                take(N_ATT - 2)
                output_lower(N_ATT - 2)
                output_lower(N_ATT - 1)
                take(N_ATT - 1)

                for h in range(RET_HEADS):
                    if h >= 2:
                        dve.wait_ge(inner_ready, l * RET_HEADS + (h - 1))
                    for t in range(TT):
                        dve.wait_ge(rs_ready, l * 16 + (4 * h + (t + 1 if t < 2 else 4)))
                        c = slice(RET_COL[t], RET_COL[t + 1])
                        wide = SEQ - t * P
                        src = ps[:, t, 0:wide] if t < 3 else ps[:, 2, 256:384]
                        nc.vector.tensor_tensor(a_sb[h % 2][:, c], src, decay[:, h, 0:wide], ALU.mult).then_inc(a_ready, 1)
                dve.wait_ge(rstd_ready, l + 1)
                nc.vector.reciprocal(rms[:, 1, 0:16], rms[:, 0, 0:16]).then_inc(rrinv_ready, 1)
                dve.wait_ge(rrinv_ready, l + 1)
                for h in range(RET_HEADS):
                    if h >= 1:
                        dve.wait_ge(rrb_ready, l * RET_HEADS + h)
                    nc.vector.tensor_tensor(*spread(4 * h)).then_inc(rdiag_ready, 1)
                with dve.Fori(0, 2) as i:
                    dve.wait_ge(rrb_ready, l * RET_HEADS + RET_HEADS)
                    g = g0 + i + G_RG

                    def ret_lower(j):
                        dve.wait_ge(rhi_ready, l * KT + i * 4 + (j + 1))
                        one = (slice(None), ds(i * 4 + j, 1), slice(None))
                        nc.vector.tensor_tensor(r_lo[one].rearrange("p o t -> p (o t)"), tmp_2[:, j % 2, :],
                                                r_hi[one].rearrange("p o t -> p (o t)").bitcast(F), ALU.subtract).then_inc(rlo_ready, 1)

                    for j in range(RING):
                        dve.wait_ge(tanh_ready, l * KT + i * 4 + (j + 1))
                        nc.vector.scalar_tensor_tensor(stage_2[:, j % 2, :], stage[:, j % 2, :], 1.0, ps[:, j, :], ALU.add, ALU.mult).then_inc(bank_read[j], 1)
                        nc.vector.tensor_tensor(tmp[:, j % 2, :], r_raw[:, ds(i * 4 + j, 1), :].rearrange("p o t -> p (o t)"),
                                                ps[:, ds(i * 2 + (4 + j // 2), 1), :].rearrange("p o t -> p (o t)"), ALU.mult).then_inc(sl_ready, 1)
                        dve.wait_ge(sl_ready, l * KT + i * 4 + (j + 1))
                        dve.wait_ge(bank_read[j], g + 3)
                        if j >= 2:
                            dve.wait_ge(rlo_ready, l * KT + i * 4 + (j - 1))
                        nc.vector.tensor_tensor(tmp_2[:, j % 2, :], stage_2[:, j % 2, :], tmp[:, j % 2, :], ALU.mult).then_inc(rr_ready, 1)
                        if j >= 1:
                            ret_lower(j - 1)
                    ret_lower(RING - 1)
                    dve.wait_ge(rlo_ready, l * KT + i * 4 + RING)
                with dve.Fori(0, 2) as i:
                    for m in range(RING):
                        (ga, ja), (gb, jb), (gy, jy) = [(g0 + i * 3 + (G_MIX + c // RING), c % RING) for c in range(3 * m, 3 * m + 3)]
                        one = (slice(None), ds(i * 4 + m, 1), slice(None))
                        dve.wait_ge(bank_read[ja], ga + 3)
                        nc.vector.scalar_tensor_tensor(tmp[:, m % 2, :], stage[:, m % 2, :], 1.0, y_a[one].rearrange("p o t -> p (o t)"),
                                                       ALU.add, ALU.mult).then_inc(t12_ready, 1)
                        dve.wait_ge(bank_read[jb], gb + 3)
                        dve.wait_ge(chunk_used, gy * RING + (jy + 1))
                        nc.vector.scalar_tensor_tensor(tmp_3[:, m % 2, :], stage_2[:, m % 2, :], 1.0, ps[:, jy, :],
                                                       ALU.add, ALU.mult).then_inc(bank_read[jy], 1)
                        dve.wait_ge(t12_ready, l * KT + i * 4 + (m + 1))
                        dve.wait_ge(bank_read[jy], gy + 3)
                        if m >= 2:
                            dve.wait_ge(mlo_ready, l * KT + i * 4 + (m - 1))
                        nc.vector.scalar_tensor_tensor(tmp_2[:, m % 2, :], tmp_3[:, m % 2, :], 0.5, tmp[:, m % 2, :],
                                                       ALU.mult, ALU.add).then_inc(mx_ready, 1)
                        dve.wait_ge(mhi_ready, l * KT + i * 4 + (m + 1))
                        nc.vector.tensor_tensor(mix_lo[one].rearrange("p o t -> p (o t)"), tmp_2[:, m % 2, :],
                                                mix_hi[one].rearrange("p o t -> p (o t)").bitcast(F), ALU.subtract).then_inc(mlo_ready, 1)
                    dve.wait_ge(mlo_ready, l * KT + i * 4 + RING)
                with dve.Fori(0, 2) as i:
                    for j in range(RING):
                        dve.wait_ge(chunk_used, (g0 + i + G_OUT) * RING + (j + 1))
                        one = x[:, ds(i * 4 + j, 1), :].rearrange("p o t -> p (o t)")
                        nc.vector.scalar_tensor_tensor(one, ps[:, j, :], 0.5, one, ALU.mult, ALU.add).then_inc(bank_read[j], 1)
                nc.vector.tensor_copy(gain_now[:, :], vec[:, ds(l * KT + V_GMLP, KT)]).then_inc(layer_vec, 1)
                dve.wait_ge(layer_vec, l * 4 + 4)
                norm(2 * l + 1)
                dve.wait_ge(ct_ready, l + 1)
                nc.vector.scalar_tensor_tensor(c_silu[:, :, :], c_silu[:, :, :], 1.0, c_raw[:, :, :], ALU.add, ALU.mult).then_inc(cs_ready, 1)
                def ada_products(n):
                    for s in range(3):
                        dve.wait_ge(ada_ready[s], n * 16 + 16)
                        for v in range(2):
                            if s or v:
                                dve.wait_ge(ada_sum, n * 6 + (2 * s + v))
                            nc.vector.scalar_tensor_tensor(ada_junk[:, :], ada_w[:, s, :], 0.5, c_silu[:, v, :], ALU.mult, ALU.mult,
                                                           accum_out=mod_3[:, v, s:s + 1]).then_inc(ada_sum, 1)
                    dve.wait_ge(ada_sum, n * 6 + 6)
                    nc.vector.tensor_copy(mod[:, :, ds(n * 3, 3)], mod_3[:, :, :]).then_inc(ada_used, 1)

                with dve.Fori(0, QUARTERS) as q:
                    with dve.Fori(0, 2) as i:
                        dve.wait_ge(cs_ready, l + 1)
                        g = g0 + q * 4 + i + G_MLP

                        def hidden_lower(j):
                            dve.wait_ge(uhi_ready, l * N_MLP + q * KT + i * 4 + (j + 1))
                            one = (slice(None), ds(i * 4 + j, 1), slice(None))
                            nc.vector.tensor_tensor(u_lo[one].rearrange("p o t -> p (o t)"), tmp[:, j % 2, :],
                                                    u_hi[one].rearrange("p o t -> p (o t)").bitcast(F), ALU.subtract).then_inc(ulo_ready, 1)

                        for j in range(RING):
                            dve.wait_ge(bank_read[j], g + 3)
                            if j >= 2:
                                dve.wait_ge(ulo_ready, l * N_MLP + q * KT + i * 4 + (j - 1))
                            nc.vector.tensor_tensor(tmp[:, j % 2, :], stage[:, j % 2, :], stage[:, j % 2, :], ALU.mult).then_inc(v2_ready, 1)
                            if j >= 1:
                                hidden_lower(j - 1)
                        hidden_lower(RING - 1)
                        dve.wait_ge(ulo_ready, l * N_MLP + q * KT + i * 4 + RING)
                        ada_products(l * 16 + q * 4 + i)
                    with dve.Fori(0, 2) as i:
                        g = g0 + q * 4 + i + (G_MLP + 2)
                        for j in range(RING):
                            dve.wait_ge(chunk_used, g * RING + (j + 1))
                            one = x[:, ds(i * 4 + j, 1), :].rearrange("p o t -> p (o t)")
                            nc.vector.tensor_tensor(one, ps[:, j, :], one, ALU.add).then_inc(bank_read[j], 1)
                        ada_products(l * 16 + q * 4 + i + 2)

            def norm_2(n, first):
                add_squares(n, [tile[:, first * P:ALL] for tile in squares_2[HALF_KT:]])
                dve.wait_ge(std_ready, n + 1)
                nc.vector.reciprocal(rms[:, 1, first:ST], rms[:, 0, first:ST]).then_inc(rinv_ready, 1)
                dve.wait_ge(rinv_ready, n + 1)
                wide = [P, ST - first, P]
                nc.vector.tensor_tensor(diag_2[:, first:ST, :], ident.rearrange("p (o q) -> p o q", o=1).broadcast_to(wide),
                                        rms[:, 1, first:ST].rearrange("p (t o) -> p t o", o=1).broadcast_to(wide), ALU.mult).then_inc(diag_ready, 1)
                dve.wait_ge(rb_ready, n + 1)

            def plain(gain):
                for k in range(KT):
                    nc.vector.scalar_tensor_tensor(x[:, k, :], x[:, k, :], vec[:, gain + k:gain + k + 1], ps[:, 5, :],
                                                   ALU.mult, ALU.mult).then_inc(xf_done, 1)

            def modulated(n, first, m, L, gain, col):
                for v in range(2):
                    at = L * ADA + col + KT
                    nc.vector.scalar_tensor_tensor(gain_2[:, v, :], mod[:, v, at:at + KT], 1.0, vec[:, gain + L * KT:gain + (L + 1) * KT],
                                                   ALU.add, ALU.mult).then_inc(gain_ready, 1)
                dve.wait_ge(gain_ready, 2 * (m - FIRST_MOD) + 2)
                norm_2(n, first)
                parts = ((C, cx, 1, ps[:, 6, 0:CTX]), (X, x, 0, ps[:, 5, :]))[1 if first else 0:]

                def lower(k):
                    dve.wait_ge(hhi_ready, m * KT + (k + 1))
                    at = L * ADA + col + k
                    for part, stream, v, bank in parts:
                        last = nc.vector.scalar_tensor_tensor(c_lo[:, k, part], hf_2[:, k % 2, part], mod[:, v, at:at + 1],
                                                              c_hi[:, k, part].bitcast(F), ALU.add, ALU.subtract)
                    last.then_inc(hlo_ready, 1)

                for k in range(KT):
                    if k >= 2:
                        dve.wait_ge(hlo_ready, m * KT + (k - 1))
                    for part, stream, v, bank in parts:
                        last = nc.vector.scalar_tensor_tensor(hf_2[:, k % 2, part], stream[:, k, :], gain_2[:, v, k:k + 1], bank, ALU.mult, ALU.mult)
                    last.then_inc(hf_ready, 1)
                    if k >= 1:
                        lower(k - 1)
                lower(KT - 1)

            def tokens(j, n, dst, x_bank, c_bank):
                dve.wait_ge(ztok_ready, n + 1)
                for one, bank, n in ((dst[0], ps[:, c_bank, 0:CTX], CT), (dst[1], ps[:, x_bank, :], TT)):
                    form = "p (t d) -> p t d" if len(one.shape) == 3 else "p (t h d) -> p t h d"
                    more = {} if len(one.shape) == 3 else {"h": 2}
                    last = nc.vector.tensor_copy(one, bank.rearrange(form, t=n, **more))
                last.then_inc(bank_read[j], 1)

            def gate_rows(L):
                f = slice(64, P)
                nc.vector.tensor_scalar(cum_f[f, :], gates[f, :], -1.0, None, ALU.mult).then_inc(gate_v, 1)
                dve.wait_ge(gate_v, L * 9 + 1)
                nc.vector.tensor_tensor(cum_f[f, :], cum_f[f, :], gates[f, :], ALU.min).then_inc(gate_v, 1)

            def gate_sums(L):
                fw, bw, both, f = slice(0, 32), slice(32, 64), slice(0, 64), slice(64, P)
                back_c = (bw, slice(CTX - 1, None, -1))

                def scans(dst, first_op, second_op, one, src, step):
                    n = CTX
                    nc.vector.tensor_tensor_scan(dst[fw, :], one(fw, ALL), src[fw, :], 0.0, first_op, second_op)
                    nc.vector.tensor_tensor_scan(dst[bw, C][:, ::-1], one(bw, n), src[bw, C][:, ::-1], 0.0, first_op, second_op).then_inc(gate_v, 1)
                    dve.wait_ge(gate_v, L * 9 + step)
                    nc.vector.tensor_tensor_scan(dst[bw, X][:, ::-1], one(bw, SEQ), src[bw, X][:, ::-1], dst[bw, 0:1], first_op, second_op).then_inc(gate_v, 1)
                    dve.wait_ge(gate_v, L * 9 + step + 1)

                dve.wait_ge(gate_a, L * 3 + 2)
                nc.vector.scalar_tensor_tensor(run_m[both, :], gates[f, :], 0.0, cum_f[f, :], ALU.min, ALU.subtract).then_inc(gate_v, 1)
                dve.wait_ge(gate_v, L * 9 + 3)
                scans(cum_f, ALU.mult, ALU.add, lambda rows, n: ones[rows, 0:1].broadcast_to([32, n]), run_m, 4)
                nc.vector.tensor_tensor(key_w[both, :], gates[both, :], cum_f[both, :], ALU.subtract).then_inc(gate_v, 1)
                dve.wait_ge(gate_v, L * 9 + 6)
                same = {ALL: lambda r: key_w[r, :], CTX: lambda r: key_w[r, C][:, ::-1], SEQ: lambda r: key_w[r, X][:, ::-1]}
                scans(run_m, ALU.max, ALU.max, lambda rows, n: same[n](rows), key_w, 7)
                nc.vector.tensor_tensor(key_w[f, :], cum_f[both, :], run_m[both, :], ALU.add).then_inc(gate_v, 1)

            def neighborhood(L, need_ctx, g0):
                units, base = natt_units(need_ctx), L * N_UNITS

                def normalised(u):
                    wide = CTX if units[u][1] else ALL
                    dve.wait_ge(nexp_done, base + (u + 1))
                    nc.vector.reciprocal(tiny[:, u % 2, 2:3], tiny[:, u % 2, 1:2]).then_inc(nrec_done, 1)
                    dve.wait_ge(nrec_done, base + (u + 1))
                    nc.vector.tensor_scalar(sn[:, u % 3, 0:wide], sn[:, u % 3, 0:wide], tiny[:, u % 2, 2:3], None, ALU.mult).then_inc(np_ready, 1)

                def lower(u):
                    h, c, t = units[u]
                    rows, part = slice(h % 2 * HEAD, h % 2 * HEAD + HEAD), C if c else X
                    dve.wait_ge(nhi_ready, L * (2 * H2) + group_end(u, units) + 1)
                    nc.vector.tensor_tensor(yn_lo[rows, h // 2, part], ps[rows, 7, 0:part.stop - part.start],
                                            yn_hi[rows, h // 2, part].bitcast(F), ALU.subtract).then_inc(nlo_ready, 1)

                def take(c):
                    n, j, g = L * 8 + c, c % RING, g0 + G_QM + c // RING
                    if c >= 2 * RING:
                        tokens(j, L * 8 + 4 + j, [vm[:, s, 2 * j:2 * j + 2, 0:HEAD] for s in (slice(0, CT), slice(CT, ST))], c % 2, 2)
                        return
                    dve.wait_ge(z_ready, L * 16 + 5 + c)
                    if n:
                        dve.wait_ge(rope_2, n)
                    nc.vector.tensor_tensor(rope_a[:, :], zm[:, j % 2, X], rope_cos, ALU.mult).then_inc(rope_part, 1)
                    dve.wait_ge(zrot_ready, n + 1)
                    nc.vector.tensor_tensor(rope_b[:, :], ps[:, c % 2, :], rope_sin, ALU.mult).then_inc(bank_read[j], 1)
                    dve.wait_ge(rope_part, n + 1)
                    dve.wait_ge(bank_read[j], g + 3)
                    nc.vector.tensor_tensor((qm, km)[c // RING][:, j, X], rope_a[:, :], rope_b[:, :], ALU.add).then_inc(rope_2, 1)

                nc.vector.memset(vm[:, :, :, HEAD:HEAD + 1], 1.0)
                for u, (h, c, t) in enumerate(units):
                    wide = CTX if c else ALL
                    if c == 0 and t == 0:
                        table = bias[:, h % 2, :].rearrange("p (e k) -> p e k", k=GRID_W)
                        dve.wait_ge(bias_loaded[h % 2], (L * 4 + h // 2 + 1) * 16)
                        nc.vector.tensor_tensor(table, table, col_mask.rearrange("p (o k) -> p o k", o=1).broadcast_to([P, 2 * NA_ROWS - 2, GRID_W]),
                                                ALU.add).then_inc(bias_ready, 1)
                        dve.wait_ge(bias_ready, L * H2 + h + 1)
                    dve.wait_ge(ns_ready, base + (u + 1))
                    if u >= 3:
                        dve.wait_ge(npt_ready, L * N_FILLS + fills_before(u - 2, units))
                    if not c:
                        at = (NA_ROWS - 2 - 2 * t) * GRID_W
                        nc.vector.scalar_tensor_tensor(sn[:, u % 3, X], ps[:, 3 + u % 2, :], HEAD ** -0.5, bias[:, h % 2, at:at + SEQ],
                                                       ALU.mult, ALU.add).then_inc(nsx_done, 1)
                        dve.wait_ge(nsx_done, L * (H2 * TT) + h * TT + t + 1)
                    if u >= 1:
                        normalised(u - 1)
                    dve.wait_ge(nsc_done, base + (u + 1))
                    nc.vector.tensor_reduce(tiny[:, u % 2, 3:4], sn[:, u % 3, 0:wide], AX.X, ALU.max).then_inc(nmx_done, 1)
                    dve.wait_ge(nmx_done, base + (u + 1))
                    nc.vector.tensor_scalar(tiny[:, u % 2, 0:1], tiny[:, u % 2, 3:4], -1.0, None, ALU.mult).then_inc(nneg_ready, 1)
                    if u >= 3 and group_end(u - 3, units) is not None:
                        lower(u - 3)
                    for i in tiles_after(u, units, need_ctx, 1):
                        take(i)
                normalised(len(units) - 1)
                take(M_TILES - 1)
                for u in range(len(units) - 3, len(units)):
                    if group_end(u, units) is not None:
                        lower(u)

            def mlstm(L, first):
                runs, where = gw_layout(first)
                def diagonals(h):
                    dve.wait_ge(m_loaded[h % 2], (L * 4 + h // 2 + 1) * 16)
                    if h >= 2:
                        dve.wait_ge(mpv_ready, 2 * (L * H2 + h - 1))
                    for s in range(first, ST):
                        for d in range(2):
                            at = where[d, s, s]
                            last = nc.vector.scalar_tensor_tensor(gw[:, h % 2, at:at + P], m_row[:, h % 2, d, s * P:(s + 1) * P],
                                                                  key_t[:, s, 32 * d + h:32 * d + h + 1], causal[d], ALU.subtract, ALU.max)
                    last.then_inc(mdiag_ready, 1)

                def scored(h, a=0, b=ST):
                    for s in range(a, b):
                        n = h * ST + s
                        dve.wait_ge(mw_ready, L * N_UNITS + (n + 1))
                        dve.wait_ge(ms_ready, L * N_UNITS + (n + 1))
                        bank = 2 * (n % 2)
                        score = ps[:, bank:bank + 2, :].rearrange("p b t -> p (b t)")
                        for d, t0, t1, at in runs[s]:
                            w = gw[:, h % 2, at:at + (t1 - t0) * P]
                            last = nc.vector.scalar_tensor_tensor(w, score[:, t0 * P:t1 * P], HEAD ** -0.5, w, ALU.mult, ALU.mult)
                        last.then_inc(mg_ready, 1)

                def result(h):
                    n = (L * H2 + h) * 6
                    both = ps[:, 4 * (h % 2):4 * (h % 2) + 4:2, 0:ST * (HEAD + 1)].rearrange("p d (t c) -> p d t c", c=HEAD + 1)[:, :, first:ST, :]
                    total = both[:, :, :, HEAD]
                    least = key_t[:, first:ST, 64:P].rearrange("p t (d c) -> p d t c", c=32)[:, :, :, h]
                    den, inv = [cols[:, i, 0:2 * ST].rearrange("p (d t) -> p d t", d=2)[:, :, first:ST] for i in range(2)]

                    def over(d):
                        return inv[:, d, :].rearrange("p (t o) -> p t o", o=1).broadcast_to([P, ST - first, HEAD])

                    dve.wait_ge(num_token, 2 * (L * H2 + h + 1))
                    nc.vector.tensor_scalar(den, total, -1.0, None, ALU.mult).then_inc(post_v, 1)
                    dve.wait_ge(post_v, n + 1)
                    nc.vector.tensor_tensor(den, den, total, ALU.max).then_inc(post_v, 1)
                    dve.wait_ge(post_v, n + 2)
                    nc.vector.tensor_tensor(den, den, least, ALU.max).then_inc(post_v, 1)
                    dve.wait_ge(post_v, n + 3)
                    nc.vector.reciprocal(inv, den).then_inc(post_v, 1)
                    dve.wait_ge(post_v, n + 4)
                    nc.vector.tensor_tensor(hs[:, first:ST, h, :], both[:, 0, :, 0:HEAD], over(0), ALU.mult).then_inc(post_v, 1)
                    nc.vector.tensor_tensor(hb[:, first:ST, :], both[:, 1, :, 0:HEAD], over(1), ALU.mult).then_inc(head_done, 1)
                    dve.wait_ge(post_v, n + 5)
                    dve.wait_ge(head_done, L * H2 + (h + 1))
                    nc.vector.tensor_tensor(hs[:, first:ST, h, :], hs[:, first:ST, h, :], hb[:, first:ST, :], ALU.add).then_inc(post_v, 1)

                dve.wait_ge(key_copied, L + 1)
                diagonals(0)
                diagonals(1)
                scored(0)
                scored(1)
                for h in range(0, H2, 2):
                    if h + 2 < H2:
                        diagonals(h + 2)
                    result(h)
                    if h + 2 < H2:
                        scored(h + 2, 0, ST // 2)
                        diagonals(h + 3)
                        scored(h + 2, ST // 2)
                    result(h + 1)
                    if h + 2 < H2:
                        scored(h + 3)
                dve.wait_ge(post_v, (L + 1) * H2 * 6)
                heads = hs[:, first:ST, :, :].rearrange("p t h d -> p (t h) d")
                c = slice(first * H2, ST * H2)

                def spread(i):
                    return cols[:, i, c].rearrange("p (t o) -> p t o", o=1).broadcast_to([P, (ST - first) * H2, HEAD])

                nc.vector.tensor_reduce(cols[:, 0, c], heads, AX.X, ALU.add).then_inc(ln_v, 1)
                dve.wait_ge(ln_v, L * 6 + 1)
                nc.vector.tensor_scalar(cols[:, 0, c], cols[:, 0, c], -1.0 / HEAD, None, ALU.mult).then_inc(ln_v, 1)
                dve.wait_ge(ln_v, L * 6 + 2)
                nc.vector.tensor_tensor(heads, heads, spread(0), ALU.add).then_inc(ln_v, 1)
                dve.wait_ge(ln_a, L * 2 + 1)
                nc.vector.tensor_reduce(cols[:, 1, c], hq[:, first:ST, :, :].rearrange("p t h d -> p (t h) d"), AX.X, ALU.add).then_inc(ln_v, 1)
                dve.wait_ge(ln_a, L * 2 + 2)
                nc.vector.reciprocal(cols[:, 3, c], cols[:, 2, c]).then_inc(ln_v, 1)
                dve.wait_ge(ln_v, L * 6 + 5)
                nc.vector.tensor_tensor(heads, heads, spread(3), ALU.mult).then_inc(ln_v, 1)
                dve.wait_ge(om_half, (L + 1) * 4)
                lo = first * P

                def lower(f):
                    dve.wait_ge(yhi_ready, L * 4 + (f + 1))
                    nc.vector.tensor_tensor(ym_lo[:, f, lo:ALL], yu[:, f, lo:ALL], ym_hi[:, f, lo:ALL].bitcast(F), ALU.subtract).then_inc(ylo_ready, 1)

                for f in range(4):
                    g = vec[:, V_MN + L * 4 + f:V_MN + L * 4 + f + 1]
                    dve.wait_ge(yt_ready, L * 4 + (f + 1))
                    if first == 0:
                        nc.vector.scalar_tensor_tensor(yu[:, f, C], ps[:, 2 * f + 1, 0:CTX], g, om[:, f, C], ALU.mult, ALU.mult)
                    nc.vector.scalar_tensor_tensor(yu[:, f, X], ps[:, 2 * f, :], g, om[:, f, X], ALU.mult, ALU.mult).then_inc(yu_ready, 1)
                    if f >= 1:
                        lower(f - 1)
                lower(3)

            def add_to_stream(g, j, k, at, need_ctx):
                dve.wait_ge(chunk_used, g * RING + (j + 1))
                if need_ctx:
                    one = cx[:, ds(k, 1), :].rearrange("p o t -> p (o t)")
                    nc.vector.scalar_tensor_tensor(one, ps[:, 4 + j, 0:CTX], mod[:, 1, ds(k + at, 1)], one, ALU.mult, ALU.add)
                one = x[:, ds(k, 1), :].rearrange("p o t -> p (o t)")
                nc.vector.scalar_tensor_tensor(one, ps[:, j, :], mod[:, 0, ds(k + at, 1)], one, ALU.mult, ALU.add).then_inc(bank_read[j], 1)

            dve.wait_ge(ada_used, DEPTH * (ADA // 3) + 1)
            for v in range(2):
                nc.vector.tensor_tensor(mod[:, v, :], mod[:, v, :], vec[:, V_BADA:V_BADA + DEPTH * ADA], ALU.add).then_inc(mod_ready, 1)
            dve.wait_ge(mod_ready, 2)
            root(FIRST_MOD)
            plain(V_GF)
            dve.wait_ge(xf_done, KT)
            dve.wait_ge(c2_loaded, 16)
            dve.wait_ge(cx_loaded, 16)
            for L in range(DEPTH):
                need_ctx = L + 1 < DEPTH
                first = 0 if need_ctx else CT
                g0 = START_2 + L * G2
                modulated(FIRST_MOD + 1 + 2 * L, 0, FIRST_MOD + 2 * L, L, V_N1, 0)
                for j in range(RING):
                    tokens(j, L * 8 + j, [vn[:, s, j * P:(j + 1) * P] for s in (slice(0, CT), slice(CT, ST))], j, 4 + j)
                dve.wait_ge(chunk_used, (g0 + G_GATE) * RING + 1)
                b = vec[:, V_BG + L:V_BG + L + 1]
                nc.vector.tensor_scalar(gates[:, C], ps[:, 4, 0:CTX], b, None, ALU.add)
                nc.vector.tensor_scalar(gates[:, X], ps[:, 0, :], b, None, ALU.add).then_inc(bank_read[0], 1)
                dve.wait_ge(bank_read[0], g0 + G_GATE + 3)
                neighborhood(L, need_ctx, g0)
                gate_rows(L)
                gate_sums(L)
                for j in range(RING):
                    dve.wait_ge(bank_read[j], g0 + G_OM + 3)
                    nc.vector.tensor_scalar(om[:, j, :], om[:, j, :], 0.5, 0.5, ALU.mult, ALU.add).then_inc(om_half, 1)
                mlstm(L, first)
                dve.wait_ge(reloaded, (L + 1) * 32)
                with dve.Fori(0, 2) as i:
                    for j in range(RING):
                        add_to_stream(g0 + i + G_OUT2, j, i * 4 + j, L * ADA + 2 * KT, need_ctx)
                modulated(FIRST_MOD + 2 + 2 * L, first, FIRST_MOD + 2 * L + 1, L, V_N2, 3 * KT)
                lo = first * P
                with dve.Fori(0, QUARTERS) as q:
                    with dve.Fori(0, 2) as i:
                        g = g0 + q * 4 + i + G_UP

                        def hidden_lower_2(j):
                            done = q * KT + i * 4 + ((DEPTH + L) * N_MLP + j + 1)
                            dve.wait_ge(uhi_ready, done)
                            one = (slice(None), ds(i * 4 + j, 1), slice(lo, ALL))
                            nc.vector.tensor_tensor(u2_lo[one].rearrange("p o t -> p (o t)"), hf_2[:, j % 2, lo:ALL],
                                                    u2_hi[one].rearrange("p o t -> p (o t)").bitcast(F), ALU.subtract).then_inc(ulo_ready, 1)

                        for j in range(RING):
                            dve.wait_ge(bank_read[j], g + 3)
                            if j >= 2:
                                dve.wait_ge(ulo_ready, q * KT + i * 4 + ((DEPTH + L) * N_MLP + j - 1))
                            nc.vector.tensor_tensor(hf_2[:, j % 2, lo:ALL], sq_2[:, j % 2, lo:ALL], sq_2[:, j % 2, lo:ALL], ALU.mult).then_inc(v2_ready, 1)
                            if j >= 1:
                                hidden_lower_2(j - 1)
                        hidden_lower_2(RING - 1)
                        dve.wait_ge(ulo_ready, q * KT + i * 4 + ((DEPTH + L) * N_MLP + RING))
                    with dve.Fori(0, 2) as i:
                        for j in range(RING):
                            add_to_stream(g0 + q * 4 + i + (G_UP + 2), j, i * 4 + j, L * ADA + 5 * KT, need_ctx)
            norm_2(FIRST_MOD + 1 + 2 * DEPTH, CT)
            plain(V_FIN)


def constants_2():
    import numpy as np
    f = np.float32
    p = np.arange(P)
    pos = np.arange(SEQ)
    inv = f(10000.0) ** (-np.arange(16, dtype=f) / f(16))
    d = p % 32
    ang = np.where((d < 16)[:, None], (pos // GRID_W).astype(f)[None, :], (pos % GRID_W).astype(f)[None, :]) * inv[d % 16][:, None]
    cos, sin = np.cos(ang), np.sin(ang) * np.where(p % HEAD < 32, -1, 1)[:, None]
    key, query = p[:, None], p[None, :]
    col = p % GRID_W
    start = np.clip(col - NA_COLS // 2, 0, GRID_W - NA_COLS)[:, None]
    c = np.arange(GRID_W)[None, :]
    window = np.where((c >= start) & (c < start + NA_COLS), 0.0, MASKED)
    causal = [np.where(seen, 0.0, -MASKED) for seen in (key <= query, key >= query)]
    return np.concatenate([cos, sin, *causal, window], axis=1).astype(f)


def bias_tiles(rpb):
    import numpy as np
    p, e, k = np.arange(P)[:, None, None], np.arange(1, 2 * NA_ROWS - 1)[None, :, None], np.arange(GRID_W)[None, None, :]
    dc = np.clip(k - p % GRID_W + NA_COLS - 1, 0, 2 * NA_COLS - 2)
    return np.ascontiguousarray(rpb[:, :, e - p // GRID_W, dc].reshape(*rpb.shape[:2], P, -1))


def gate_columns(b):
    import numpy as np
    out = np.zeros((P, b.shape[0]), np.float32)
    for g in range(4):
        out[32 * g:32 * g + H2] = b[:, g * H2:(g + 1) * H2].T
    return out


def kernel(x, g_mix, w_in, sinks, w_a, w_b, w_out, g_mlp, w_up, w_down, g_final, c_2, ctx_2, c_ctx_2,
           w_ada_2, b_ada_2, norm1_g_2, w_in_2, b_gate_2, mlstm_norm_g_2, rpb_2, w_out_2, norm2_g_2,
           w_mlp1_2, w_mlp2_2, final_g_2):
    import concourse.bacc as bacc
    import numpy as np
    from concourse import mybir
    from concourse.bass_utils import run_bass_kernel_spmd

    def host(a):
        return np.asarray(a)

    def by_feature(a):
        return np.ascontiguousarray(a.T.reshape(KT, P, -1).transpose(1, 0, 2))

    weights = weight_stream({n: host(a) for n, a in dict(
        w_in=w_in, w_a=w_a, w_b=w_b, w_out=w_out, w_up=w_up, w_down=w_down, w_in_2=w_in_2,
        w_out_2=w_out_2, w_mlp1_2=w_mlp1_2, w_mlp2_2=w_mlp2_2).items()})
    vectors = np.concatenate([*[columns(host(v)) for v in (g_mix, g_mlp, norm1_g_2, norm2_g_2, g_final, final_g_2,
                                                           b_ada_2, mlstm_norm_g_2)],
                              gate_columns(host(b_gate_2)),
                              np.broadcast_to(host(sinks).reshape(1, -1), (P, DEPTH * ATT_HEADS))], axis=1)
    arrays = {
        "x": by_feature(host(x)[0]), "ctx": by_feature(host(ctx_2)[0]), "w": weights, "vec": vectors,
        "c0": constants_0(), "c1": constants_1(), "c2": constants_2(), "rpb": bias_tiles(host(rpb_2)),
        "ada": np.ascontiguousarray(host(w_ada_2).transpose(0, 2, 1).reshape(DEPTH * ADA, P, D_MODEL)),
        "c": np.stack([host(c_2)[0], host(c_ctx_2)])[None],
    }
    nc = bacc.Bacc("TRN2", target_bir_lowering=False, num_devices=1)
    dram = {n: nc.dram_tensor(f"in_{n}", list(a.shape), mybir.dt.float32, kind="ExternalInput").ap() for n, a in arrays.items()}
    out = nc.dram_tensor("out", [P, KT, SEQ], mybir.dt.float32, kind="ExternalOutput").ap()
    hybrid_then_dit(nc, dram, out)
    results = run_bass_kernel_spmd(nc, [{f"in_{n}": a for n, a in arrays.items()}], core_ids=[0])
    got = results.results[0]["out"]
    return np.ascontiguousarray(got.transpose(1, 0, 2).reshape(D_MODEL, SEQ).T).reshape(1, SEQ, D_MODEL)
```
